# Optimizing a Trainium2 kernel written in Bass

```python
import jax, jax.numpy as jnp
from jax import lax
import numpy as np

D_MODEL = 1024
BATCH = 1
SEQ = 512
DEPTH = 1

MEM_LEN = 256
H_MEM = 4
MEM_HD = 128
MEM_WIDTH = H_MEM * MEM_HD
Q_BLOCK = 128
H_MLA = 8
MLA_NOPE = 64
MLA_ROPE = 32
MLA_V = 64
Q_LORA = 384
KV_LORA = 256
ROPE_THETA = 10000.0
MLA_WIDTH = H_MLA * MLA_V
H_FOX = 8
FOX_HD = 64
FOX_WIDTH = H_FOX * FOX_HD
MIX_WIDTH = MLA_WIDTH + FOX_WIDTH
IN_SIZES = (Q_LORA, KV_LORA, MLA_ROPE, FOX_WIDTH, FOX_WIDTH, FOX_WIDTH, H_FOX)
IN_COLS = Q_LORA + KV_LORA + MLA_ROPE + 3 * FOX_WIDTH + H_FOX
D_FF = -(-(8 * D_MODEL) // (3 * 256)) * 256
EPS = 1e-6

kernel_name = "hymba_style_mla_fox_hybrid"

def _rmsnorm(x, g):
    xf = x.astype(jnp.float32)
    y = xf * lax.rsqrt(jnp.mean(xf * xf, axis=-1, keepdims=True) + EPS)
    return (y * g.astype(jnp.float32)).astype(x.dtype)

def _rope_tables(seq, dtype):
    inv = 1.0 / (ROPE_THETA ** (jnp.arange(0, MLA_ROPE, 2, dtype=jnp.float32) / MLA_ROPE))
    ang = jnp.arange(seq, dtype=jnp.float32)[:, None] * inv[None, :]
    return jnp.cos(ang).astype(dtype), jnp.sin(ang).astype(dtype)

def _rope(x, cos, sin):
    x1, x2 = jnp.split(x, 2, axis=-1)
    return jnp.concatenate([x1 * cos - x2 * sin, x1 * sin + x2 * cos], axis=-1)

def _to_blocks(t):
    b, s = t.shape[:2]
    return t.reshape(b, s // Q_BLOCK, Q_BLOCK, *t.shape[2:]).swapaxes(0, 1)

def _from_blocks(t):
    nb, b, qb = t.shape[:3]
    return t.swapaxes(0, 1).reshape(b, nb * qb, *t.shape[3:])

def _causal_mask(i, seq):
    qpos = i * Q_BLOCK + jnp.arange(Q_BLOCK)
    return jnp.arange(seq)[None, :] <= qpos[:, None]

def _mla_attention(q_nope, q_rope, k_nope, k_rope, v):
    seq = k_nope.shape[1]
    scale = (MLA_NOPE + MLA_ROPE) ** -0.5

    def block(args):
        qn, qr, i = args
        s = (jnp.einsum('bqhd,bkhd->bhqk', qn, k_nope)
             + jnp.einsum('bqhr,bkr->bhqk', qr, k_rope)).astype(jnp.float32) * scale
        s = jnp.where(_causal_mask(i, seq), s, -jnp.inf)
        p = jax.nn.softmax(s, axis=-1).astype(v.dtype)
        return jnp.einsum('bhqk,bkhd->bqhd', p, v)

    out = lax.map(block, (_to_blocks(q_nope), _to_blocks(q_rope), jnp.arange(seq // Q_BLOCK)))
    return _from_blocks(out)

def _forgetting_attention(q, k, v, log_f):
    seq = k.shape[1]
    scale = FOX_HD ** -0.5
    cum = jnp.cumsum(log_f, axis=1)
    cum_k = cum.transpose(0, 2, 1)

    def block(args):
        qb, cum_q, i = args
        s = jnp.einsum('bqhd,bkhd->bhqk', qb, k).astype(jnp.float32) * scale
        s = s + (cum_q.transpose(0, 2, 1)[:, :, :, None] - cum_k[:, :, None, :])
        s = jnp.where(_causal_mask(i, seq), s, -jnp.inf)
        p = jax.nn.softmax(s, axis=-1).astype(v.dtype)
        return jnp.einsum('bhqk,bkhd->bqhd', p, v)

    out = lax.map(block, (_to_blocks(q), _to_blocks(cum), jnp.arange(seq // Q_BLOCK)))
    return _from_blocks(out)

def _hybrid_mixer(xn, w_in, cq_g, ckv_g, w_uq, w_ukv, f_bias, mla_g, fox_g, w_out, cos, sin):
    b, s, _ = xn.shape
    h = xn @ w_in
    offs = [int(o) for o in np.cumsum(IN_SIZES)[:-1]]
    c_q, c_kv, k_rope, q_f, k_f, v_f, f_logit = jnp.split(h, offs, axis=-1)

    q = (_rmsnorm(c_q, cq_g) @ w_uq).reshape(b, s, H_MLA, MLA_NOPE + MLA_ROPE)
    q_nope = q[..., :MLA_NOPE]
    q_rope = _rope(q[..., MLA_NOPE:], cos[:, None, :], sin[:, None, :])
    kv = (_rmsnorm(c_kv, ckv_g) @ w_ukv).reshape(b, s, H_MLA, MLA_NOPE + MLA_V)
    k_nope, v = kv[..., :MLA_NOPE], kv[..., MLA_NOPE:]
    k_rope = _rope(k_rope, cos, sin)
    o_mla = _mla_attention(q_nope, q_rope, k_nope, k_rope, v).reshape(b, s, MLA_WIDTH)

    heads = lambda t: t.reshape(b, s, H_FOX, FOX_HD)
    log_f = jax.nn.log_sigmoid((f_logit + f_bias).astype(jnp.float32))
    o_fox = _forgetting_attention(heads(q_f), heads(k_f), heads(v_f), log_f).reshape(b, s, FOX_WIDTH)

    merged = jnp.concatenate([_rmsnorm(o_mla, mla_g), _rmsnorm(o_fox, fox_g)], axis=-1)
    return merged @ w_out

def _memory_cross_attention(xn, mem, mem_g, w_mq, w_mkv, w_mo):
    b, s, _ = xn.shape
    m = mem.shape[1]
    q = (xn @ w_mq).reshape(b, s, H_MEM, MEM_HD)
    kv = (_rmsnorm(mem, mem_g) @ w_mkv).reshape(b, m, H_MEM, 2 * MEM_HD)
    k, v = kv[..., :MEM_HD], kv[..., MEM_HD:]
    sc = jnp.einsum('bqhd,bmhd->bhqm', q, k).astype(jnp.float32) * (MEM_HD ** -0.5)
    p = jax.nn.softmax(sc, axis=-1).astype(v.dtype)
    o = jnp.einsum('bhqm,bmhd->bqhd', p, v).reshape(b, s, MEM_WIDTH)
    return o @ w_mo

def _swiglu(xn, w_gate, w_up, w_down):
    return (jax.nn.silu(xn @ w_gate) * (xn @ w_up)) @ w_down

def setup_inputs(seed: int = 0) -> dict:
    key = jax.random.key(seed)
    ks = jax.random.split(key, 24)

    def dense(k, shape, fan_in):
        return jax.random.normal(k, shape, jnp.float32) * (fan_in ** -0.5)

    def gain(k, shape):
        return 1.0 + 0.02 * jax.random.normal(k, shape, jnp.float32)

    return {
        "x": jax.random.normal(ks[0], (BATCH, SEQ, D_MODEL), jnp.float32),
        "mem": jax.random.normal(ks[1], (BATCH, MEM_LEN, D_MODEL), jnp.float32),
        "mix_norm_g": gain(ks[2], (DEPTH, D_MODEL)),
        "w_in": dense(ks[3], (DEPTH, D_MODEL, IN_COLS), D_MODEL),
        "cq_norm_g": gain(ks[4], (DEPTH, Q_LORA)),
        "ckv_norm_g": gain(ks[5], (DEPTH, KV_LORA)),
        "w_uq": dense(ks[6], (DEPTH, Q_LORA, H_MLA * (MLA_NOPE + MLA_ROPE)), Q_LORA),
        "w_ukv": dense(ks[7], (DEPTH, KV_LORA, H_MLA * (MLA_NOPE + MLA_V)), KV_LORA),
        "forget_bias": jax.random.uniform(ks[8], (DEPTH, H_FOX), jnp.float32, 2.0, 6.0),
        "mla_out_g": gain(ks[9], (DEPTH, MLA_WIDTH)),
        "fox_out_g": gain(ks[10], (DEPTH, FOX_WIDTH)),
        "w_out": dense(ks[11], (DEPTH, MIX_WIDTH, D_MODEL), MIX_WIDTH),
        "mem_q_norm_g": gain(ks[12], (DEPTH, D_MODEL)),
        "mem_kv_norm_g": gain(ks[13], (DEPTH, D_MODEL)),
        "w_mq": dense(ks[14], (DEPTH, D_MODEL, MEM_WIDTH), D_MODEL),
        "w_mkv": dense(ks[15], (DEPTH, D_MODEL, 2 * MEM_WIDTH), D_MODEL),
        "w_mo": dense(ks[16], (DEPTH, MEM_WIDTH, D_MODEL), MEM_WIDTH),
        "ffn_norm_g": gain(ks[17], (DEPTH, D_MODEL)),
        "w_gate": dense(ks[18], (DEPTH, D_MODEL, D_FF), D_MODEL),
        "w_up": dense(ks[19], (DEPTH, D_MODEL, D_FF), D_MODEL),
        "w_down": dense(ks[20], (DEPTH, D_FF, D_MODEL), D_FF),
        "final_norm_g": gain(ks[21], (D_MODEL,)),
    }

def reference(x, mem, mix_norm_g, w_in, cq_norm_g, ckv_norm_g, w_uq, w_ukv, forget_bias,
              mla_out_g, fox_out_g, w_out, mem_q_norm_g, mem_kv_norm_g, w_mq, w_mkv, w_mo,
              ffn_norm_g, w_gate, w_up, w_down, final_norm_g):
    cos, sin = _rope_tables(x.shape[1], x.dtype)
    h = x
    for l in range(DEPTH):
        h = h + _hybrid_mixer(_rmsnorm(h, mix_norm_g[l]), w_in[l], cq_norm_g[l], ckv_norm_g[l],
                              w_uq[l], w_ukv[l], forget_bias[l], mla_out_g[l], fox_out_g[l],
                              w_out[l], cos, sin)
        h = h + _memory_cross_attention(_rmsnorm(h, mem_q_norm_g[l]), mem, mem_kv_norm_g[l],
                                        w_mq[l], w_mkv[l], w_mo[l])
        h = h + _swiglu(_rmsnorm(h, ffn_norm_g[l]), w_gate[l], w_up[l], w_down[l])
    return _rmsnorm(h, final_norm_g)


_drawn_inputs = setup_inputs


def setup_inputs(seed=0):
    import zlib

    import numpy as np

    out = dict(_drawn_inputs(seed))
    spreads = {}
    factors = {'cq_norm_g': 5.555,
     'ckv_norm_g': 3.524,
     'mla_out_g': 5.284,
     'fox_out_g': 5.096,
     'mem_q_norm_g': 8.0,
     'mem_kv_norm_g': 8.0,
     'ffn_norm_g': 5.162,
     'final_norm_g': 2.74}
    for name, (base, spread) in spreads.items():
        noise = np.random.default_rng([zlib.crc32(name.encode()), seed]).standard_normal(out[name].shape)
        drawn = base * np.exp(spread * noise) if base else spread * noise
        out[name] = __import__('jax').numpy.asarray(drawn.astype(out[name].dtype))
    for name, factor in factors.items():
        out[name] = (out[name] * factor).astype(out[name].dtype)
    return out
```

```python
from contextlib import ExitStack

import numpy as np
import concourse.bass as bass
from concourse import mybir

F32 = mybir.dt.float32
F32R = mybir.dt.float32r
BF16 = mybir.dt.bfloat16
ALU = mybir.AluOpType
ACT = mybir.ActivationFunctionType
AX = mybir.AxisListType

P = 128
D = 1024
SEQ = 512
MEM = 256
NT = SEQ // P
NM = MEM // P
KD = D // P
NH = 8
HD = 64
ROPE = 32
QK = HD + ROPE
Q_LORA = 384
KV_LORA = 256
CQ, CKV = Q_LORA // P, KV_LORA // P
H_MEM = 4
MEM_HD = 128
D_FF = 2816
NF = D_FF // P
HALF = 512
EPS = 1e-6
SLOT = 1024
RAW = 3
SPLIT = 2
MLA_SCALE = float(QK) ** -0.5
FOX_SCALE = float(HD) ** -0.5
MEM_SCALE = float(MEM_HD) ** -0.5
MASKED = 1e30
P_OFF = [0, 128, 384, 768]
P_COLS = 1280

C_CQ, C_CKV, C_ROPE, C_QF, C_KF, C_VF, C_F = 0, 384, 640, 672, 1184, 1696, 2208


class Banks:

    def __init__(self):
        self.turns = [0] * 8
        self.hi_turns = [0] * 8
        self.use = {}

    def add(self, key, bank, split=False):
        self.turns[bank] += 1
        if split:
            self.hi_turns[bank] += 1
        self.use[key] = (bank, self.turns[bank], self.hi_turns[bank])


def plan_banks():
    bk = Banks()
    for t in range(NT):
        for half in range(2):
            bk.add(("xT", t, half), 2 * t + half, True)
    for t in range(NT):
        bk.add(("cq", t), t)
    for t in range(NT):
        bk.add(("ckv", t), 4 + t)
    for t in range(NT):
        bk.add(("vf", t), t, True)
    bk.add(("cum",), 4)
    for t in range(NT):
        bk.add(("qf", t), 4 + t)
    for t in range(NT):
        bk.add(("kf", t), t)
    for c in range(CQ + CKV):
        bk.add(("cT", c), (4 + c) % 8, True)

    s_turn = [0]

    def attention(heads):
        first, last = heads[0], heads[-1]

        def scores(g, i):
            bk.add(("S", g, i), s_turn[0] % 2)
            s_turn[0] += 1

        def qkt(g):
            bk.add(("QT", g), 5, True)
            bk.add(("KT", g), 6, True)

        qkt(first)
        for g in heads + [None]:
            prev = last if g is None else (g - 1 if g > first else None)
            for i in (3, 2, 1, 0):
                if g is not None:
                    scores(g, i)
                if prev is not None and i in (2, 1, 0):
                    bk.add(("PT", prev, 2 - i), 2 + (2 - i), True)
            if g is not None and g < last:
                qkt(g + 1)
            if prev is not None:
                bk.add(("PV", prev), 7, True)

    attention(list(range(NH)))
    bk.add(("ssq", 0), 7)
    for t in range(NT):
        for n in range(2):
            bk.add(("uq", t, n), 2 * t + n)
    for t in range(NT):
        for n in range(2):
            bk.add(("ukv", t, n), 2 * t + n, True)
    attention(list(range(NH, 2 * NH)))
    bk.add(("ssq", 1), 7)
    for stage in range(4):
        for t in range(NT):
            bk.add(("out", stage, t), 4 * (stage % 2) + t)
    for m in range(NM):
        for half in range(2):
            bk.add(("memT", m, half), 2 * m + half, True)
    for h in range(H_MEM):
        bk.add(("mk", h), h, True)
    for m in range(NM):
        bk.add(("mv", m), 4 + m, True)
    for t in range(NT):
        for half in range(2):
            bk.add(("h1T", t, half), (2 * t + half) % 8, True)
    for h in range(H_MEM):
        bk.add(("mq", h), h, True)
    for s in range(H_MEM + 1):
        if s < H_MEM:
            for u in range(2):
                bk.add(("MS", s, u), 4 + u)
        if s > 0:
            for j in range(NM):
                bk.add(("MPT", s - 1, j), j, True)
            bk.add(("MPV", s - 1), 2, True)
    for n in range(2):
        for t in range(NT):
            bk.add(("mo", n, t), 4 * (1 - n) + t)
    for t in range(NT):
        for half in range(2):
            bk.add(("h2T", t, half), (2 * t + half) % 8, True)
    for f in range(NF):
        bk.add(("gate", f), 2 * (f % 4))
        bk.add(("up", f), 2 * (f % 4) + 1)
    for t in range(NT):
        for n in range(2):
            bk.add(("down", t, n), 2 * t + n)
    return bk.use


def build(nc, a, out):
    use = plan_banks()

    with ExitStack() as ctx:
        def sb(name, shape, dt=F32):
            return ctx.enter_context(nc.sbuf_tensor(name, shape, dt))

        def sem(name):
            return ctx.enter_context(nc.semaphore(name))

        w_raw = sb("w_raw", [P, RAW, SLOT])
        w_hi = sb("w_hi", [P, SPLIT, SLOT], F32R)
        w_lo = sb("w_lo", [P, SPLIT, SLOT], F32R)
        xt_hi = sb("xt_hi", [P, KD, SEQ], F32R)
        xt_lo = sb("xt_lo", [P, KD, SEQ], F32R)
        resid = sb("resid", [P, NT, D])
        work = sb("work", [P, 2, D])
        nat = sb("nat", [P, 2 * NT * NH * QK])
        arena = sb("arena", [P, NF * 2 * HALF], F32R)
        ident = sb("ident", [P, P])
        ident_bf = sb("ident_bf", [P, P], BF16)
        mask_bf = sb("mask_bf", [P, P], BF16)
        upto = sb("upto", [P, P])
        ones = sb("ones", [P, P])
        rope_tab = sb("rope_tab", [P, 4, NT, ROPE])
        rope_a = sb("rope_a", [P, 4, ROPE])
        rope_b = sb("rope_b", [P, 4, ROPE])
        krf = sb("krf", [P, NT, ROPE + NH])
        kro = sb("kro", [P, NT, ROPE])
        fbias = sb("fbias", [P, NH])
        fz = sb("fz", [P, NT, NH])
        fa = sb("fa", [P, NT, NH])
        fe = sb("fe", [P, NT, NH])
        fl = sb("fl", [P, NT, NH])
        logf = sb("logf", [P, NT, NH])
        g_out = sb("g_out", [P, NH])
        NNORM = 4 + 4 + 4 + 8 + 2 + 4 + 4 + 4
        ssq = sb("ssq", [P, NNORM])
        msq = sb("msq", [P, NNORM])
        rstd = sb("rstd", [P, NNORM])
        neg_half = sb("neg_half", [P, 4])
        neg_max = sb("neg_max", [P, 2 * NH, NT])
        row_sum = sb("row_sum", [P, 2 * NH, NT])
        row_inv = sb("row_inv", [P, 2 * NH, NT])

        resid_flat = resid[:, :, :].rearrange("p t n -> p (t n)")
        work_flat = work[:, :, :].rearrange("p t n -> p (t n)")
        nat_q = nat[:, 0:NT * NH * QK].rearrange("p (t h c) -> p t h c", t=NT, h=NH)
        nat_k = nat[:, NT * NH * QK:].rearrange("p (t h c) -> p t h c", t=NT, h=NH)
        g_mix = nat[:, 0:D]
        cn = resid_flat[:, 0:NT * 640].rearrange("p (t n) -> p t n", t=NT)
        g_lat = resid_flat[:, 2560:3200]
        ct_hi = xt_hi[:, 0:5, :]
        ct_lo = xt_lo[:, 0:5, :]
        mem_raw = nat[:, 0:NM * D].rearrange("p (m n) -> p m n", m=NM)
        g_memkv, g_memq, g_ffn, g_final = (nat[:, 2048 + i * D:3072 + i * D] for i in range(4))
        silu_buf = nat[:, 0:2 * HALF].rearrange("p (s n) -> p s n", s=2)
        h_buf = nat[:, 2 * HALF:4 * HALF].rearrange("p (s n) -> p s n", s=2)
        sq_acc = work_flat[:, 0:2 * HALF].rearrange("p (f n) -> p f n", f=2)
        sq_tmp = work_flat[:, 2 * HALF:4 * HALF].rearrange("p (f n) -> p f n", f=2)

        def region(start, *dims):
            n = int(np.prod(dims))
            ap = arena[:, start:start + n]
            if len(dims) == 2:
                ap = ap.rearrange("p (a b) -> p a b", a=dims[0])
            return ap

        qt_hi, qt_lo, kt_hi, kt_lo = (region(i * 1024, 2, HALF) for i in range(4))
        pt_hi, pt_lo = region(4096, 2, P_COLS), region(6656, 2, P_COLS)
        vm_hi, vm_lo = region(9216, NT, HALF), region(11264, NT, HALF)
        vf_hi, vf_lo = region(14336, NT, HALF), region(16384, NT, HALF)
        of_hi, of_lo = region(18432, NT, HALF), region(20480, NT, HALF)
        om_hi, om_lo = vf_hi, vf_lo
        mt_hi, mt_lo = region(0, KD, MEM), region(2048, KD, MEM)
        mk_hi, mk_lo = region(4096, H_MEM, MEM), region(5120, H_MEM, MEM)
        mv_hi, mv_lo = region(6144, NM, HALF), region(7168, NM, HALF)
        mq_hi, mq_lo = region(8192, H_MEM, HALF), region(10240, H_MEM, HALF)
        mp_hi, mp_lo = region(18432, 4, HALF), region(20480, 4, HALF)
        mo_hi, mo_lo = region(14336, H_MEM, HALF), region(16384, H_MEM, HALF)
        ht_hi, ht_lo = region(0, NF, HALF), region(NF * HALF, NF, HALF)

        bank = [ctx.enter_context(nc.psum_tensor(f"bank{i}", [P, HALF], F32)) for i in range(8)]

        bank_full = [sem(f"bank_full{i}") for i in range(8)]
        bank_hi = [sem(f"bank_hi{i}") for i in range(8)]
        bank_free = [sem(f"bank_free{i}") for i in range(8)]
        x_loaded = [sem(f"x_loaded{t}") for t in range(NT)]
        x_again = sem("x_again")
        consts_loaded = sem("consts_loaded")
        g_mix_loaded = sem("g_mix_loaded")
        g_lat_loaded = sem("g_lat_loaded")
        late_loaded = sem("late_loaded")
        w_loaded = [sem(f"w_loaded{i}") for i in range(RAW)]
        w_hi_done = sem("w_hi_done")
        w_lo_done = sem("w_lo_done")
        w_used = sem("w_used")
        consts_made = sem("consts_made")
        nat_cleared = sem("nat_cleared")
        ssq_ready = sem("ssq_ready")
        rstd_ready = sem("rstd_ready")
        xn_ready = sem("xn_ready")
        forget_z = sem("forget_z")
        forget_l = sem("forget_l")
        logf_ready = sem("logf_ready")
        krope_nat = sem("krope_nat")
        max_ready = sem("max_ready")
        exp_done = sem("exp_done")
        inv_ready = sem("inv_ready")
        probs_ready = sem("probs_ready")
        sq_ready = sem("sq_ready")
        sq_added = sem("sq_added")
        nope_taken = sem("nope_taken")
        resid_done = sem("resid_done")
        silu_done = sem("silu_done")
        h_done = sem("h_done")
        h_hi_done = sem("h_hi_done")
        h_lo_done = sem("h_lo_done")
        stored = [sem(f"stored{i}") for i in range(2)]
        act_chain = sem("act_chain")
        dve_chain = sem("dve_chain")
        pool_chain = sem("pool_chain")

        def rows(w):
            return w.rearrange("(k p) n -> p k n", p=P)

        slabs = []

        def slab(key, *pieces):
            slabs.append((key, pieces))

        w_in = rows(a["w_in"][0])
        for k in range(0, KD, 2):
            slab(("cq", k), (2, 384, 0, 384, w_in[:, k:k + 2, C_CQ:C_CQ + 384]))
        for k in range(0, KD, 2):
            slab(("ckv", k), (2, 296, 0, 288, w_in[:, k:k + 2, C_CKV:C_CKV + 288]),
                 (2, 296, 288, 296, w_in[:, k:k + 2, C_F:C_F + NH]))
        for name, c in (("vf", C_VF), ("qf", C_QF), ("kf", C_KF)):
            for k in range(0, KD, 2):
                slab((name, k), (2, 512, 0, 512, w_in[:, k:k + 2, c:c + 512]))
        for k in range(CQ):
            slab(("uq", k), (1, 768, 0, 768, rows(a["w_uq"][0])[:, k:k + 1, :]))
        for k in range(CKV):
            slab(("ukv", k), (1, 1024, 0, 1024, rows(a["w_ukv"][0])[:, k:k + 1, :]))
        w_o = rows(a["w_out"][0])
        for stage in range(4):
            k0, n0 = (4 if stage < 2 else 0), HALF * (stage % 2)
            for k in range(k0, k0 + 4, 2):
                slab(("out", stage, k), (2, 512, 0, 512, w_o[:, k:k + 2, n0:n0 + HALF]))
        w_mkv = a["w_mkv"][0].rearrange("(k p) (h s n) -> p k h s n", p=P, h=H_MEM, s=2)
        for h in range(H_MEM):
            slab(("mk", h), (KD, 128, 0, 128, w_mkv[:, :, h, 0, :]))
        for k in range(0, KD, 2):
            slab(("mv", k), *[(8, 128, 0, 128, (kk, w_mkv[:, k + kk, :, 1, :])) for kk in (0, 1)])
        for h in range(H_MEM):
            slab(("mq", h), (KD, 128, 0, 128, rows(a["w_mq"][0])[:, :, h * P:(h + 1) * P]))
        for n in range(2):
            for k in range(0, H_MEM, 2):
                slab(("mo", n, k), (2, 512, 0, 512, rows(a["w_mo"][0])[:, k:k + 2, n * HALF:(n + 1) * HALF]))
        for f in range(NF):
            for name in ("gate", "up"):
                slab((name, f), (KD, 128, 0, 128, rows(a[f"w_{name}"][0])[:, :, f * P:(f + 1) * P]))
        for k in range(NF):
            slab(("down", k), (1, 1024, 0, 1024, rows(a["w_down"][0])[:, k:k + 1, :]))
        NS = len(slabs)
        loads_upto, seen = [], [0] * RAW
        for n, (_, pieces) in enumerate(slabs):
            seen[n % RAW] += 16 * len(pieces)
            loads_upto.append(seen[n % RAW])
        number = {key: n for n, (key, _) in enumerate(slabs)}

        ends = {}
        for name in ("cq", "ckv", "vf", "qf", "kf"):
            ends[(name, KD - 2)] = (name, NT - 1)
        ends[("uq", CQ - 1)], ends[("ukv", CKV - 1)] = ("uq", NT - 1, 1), ("ukv", NT - 1, 1)
        for stage in range(4):
            ends[("out", stage, 6 if stage < 2 else 2)] = ("out", stage, NT - 1)
        for h in range(H_MEM):
            ends[("mk", h)], ends[("mq", h)] = ("mk", h), ("mq", h)
        ends[("mv", KD - 2)] = ("mv", NM - 1)
        for n in range(2):
            ends[("mo", n, H_MEM - 2)] = ("mo", n, NT - 1)
        for f in range(NF):
            ends[("gate", f)], ends[("up", f)] = ("gate", f), ("up", f)
        ends[("down", NF - 1)] = ("down", NT - 1, 1)
        released, count = [], 0
        for key, _ in slabs:
            if key in ends:
                b, turn, _ = use[ends[key]]
                released.append((bank_full[b], turn))
            else:
                count += 1
                released.append((w_used, count))

        def slab_cols(n):
            return slabs[n][1][0][0] * slabs[n][1][0][1]

        def split_of(key, k, c0, c1):
            n = number[key]
            width = slabs[n][1][0][1]
            s = slice(k * width + c0, k * width + c1)
            return w_hi[:, n % SPLIT, s], w_lo[:, n % SPLIT, s]

        N_X, N_CQ, N_CKV, N_OUT, N_MEM, N_H1, N_H2, N_H3 = 0, 4, 8, 12, 20, 22, 26, 30
        def ssq_step(col):
            return col + 1 if col < N_OUT else col - 7

        def norm_step(col):
            return col + 1 if col < N_OUT else (13 + (col - N_OUT) // 4 if col < N_MEM else col - 5)

        XN_X, XN_MEM, XN_H1, XN_H2, XN_H3 = 0, 4, 6, 10, 14

        block = ctx.enter_context(nc.Block())

        @block.sync
        def _(sp):
            def load_slab(n):
                key, pieces = slabs[n]
                slot = n % RAW
                if n >= RAW:
                    sp.wait_ge(w_lo_done, n - RAW + 1)
                for kk, width, c0, c1, src in pieces:
                    dst = w_raw[:, slot, 0:kk * width].rearrange("p (k n) -> p k n", k=kk)[:, :, c0:c1]
                    if isinstance(src, tuple):
                        dst = dst[:, 4 * src[0]:4 * src[0] + 4, :]
                        src = src[1]
                    sp.dma_start(dst, src).then_inc(w_loaded[slot], 16)

            for t in range(NT):
                sp.dma_start(resid[:, t, :], a["x"][0, t * P:(t + 1) * P, :]).then_inc(x_loaded[t], 16)
                if t == 0:
                    sp.dma_start(g_mix, a["mix_norm_g"].partition_broadcast(P)[:, 0, :]).then_inc(g_mix_loaded, 16)
            for n in range(RAW):
                load_slab(n)
            sp.dma_start(fbias[:, :], a["forget_bias"].partition_broadcast(P)[:, 0, :]).then_inc(consts_loaded, 16)
            sp.dma_start(rope_tab[:, :, :, :], a["rope"].rearrange("s (t p) c -> p s t c", p=P)).then_inc(consts_loaded, 16)
            sp.dma_start(g_out[:, 0:4], a["fox_out_g"][0].rearrange("(c p) -> p c", p=P),
                         allow_slow_non_contiguous=True).then_inc(consts_loaded, 16)
            sp.dma_start(g_out[:, 4:8], a["mla_out_g"][0].rearrange("(c p) -> p c", p=P),
                         allow_slow_non_contiguous=True).then_inc(consts_loaded, 16)
            sp.wait_ge(xn_ready, XN_X + NT)
            sp.dma_start(g_lat[:, 0:Q_LORA], a["cq_norm_g"].partition_broadcast(P)[:, 0, :]).then_inc(g_lat_loaded, 16)
            sp.dma_start(g_lat[:, Q_LORA:640], a["ckv_norm_g"].partition_broadcast(P)[:, 0, :]).then_inc(g_lat_loaded, 16)
            first_late = number[("out", 0, 4)] + RAW
            for n in range(RAW, first_late):
                load_slab(n)
            b, n_turn, _ = use[("KT", 2 * NH - 1)]
            sp.wait_ge(bank_full[b], n_turn)
            sp.dma_start(mem_raw, a["mem"][0].rearrange("(m p) n -> p m n", p=P)).then_inc(late_loaded, 16)
            for g, name in ((g_memkv, "mem_kv_norm_g"), (g_memq, "mem_q_norm_g"), (g_ffn, "ffn_norm_g")):
                sp.dma_start(g, a[name].partition_broadcast(P)[:, 0, :]).then_inc(late_loaded, 16)
            sp.dma_start(g_final, a["final_norm_g"].partition_broadcast(P)).then_inc(late_loaded, 16)
            b, n_turn, _ = use[("PT", 2 * NH - 1, 2)]
            sp.wait_ge(bank_full[b], n_turn)
            sp.dma_start(resid[:, :, :], a["x"][0].rearrange("(t p) n -> p t n", p=P)).then_inc(x_again, 16)
            for n in range(first_late, NS):
                load_slab(n)
            for t in range(NT):
                sp.wait_ge(xn_ready, XN_H3 + t + 1)
                sp.dma_start(out[0, t * P:(t + 1) * P, :], work[:, t % 2, :]).then_inc(stored[t % 2], 16)
            for i in range(2):
                sp.wait_ge(stored[i], 16 * (NT // 2))

        @block.gpsimd
        def _(pool):
            pool.memset(neg_half[:, :], -0.5).then_inc(pool_chain, 1)
            pool.memset(ones[:, :], 1.0).then_inc(pool_chain, 1)
            pool.memset(ident[:, :], 0.0).then_inc(pool_chain, 1)
            pool.memset(ident_bf[:, :], 0.0).then_inc(pool_chain, 1)
            pool.memset(mask_bf[:, :], 0.0).then_inc(pool_chain, 1)
            pool.wait_ge(pool_chain, 5)
            for m in (ident, ident_bf):
                pool.affine_select(out=m[:, :], in_=m[:, :], compare_op=ALU.not_equal, fill=1.0, base=0,
                                   pattern=[[-1, P]], channel_multiplier=1).then_inc(consts_made, 1)
            pool.affine_select(out=mask_bf[:, :], in_=mask_bf[:, :], compare_op=ALU.is_ge, fill=MASKED, base=0,
                               pattern=[[-1, P]], channel_multiplier=1).then_inc(consts_made, 1)
            pool.affine_select(out=upto[:, :], in_=ones[:, :], compare_op=ALU.is_ge, fill=0.0, base=0,
                               pattern=[[1, P]], channel_multiplier=-1).then_inc(consts_made, 1)
            chain = [5]

            def link(ins):
                chain[0] += 1
                ins.then_inc(pool_chain, 1)
                pool.wait_ge(pool_chain, chain[0])

            def make_rstd(col, width, dim):
                if N_OUT <= col < N_MEM:
                    b, n, _ = use[("ssq", (col - N_OUT) // 4)]
                    pool.wait_ge(bank_free[b], n)
                else:
                    pool.wait_ge(ssq_ready, ssq_step(col))
                c = slice(col, col + width)
                link(pool.tensor_scalar(msq[:, c], ssq[:, c], 1.0 / dim, EPS, ALU.mult, ALU.add))
                pool.tensor_tensor(rstd[:, c], msq[:, c], neg_half[:, 0:width], ALU.pow).then_inc(rstd_ready, 1)

            for t in range(NT):
                make_rstd(N_X + t, 1, D)
            pool.wait_ge(xn_ready, XN_X + NT)
            link(pool.memset(nat[:, :], 0.0))
            pool.memset(nat_q[:, :, :, HD + 1:HD + 2], 1.0).then_inc(nat_cleared, 1)
            pool.memset(nat_k[:, :, :, HD:HD + 1], 1.0).then_inc(nat_cleared, 1)
            for t in range(NT):
                make_rstd(N_CQ + t, 1, Q_LORA)
            for t in range(NT):
                make_rstd(N_CKV + t, 1, KV_LORA)

            def normalise(g, i):
                n = 4 * g + (3 - i)
                pool.wait_ge(inv_ready, n + 1)
                s = (g % 2) * P_COLS + P_OFF[i]
                p = resid_flat[:, s:s + P * (i + 1)]
                pool.tensor_scalar(p, p, row_inv[:, g, i:i + 1], None, ALU.mult).then_inc(probs_ready, 1)

            def add_squares(g):
                if g % 2 == 0:
                    return
                fam, pair = g // NH, (g % NH) // 2
                pool.wait_ge(sq_ready, g + 1)
                if pair == 0:
                    pool.tensor_copy(sq_acc[:, fam, :], sq_tmp[:, (g // 2) % 2, :]).then_inc(sq_added, 1)
                else:
                    pool.wait_ge(sq_added, g // 2)
                    pool.tensor_tensor(sq_acc[:, fam, :], sq_acc[:, fam, :], sq_tmp[:, (g // 2) % 2, :],
                                       ALU.add).then_inc(sq_added, 1)

            for fam in range(2):
                for g in range(fam * NH, (fam + 1) * NH):
                    for i in (3, 2, 1, 0):
                        normalise(g, i)
                    if g > fam * NH:
                        add_squares(g - 1)
                add_squares((fam + 1) * NH - 1)
                make_rstd(N_OUT + 4 * fam, 4, HALF)
            for m in range(NM):
                make_rstd(N_MEM + m, 1, D)
            for base in (N_H1, N_H2, N_H3):
                for t in range(NT):
                    make_rstd(base + t, 1, D)

        @block.scalar
        def _(act):
            chain = [0]

            def full(key):
                b, n, _ = use[key]
                act.wait_ge(bank_full[b], n)
                return b

            def take_hi(key, dst, rows_=slice(0, P), cols=slice(0, HALF), scale=1.0, view=None):
                b = full(key)
                src = bank[b][rows_, cols]
                if view:
                    src = view(src)
                act.activation(dst, src, ACT.Copy, scale=scale).then_inc(bank_hi[b], 1)

            def summed(key):
                b, n, _ = use[key]
                act.wait_ge(bank_free[b], n)

            def split_slab(n):
                if n >= NS:
                    return
                cols = slab_cols(n)
                act.wait_ge(w_loaded[n % RAW], loads_upto[n])
                if n >= SPLIT:
                    act.wait_ge(*released[n - SPLIT])
                act.activation(w_hi[:, n % SPLIT, 0:cols], w_raw[:, n % RAW, 0:cols], ACT.Copy).then_inc(w_hi_done, 1)

            def square_rows(src, junk, col):
                act.activation(junk, src, ACT.Square, accum_out=ssq[:, col:col + 1]).then_inc(ssq_ready, 1)

            def take_transposed(name, t, hi):
                for half in range(2):
                    take_hi((name, t, half), hi[:, 4 * half:4 * half + 4, t * P:(t + 1) * P],
                            view=lambda s: s.rearrange("p (c n) -> p c n", c=4))

            for t in range(NT):
                act.wait_ge(x_loaded[t], 16)
                if t >= 2:
                    b, n, _ = use[("xT", t - 2, 1)]
                    act.wait_ge(bank_full[b], n)
                square_rows(resid[:, t, :], work[:, t % 2, :], N_X + t)
                if t >= 1:
                    take_transposed("xT", t - 1, xt_hi)
            take_transposed("xT", NT - 1, xt_hi)
            split_slab(0)
            split_slab(1)

            def eat(keys):
                for key in keys:
                    if number[key] >= 1:
                        split_slab(number[key] + 1)

            eat([("cq", k) for k in range(0, KD, 2)])
            act.wait_ge(xn_ready, XN_X + NT)
            for t in range(NT):
                b = full(("cq", t))
                square_rows(bank[b][:, 0:Q_LORA], cn[:, t, 0:Q_LORA], N_CQ + t)
            eat([("ckv", k) for k in range(0, KD, 2)])
            for t in range(NT):
                b = full(("ckv", t))
                act.activation(krf[:, t, :], bank[b][:, KV_LORA:KV_LORA + ROPE + NH], ACT.Copy).then_inc(forget_z, 1)
                square_rows(bank[b][:, 0:KV_LORA], cn[:, t, Q_LORA:640], N_CKV + t)
            act.wait_ge(forget_z, NT + 1)
            act.activation(fe[:, :, :], fa[:, :, :], ACT.Exp, scale=-1.0).then_inc(act_chain, 1)
            act.wait_ge(act_chain, 1)
            act.activation(fl[:, :, :], fe[:, :, :], ACT.Ln, bias=1.0).then_inc(forget_l, 1)
            eat([("vf", k) for k in range(0, KD, 2)])
            for t in range(NT):
                take_hi(("vf", t), vf_hi[:, t, :])
            eat([("qf", k) for k in range(0, KD, 2)])
            act.wait_ge(nat_cleared, 2)
            for t in range(NT):
                b = full(("qf", t))
                act.activation(nat_q[:, t, :, 0:HD], bank[b][:, :].rearrange("p (h c) -> p h c", h=NH), ACT.Copy,
                               scale=-FOX_SCALE).then_inc(bank_free[b], 1)
            eat([("kf", k) for k in range(0, KD, 2)])
            for t in range(NT):
                b = full(("kf", t))
                act.activation(nat_k[:, t, :, 0:HD], bank[b][:, :].rearrange("p (h c) -> p h c", h=NH),
                               ACT.Copy).then_inc(bank_free[b], 1)
            for c in range(CQ + CKV):
                take_hi(("cT", c), ct_hi[:, c, :])

            def exp_scores(g, i):
                b, n, _ = use[("S", g, i)]
                act.wait_ge(max_ready, 4 * g + (3 - i) + 1)
                s = (g % 2) * P_COLS + P_OFF[i]
                w = P * (i + 1)
                act.activation(resid_flat[:, s:s + w], bank[b][:, 0:w], ACT.Exp, scale=-1.0,
                               bias=neg_max[:, g, i:i + 1],
                               accum_out=row_sum[:, g, i:i + 1]).then_inc(bank_free[b], 1)

            def pt_hi_half(g, part):
                lo, hi = ((0, 512), (512, 1024), (1024, 1280))[part]
                take_hi(("PT", g, part), pt_hi[:, g % 2, lo:hi], cols=slice(0, hi - lo))

            def attention(first, last, o_hi):
                def qk_hi(g):
                    take_hi(("QT", g), qt_hi[0:QK, g % 2, :], rows_=slice(0, QK))
                    take_hi(("KT", g), kt_hi[0:QK, g % 2, :], rows_=slice(0, QK))

                def head_out(g):
                    r = slice(HD * (g % 2), HD * (g % 2) + HD)
                    b, n, m = use[("PV", g)]
                    act.wait_ge(bank_full[b], n)
                    if g >= 4 and g % 2 == 0:
                        act.wait_ge(sq_added, (g - 4) // 2 + 1)
                    act.activation(sq_tmp[r, (g // 2) % 2, :], bank[b][r, :], ACT.Square).then_inc(sq_ready, 1)
                    act.activation(o_hi[r, (g % NH) // 2, :], bank[b][r, :], ACT.Copy,
                                   scale=g_out[r, g // 2:g // 2 + 1]).then_inc(bank_hi[b], 1)

                qk_hi(first)
                for g in list(range(first, last + 1)) + [None]:
                    prev = last if g is None else (g - 1 if g > first else None)
                    for i in (3, 2, 1, 0):
                        if g is not None:
                            exp_scores(g, i)
                        if prev is not None and i < 3:
                            pt_hi_half(prev, 2 - i)
                    if g is not None and g < last:
                        qk_hi(g + 1)
                    if prev is not None:
                        head_out(prev)

            def take_ssq(fam):
                b = full(("ssq", fam))
                act.activation(ssq[:, N_OUT + 4 * fam:N_OUT + 4 * fam + 4], bank[b][:, 0:4],
                               ACT.Copy).then_inc(bank_free[b], 1)

            act.wait_ge(consts_loaded, 64)
            attention(0, NH - 1, of_hi)
            take_ssq(0)
            eat([("uq", k) for k in range(CQ)])
            for t in range(NT):
                for n in range(2):
                    b = full(("uq", t, n))
                    act.activation(nat_q[:, t, 4 * n:4 * n + 4, 0:HD],
                                   bank[b][:, 0:384].rearrange("p (h c) -> p h c", h=4)[:, :, 0:HD], ACT.Copy,
                                   scale=-MLA_SCALE).then_inc(nope_taken, 1)
            eat([("ukv", k) for k in range(CKV)])
            for t in range(NT):
                for n in range(2):
                    b = full(("ukv", t, n))
                    kv = bank[b][:, :].rearrange("p (h s c) -> p h s c", h=4, s=2)
                    act.activation(nat_k[:, t, 4 * n:4 * n + 4, 0:HD], kv[:, :, 0, :], ACT.Copy).then_inc(act_chain, 1)
                    act.activation(vm_hi[:, t, 256 * n:256 * n + 256].rearrange("p (h c) -> p h c", h=4),
                                   kv[:, :, 1, :], ACT.Copy).then_inc(bank_hi[b], 1)
            attention(NH, 2 * NH - 1, om_hi)
            take_ssq(1)
            for stage in range(4):
                eat([("out", stage, k) for k in ((4, 6) if stage < 2 else (0, 2))])
                if stage == 0:
                    act.wait_ge(late_loaded, 80)
                    summed(("out", 0, 0))
                    for m in range(NM):
                        square_rows(mem_raw[:, m, :], work[:, m, :], N_MEM + m)
            for m in range(NM):
                take_transposed("memT", m, mt_hi)
            eat([("mk", 0), ("mk", 1)])
            b, n, _ = use[("memT", NM - 1, 1)]
            for t in range(2):
                summed(("out", 3, t))
                act.wait_ge(bank_full[b], n)
                square_rows(resid[:, t, :], work[:, t % 2, :], N_H1 + t)
            eat([("mk", 2), ("mk", 3)])
            for h in range(H_MEM):
                take_hi(("mk", h), mk_hi[:, h, :], cols=slice(0, MEM))
            eat([("mv", k) for k in range(0, KD, 2)])
            for m in range(NM):
                take_hi(("mv", m), mv_hi[:, m, :])
            for t in range(NT):
                take_transposed("h1T", t, xt_hi)
                if t + 2 < NT:
                    summed(("out", 3, t + 2))
                    b, n, _ = use[("h1T", t, 1)]
                    act.wait_ge(bank_full[b], n)
                    square_rows(resid[:, t + 2, :], work[:, t % 2, :], N_H1 + t + 2)
            for h in range(H_MEM):
                eat([("mq", h)])
                take_hi(("mq", h), mq_hi[:, h, :], scale=-MEM_SCALE)
            for s in range(H_MEM + 1):
                if s < H_MEM:
                    for u in range(2):
                        b = use[("MS", s, u)][0]
                        act.wait_ge(max_ready, 64 + 2 * s + u + 1)
                        for i in range(2):
                            t = 2 * u + i
                            p = work_flat[:, (s % 2) * D + t * MEM:(s % 2) * D + (t + 1) * MEM]
                            ins = act.activation(p, bank[b][:, i * MEM:(i + 1) * MEM], ACT.Exp, scale=-1.0,
                                                 bias=neg_max[:, s, t:t + 1], accum_out=row_sum[:, s, t:t + 1])
                            if i:
                                ins.then_inc(bank_free[b], 1)
                if s > 0:
                    for j in range(NM):
                        take_hi(("MPT", s - 1, j), mp_hi[:, 2 * ((s - 1) % 2) + j, :])
                    take_hi(("MPV", s - 1), mo_hi[:, s - 1, :])
            for n in range(2):
                eat([("mo", n, k) for k in range(0, H_MEM, 2)])
            for t in range(NT):
                summed(("mo", 1, t))
                if t >= 2:
                    b, n, _ = use[("h2T", t - 2, 1)]
                    act.wait_ge(bank_full[b], n)
                square_rows(resid[:, t, :], work[:, t % 2, :], N_H2 + t)
                if t >= 1:
                    take_transposed("h2T", t - 1, xt_hi)
            take_transposed("h2T", NT - 1, xt_hi)

            def act_ffn(f):
                b, n, _ = use[("gate", f)]
                act.wait_ge(bank_full[b], n)
                if f >= 2:
                    act.wait_ge(h_done, f - 1)
                act.activation(silu_buf[:, f % 2, :], bank[b][:, :], ACT.Silu).then_inc(silu_done, 1)
                act.wait_ge(h_done, f + 1)
                act.activation(ht_hi[:, f, :], h_buf[:, f % 2, :], ACT.Copy).then_inc(h_hi_done, 1)

            for f in range(NF):
                eat([("gate", f), ("up", f)])
                if f >= 1:
                    act_ffn(f - 1)
            eat([("down", 0)])
            act_ffn(NF - 1)
            eat([("down", k) for k in range(1, NF)])
            for t in range(NT):
                act.wait_ge(resid_done, t + 1)
                if t >= 2:
                    act.wait_ge(stored[t % 2], 16)
                square_rows(resid[:, t, :], work[:, t % 2, :], N_H3 + t)

        @block.vector
        def _(dve):
            chain = [0]

            def link(ins):
                chain[0] += 1
                ins.then_inc(dve_chain, 1)
                dve.wait_ge(dve_chain, chain[0])

            def take_lo(key, dst, hi, rows_=slice(0, P), cols=slice(0, HALF), scale=None, view=None):
                b, n, m = use[key]
                dve.wait_ge(bank_hi[b], m)
                src = bank[b][rows_, cols]
                if view:
                    src = view(src)
                if scale is None:
                    dve.tensor_tensor(dst, src, hi.bitcast(F32), ALU.subtract).then_inc(bank_free[b], 1)
                else:
                    dve.scalar_tensor_tensor(dst, src, scale, hi.bitcast(F32), ALU.mult,
                                             ALU.subtract).then_inc(bank_free[b], 1)

            def split_slab(n):
                if n >= NS:
                    return
                cols = slab_cols(n)
                dve.wait_ge(w_hi_done, n + 1)
                dve.tensor_tensor(w_lo[:, n % SPLIT, 0:cols], w_raw[:, n % RAW, 0:cols],
                                  w_hi[:, n % SPLIT, 0:cols].bitcast(F32), ALU.subtract).then_inc(w_lo_done, 1)

            def eat(keys):
                for key in keys:
                    if number[key] >= 1:
                        split_slab(number[key] + 1)

            def norm_rows(dst, src, col, gain):
                dve.wait_ge(rstd_ready, norm_step(col))
                return dve.scalar_tensor_tensor(dst, src, rstd[:, col:col + 1], gain, ALU.mult, ALU.mult)

            def take_transposed(name, t, hi, lo):
                for half in range(2):
                    s = (slice(None), slice(4 * half, 4 * half + 4), slice(t * P, (t + 1) * P))
                    take_lo((name, t, half), lo[s], hi[s], view=lambda x: x.rearrange("p (c n) -> p c n", c=4))

            dve.wait_ge(g_mix_loaded, 16)
            for t in range(NT):
                norm_rows(work[:, t % 2, :], resid[:, t, :], N_X + t, g_mix).then_inc(xn_ready, 1)
                if t >= 1:
                    take_transposed("xT", t - 1, xt_hi, xt_lo)
            take_transposed("xT", NT - 1, xt_hi, xt_lo)
            split_slab(0)
            split_slab(1)
            eat([("cq", k) for k in range(0, KD, 2)])
            dve.wait_ge(g_lat_loaded, 32)
            for t in range(NT):
                b = use[("cq", t)][0]
                norm_rows(cn[:, t, 0:Q_LORA], bank[b][:, 0:Q_LORA], N_CQ + t,
                          g_lat[:, 0:Q_LORA]).then_inc(bank_free[b], 1)
            eat([("ckv", k) for k in range(0, KD, 2)])
            for t in range(NT):
                b = use[("ckv", t)][0]
                norm_rows(cn[:, t, Q_LORA:640], bank[b][:, 0:KV_LORA], N_CKV + t,
                          g_lat[:, Q_LORA:640]).then_inc(bank_free[b], 1)
            dve.wait_ge(consts_loaded, 64)
            dve.wait_ge(forget_z, NT)
            link(dve.tensor_tensor(fz[:, :, :], krf[:, :, ROPE:], fbias[:, :].unsqueeze(1).to_broadcast([P, NT, NH]), ALU.add))
            dve.scalar_tensor_tensor(fa[:, :, :], fz[:, :, :], -1.0, fz[:, :, :], ALU.mult,
                                     ALU.max).then_inc(forget_z, 1)
            x1, x2 = krf[:, :, 0:16], krf[:, :, 16:32]
            cos, sin = rope_tab[:, 2, :, 0:16], rope_tab[:, 3, :, 0:16]
            ra, rb = rope_a[:, :, :], rope_b[:, :, :]
            link(dve.tensor_tensor(ra[:, :, 0:16], x1, cos, ALU.mult))
            link(dve.tensor_tensor(ra[:, :, 16:32], x2, cos, ALU.mult))
            link(dve.tensor_tensor(rb[:, :, 0:16], x2, sin, ALU.mult))
            link(dve.tensor_tensor(rb[:, :, 16:32], x1, sin, ALU.mult))
            link(dve.tensor_tensor(kro[:, :, 0:16], ra[:, :, 0:16], rb[:, :, 0:16], ALU.subtract))
            link(dve.tensor_tensor(kro[:, :, 16:32], ra[:, :, 16:32], rb[:, :, 16:32], ALU.add))
            dve.wait_ge(forget_l, 1)
            dve.scalar_tensor_tensor(logf[:, :, :], fz[:, :, :], 0.0, fl[:, :, :], ALU.min,
                                     ALU.subtract).then_inc(logf_ready, 1)
            eat([("vf", k) for k in range(0, KD, 2)])
            for t in range(NT):
                take_lo(("vf", t), vf_lo[:, t, :], vf_hi[:, t, :])
            b, n, _ = use[("cum",)]
            dve.wait_ge(bank_full[b], n)
            dve.wait_ge(nat_cleared, 2)
            cum = bank[b][:, 0:NT * NH].rearrange("p (t h) -> p t h", t=NT)
            dve.tensor_scalar(nat_q[:, :, :, HD], cum, -1.0, None, ALU.mult).then_inc(krope_nat, 1)
            dve.tensor_copy(nat_k[:, :, :, HD + 1], cum).then_inc(bank_free[b], 1)
            eat([("qf", k) for k in range(0, KD, 2)])
            eat([("kf", k) for k in range(0, KD, 2)])
            for c in range(CQ + CKV):
                take_lo(("cT", c), ct_lo[:, c, :], ct_hi[:, c, :])

            def negated_max(g, i):
                b, n, _ = use[("S", g, i)]
                dve.wait_ge(bank_full[b], n)
                dve.tensor_reduce(neg_max[:, g, i:i + 1], bank[b][:, 0:P * (i + 1)], AX.X,
                                  ALU.min).then_inc(max_ready, 1)

            def invert(g, i):
                b, n, _ = use[("S", g, i)]
                dve.wait_ge(bank_free[b], n)
                dve.reciprocal(row_inv[:, g, i:i + 1], row_sum[:, g, i:i + 1]).then_inc(inv_ready, 1)

            def pt_lo_half(g, part):
                lo, hi = ((0, 512), (512, 1024), (1024, 1280))[part]
                take_lo(("PT", g, part), pt_lo[:, g % 2, lo:hi], pt_hi[:, g % 2, lo:hi], cols=slice(0, hi - lo))

            def attention(first, last, o_hi, o_lo):
                def qk_lo(g):
                    r = slice(0, QK)
                    take_lo(("QT", g), qt_lo[r, g % 2, :], qt_hi[r, g % 2, :], rows_=r)
                    take_lo(("KT", g), kt_lo[r, g % 2, :], kt_hi[r, g % 2, :], rows_=r)

                def head_out(g):
                    r = slice(HD * (g % 2), HD * (g % 2) + HD)
                    c = (g % NH) // 2
                    take_lo(("PV", g), o_lo[r, c, :], o_hi[r, c, :], rows_=r, scale=g_out[r, g // 2:g // 2 + 1])

                qk_lo(first)
                for g in list(range(first, last + 1)) + [None]:
                    prev = last if g is None else (g - 1 if g > first else None)
                    for i in (3, 2, 1, 0):
                        if g is not None:
                            negated_max(g, i)
                            if i < 3:
                                invert(g, i + 1)
                        if prev is not None and i < 3:
                            pt_lo_half(prev, 2 - i)
                    if g is not None:
                        invert(g, 0)
                        if g < last:
                            qk_lo(g + 1)
                    if prev is not None:
                        head_out(prev)

            attention(0, NH - 1, of_hi, of_lo)
            b, n, _ = use[("KT", NH - 1)]
            dve.wait_ge(bank_full[b], n)
            dve.tensor_copy(nat_k[:, :, :, HD:QK],
                            kro[:, :, :].unsqueeze(2).to_broadcast([P, NT, NH, ROPE])).then_inc(krope_nat, 1)
            eat([("uq", k) for k in range(CQ)])
            for t in range(NT):
                for n in range(2):
                    b, _, _ = use[("uq", t, n)]
                    dve.wait_ge(nope_taken, 2 * t + n + 1)
                    if t or n:
                        before, turn, _ = use[("uq", t, 0) if n else ("uq", t - 1, 1)]
                        dve.wait_ge(bank_free[before], turn)
                    src = bank[b][:, 0:384].rearrange("p (h c) -> p h c", h=4)[:, :, HD:QK]
                    link(dve.tensor_tensor(ra, src, rope_tab[:, 0, t, :].unsqueeze(1).to_broadcast([P, 4, ROPE]), ALU.mult))
                    link(dve.tensor_tensor(rb, src, rope_tab[:, 1, t, :].unsqueeze(1).to_broadcast([P, 4, ROPE]), ALU.mult))
                    dst = nat_q[:, t, 4 * n:4 * n + 4, HD:QK]
                    link(dve.tensor_tensor(dst[:, :, 0:16], ra[:, :, 0:16], rb[:, :, 16:32], ALU.subtract))
                    dve.tensor_tensor(dst[:, :, 16:32], ra[:, :, 16:32], rb[:, :, 0:16],
                                      ALU.add).then_inc(bank_free[b], 1)
            eat([("ukv", k) for k in range(CKV)])
            for t in range(NT):
                for n in range(2):
                    s = slice(256 * n, 256 * n + 256)
                    take_lo(("ukv", t, n), vm_lo[:, t, s].rearrange("p (h c) -> p h c", h=4),
                            vm_hi[:, t, s].rearrange("p (h c) -> p h c", h=4),
                            view=lambda x: x.rearrange("p (h s c) -> p h s c", h=4, s=2)[:, :, 1, :])
            attention(NH, 2 * NH - 1, om_hi, om_lo)
            dve.wait_ge(x_again, 16)
            for stage in range(4):
                eat([("out", stage, k) for k in ((4, 6) if stage < 2 else (0, 2))])
                fam, s = stage // 2, slice(HALF * (stage % 2), HALF * (stage % 2) + HALF)
                dve.wait_ge(rstd_ready, norm_step(N_OUT + 4 * fam))
                for t in range(NT):
                    b, n, _ = use[("out", stage, t)]
                    if stage >= 2:
                        before, turn, _ = use[("out", stage - 2, t)]
                        dve.wait_ge(bank_free[before], turn)
                    dve.wait_ge(bank_full[b], n)
                    dve.scalar_tensor_tensor(resid[:, t, s], bank[b][:, :],
                                             rstd[:, N_OUT + 4 * fam + t:N_OUT + 4 * fam + t + 1], resid[:, t, s],
                                             ALU.mult, ALU.add).then_inc(bank_free[b], 1)
                if stage == 0:
                    for m in range(NM):
                        norm_rows(work[:, m, :], mem_raw[:, m, :], N_MEM + m, g_memkv).then_inc(xn_ready, 1)
            for m in range(NM):
                take_transposed("memT", m, mt_hi, mt_lo)
            eat([("mk", 0), ("mk", 1)])
            for t in range(2):
                norm_rows(work[:, t, :], resid[:, t, :], N_H1 + t, g_memq).then_inc(xn_ready, 1)
            eat([("mk", 2), ("mk", 3)])
            for h in range(H_MEM):
                take_lo(("mk", h), mk_lo[:, h, :], mk_hi[:, h, :], cols=slice(0, MEM))
            eat([("mv", k) for k in range(0, KD, 2)])
            for m in range(NM):
                take_lo(("mv", m), mv_lo[:, m, :], mv_hi[:, m, :])
            for t in range(NT):
                take_transposed("h1T", t, xt_hi, xt_lo)
                if t + 2 < NT:
                    norm_rows(work[:, t % 2, :], resid[:, t + 2, :], N_H1 + t + 2, g_memq).then_inc(xn_ready, 1)
            for h in range(H_MEM):
                eat([("mq", h)])
                take_lo(("mq", h), mq_lo[:, h, :], mq_hi[:, h, :], scale=-MEM_SCALE)
            for s in range(H_MEM + 1):
                if s < H_MEM:
                    for u in range(2):
                        b, n, _ = use[("MS", s, u)]
                        dve.wait_ge(bank_full[b], n)
                        dve.tensor_reduce(neg_max[:, s, 2 * u:2 * u + 2],
                                          bank[b][:, :].rearrange("p (i k) -> p i k", i=2), AX.X,
                                          ALU.min).then_inc(max_ready, 1)
                if s > 0:
                    for j in range(NM):
                        take_lo(("MPT", s - 1, j), mp_lo[:, 2 * ((s - 1) % 2) + j, :], mp_hi[:, 2 * ((s - 1) % 2) + j, :])
                if s < H_MEM:
                    b, n, _ = use[("MS", s, 1)]
                    dve.wait_ge(bank_free[b], n)
                    b, n, _ = use[("MS", s, 0)]
                    dve.wait_ge(bank_free[b], n)
                    link(dve.reciprocal(row_inv[:, s, :], row_sum[:, s, :]))
                    for t in range(NT):
                        p = work_flat[:, (s % 2) * D + t * MEM:(s % 2) * D + (t + 1) * MEM]
                        dve.tensor_scalar(p, p, row_inv[:, s, t:t + 1], None, ALU.mult).then_inc(inv_ready, 1)
                if s > 0:
                    take_lo(("MPV", s - 1), mo_lo[:, s - 1, :], mo_hi[:, s - 1, :])
            for n in range(2):
                eat([("mo", n, k) for k in range(0, H_MEM, 2)])
                for t in range(NT):
                    b, turn, _ = use[("mo", n, t)]
                    dve.wait_ge(bank_full[b], turn)
                    s = slice(n * HALF, (n + 1) * HALF)
                    dve.tensor_tensor(resid[:, t, s], bank[b][:, :], resid[:, t, s],
                                      ALU.add).then_inc(bank_free[b], 1)
            for t in range(NT):
                norm_rows(work[:, t % 2, :], resid[:, t, :], N_H2 + t, g_ffn).then_inc(xn_ready, 1)
                if t >= 1:
                    take_transposed("h2T", t - 1, xt_hi, xt_lo)
            take_transposed("h2T", NT - 1, xt_hi, xt_lo)

            def dve_ffn(f):
                b, n, _ = use[("up", f)]
                bg = use[("gate", f)][0]
                dve.wait_ge(bank_full[b], n)
                dve.wait_ge(silu_done, f + 1)
                if f >= 2:
                    dve.wait_ge(h_lo_done, f - 1)
                    dve.wait_ge(h_hi_done, f - 1)
                dve.tensor_tensor(h_buf[:, f % 2, :], bank[b][:, :], silu_buf[:, f % 2, :], ALU.mult).then_inc(h_done, 1)
                dve.wait_ge(h_hi_done, f + 1)
                dve.tensor_tensor(ht_lo[:, f, :], h_buf[:, f % 2, :], ht_hi[:, f, :].bitcast(F32),
                                  ALU.subtract).then_inc(h_lo_done, 1)

            for f in range(NF):
                eat([("gate", f), ("up", f)])
                if f >= 1:
                    dve_ffn(f - 1)
            eat([("down", 0)])
            dve_ffn(NF - 1)
            eat([("down", k) for k in range(1, NF)])
            for t in range(NT):
                for n in range(2):
                    b, turn, _ = use[("down", t, n)]
                    dve.wait_ge(bank_full[b], turn)
                    s = slice(n * HALF, (n + 1) * HALF)
                    ins = dve.tensor_tensor(resid[:, t, s], bank[b][:, :], resid[:, t, s], ALU.add)
                    if n == 1:
                        ins.then_inc(resid_done, 1)
                    else:
                        ins.then_inc(dve_chain, 1)
                        chain[0] += 1
                if t >= 1:
                    norm_rows(work[:, (t - 1) % 2, :], resid[:, t - 1, :], N_H3 + t - 1, g_final).then_inc(xn_ready, 1)
            norm_rows(work[:, (NT - 1) % 2, :], resid[:, NT - 1, :], N_H3 + NT - 1, g_final).then_inc(xn_ready, 1)

        @block.tensor
        def _(pe):
            def claim(key):
                b, n, _ = use[key]
                if n > 1:
                    pe.wait_ge(bank_free[b], n - 1)
                return b

            def ready(key):
                b, n, _ = use[key]
                pe.wait_ge(bank_free[b], n)

            def product(dst, a_hi, a_lo, b_hi, b_lo, first, last):
                pe.matmul(dst, a_hi, b_hi, start=first, stop=False, skip_group_check=True)
                pe.matmul(dst, a_hi, b_lo, start=False, stop=False, skip_group_check=True)
                return pe.matmul(dst, a_lo, b_hi, start=False, stop=last, skip_group_check=True)

            def slab_ready(key):
                pe.wait_ge(w_lo_done, number[key] + 1)

            def transpose_rows(name, t, row):
                for half in range(2):
                    b = claim((name, t, half))
                    for c in range(4):
                        mm = pe.transpose(bank[b][:, c * P:(c + 1) * P],
                                          work[:, row, (4 * half + c) * P:(4 * half + c + 1) * P], ident[:, :])
                    mm.then_inc(bank_full[b], 1)

            def tokens_times_weights(keys, out_key, lhs_hi, lhs_lo, cols, chunks, halves=1):
                per = slabs[number[keys[0]]][1][0][0]
                for s, key in enumerate(keys):
                    slab_ready(key)
                    for t in range(NT):
                        for n in range(halves):
                            okey = out_key(t, n)
                            b = claim(okey) if s == 0 else use[okey][0]
                            for k in range(per):
                                c = chunks[s * per + k]
                                ts = slice(t * P, (t + 1) * P)
                                wh, wl = split_of(key, k, n * cols, (n + 1) * cols)
                                mm = product(bank[b][:, 0:cols], lhs_hi[:, c, ts], lhs_lo[:, c, ts], wh, wl,
                                             s == 0 and k == 0, s == len(keys) - 1 and k == per - 1)
                            last = t == NT - 1 and n == halves - 1
                            if s == len(keys) - 1:
                                mm.then_inc(bank_full[b], 1)
                            elif last:
                                mm.then_inc(w_used, 1)

            def in_projection(name, cols):
                tokens_times_weights([(name, k) for k in range(0, KD, 2)], lambda t, n: (name, t), xt_hi, xt_lo,
                                     cols, list(range(KD)))

            pe.wait_ge(consts_made, 4)
            for t in range(NT):
                pe.wait_ge(xn_ready, XN_X + t + 1)
                transpose_rows("xT", t, t % 2)
            for t in range(NT):
                ready(("xT", t, 0))
                ready(("xT", t, 1))
            in_projection("cq", Q_LORA)
            in_projection("ckv", KV_LORA + ROPE + NH)
            in_projection("vf", HALF)
            b = claim(("cum",))
            pe.wait_ge(logf_ready, 1)
            for t in range(NT):
                for u in range(t + 1):
                    mm = pe.matmul(bank[b][:, t * NH:(t + 1) * NH], upto[:, :] if u == t else ones[:, :],
                                   logf[:, u, :], start=(u == 0), stop=(u == t), skip_group_check=True)
            mm.then_inc(bank_full[b], 1)
            in_projection("qf", HALF)
            in_projection("kf", HALF)
            for c in range(CQ + CKV):
                if c == 0:
                    for t in range(NT):
                        ready(("cq", t))
                        ready(("ckv", t))
                b = claim(("cT", c))
                for t in range(NT):
                    mm = pe.transpose(bank[b][:, t * P:(t + 1) * P], cn[:, t, c * P:(c + 1) * P], ident[:, :])
                mm.then_inc(bank_full[b], 1)

            def attention(first, last, v_hi, v_lo):
                def qk_transposes(g):
                    h = g % NH
                    for name, src in (("QT", nat_q), ("KT", nat_k)):
                        b = claim((name, g))
                        for t in range(NT):
                            mm = pe.transpose(bank[b][0:QK, t * P:(t + 1) * P], src[:, t, h, :], ident[:, :])
                        mm.then_inc(bank_full[b], 1)

                def scores(g, i):
                    b = claim(("S", g, i))
                    if i == 3:
                        ready(("QT", g))
                        ready(("KT", g))
                    w = P * (i + 1)
                    q, k = slice(i * P, w), slice(0, w)
                    product(bank[b][:, 0:w], qt_hi[0:QK, g % 2, q], qt_lo[0:QK, g % 2, q], kt_hi[0:QK, g % 2, k],
                            kt_lo[0:QK, g % 2, k], True, False)
                    pe.matmul(bank[b][:, i * P:w], ident_bf[:, :], mask_bf[:, :], start=False, stop=True,
                              skip_group_check=True).then_inc(bank_full[b], 1)

                def probs_transposes(g, part):
                    if part == 0:
                        pe.wait_ge(probs_ready, 4 * (g + 1))
                    b = claim(("PT", g, part))
                    blocks = (((0, 0), (1, 0), (2, 0), (3, 0)), ((1, 1), (2, 1), (3, 1), (3, 3)),
                              ((2, 2), (3, 2)))[part]
                    for n, (i, j) in enumerate(blocks):
                        s = (g % 2) * P_COLS + P_OFF[i] + j * P
                        mm = pe.transpose(bank[b][:, n * P:(n + 1) * P], resid_flat[:, s:s + P], ident[:, :])
                    mm.then_inc(bank_full[b], 1)

                def values(g):
                    b = claim(("PV", g))
                    c = (g % NH) // 2
                    for part in range(3):
                        ready(("PT", g, part))
                    for j, s in enumerate((0, 512, 1024, 896)):
                        w = SEQ - P * j
                        vs = slice(c * P, (c + 1) * P)
                        mm = product(bank[b][:, P * j:SEQ], v_hi[:, j, vs], v_lo[:, j, vs],
                                     pt_hi[:, g % 2, s:s + w], pt_lo[:, g % 2, s:s + w], j == 0, j == NT - 1)
                    mm.then_inc(bank_full[b], 1)

                qk_transposes(first)
                for g in list(range(first, last + 1)) + [None]:
                    prev = last if g is None else (g - 1 if g > first else None)
                    for i in (3, 2, 1, 0):
                        if g is not None:
                            scores(g, i)
                        if prev is not None and i < 3:
                            probs_transposes(prev, 2 - i)
                    if g is not None and g < last:
                        qk_transposes(g + 1)
                    if prev is not None:
                        values(prev)

            def sum_squares(fam):
                b = claim(("ssq", fam))
                pe.wait_ge(sq_added, 4 * (fam + 1))
                for t in range(NT):
                    mm = pe.matmul(bank[b][:, t:t + 1], sq_acc[:, fam, t * P:(t + 1) * P], ones[:, 0:1],
                                   start=True, stop=True)
                mm.then_inc(bank_full[b], 1)

            for t in range(NT):
                ready(("qf", t))
                ready(("kf", t))
                ready(("vf", t))
            ready(("cum",))
            pe.wait_ge(krope_nat, 1)
            attention(0, NH - 1, vf_hi, vf_lo)
            sum_squares(0)
            for c in range(CQ + CKV):
                ready(("cT", c))
            tokens_times_weights([("uq", k) for k in range(CQ)], lambda t, n: ("uq", t, n), ct_hi, ct_lo, 384,
                                 [0, 1, 2], 2)
            tokens_times_weights([("ukv", k) for k in range(CKV)], lambda t, n: ("ukv", t, n), ct_hi, ct_lo, 512,
                                 [3, 4], 2)
            for t in range(NT):
                for n in range(2):
                    ready(("uq", t, n))
                    ready(("ukv", t, n))
            pe.wait_ge(krope_nat, 2)
            attention(NH, 2 * NH - 1, vm_hi, vm_lo)
            sum_squares(1)
            for stage in range(4):
                fam = stage // 2
                oh, ol = ((of_hi, of_lo), (om_hi, om_lo))[fam]
                ready(("PV", NH * (fam + 1) - 1))
                tokens_times_weights([("out", stage, k) for k in ((4, 6) if stage < 2 else (0, 2))],
                                     lambda t, n: ("out", stage, t), oh, ol, HALF, [0, 1, 2, 3])
            for m in range(NM):
                pe.wait_ge(xn_ready, XN_MEM + m + 1)
                transpose_rows("memT", m, m)
            for m in range(NM):
                ready(("memT", m, 0))
                ready(("memT", m, 1))
            for h in range(H_MEM):
                slab_ready(("mk", h))
                b = claim(("mk", h))
                for k in range(KD):
                    wh, wl = split_of(("mk", h), k, 0, P)
                    mm = product(bank[b][:, 0:MEM], wh, wl, mt_hi[:, k, :], mt_lo[:, k, :], k == 0, k == KD - 1)
                mm.then_inc(bank_full[b], 1)
            for k in range(0, KD, 2):
                slab_ready(("mv", k))
                for m in range(NM):
                    b = claim(("mv", m)) if k == 0 else use[("mv", m)][0]
                    ms = slice(m * P, (m + 1) * P)
                    for kk in range(2):
                        n = number[("mv", k)] % SPLIT
                        ws = slice(kk * HALF, (kk + 1) * HALF)
                        mm = product(bank[b][:, :], mt_hi[:, k + kk, ms], mt_lo[:, k + kk, ms], w_hi[:, n, ws],
                                     w_lo[:, n, ws], k + kk == 0, k + kk == KD - 1)
                    if k == KD - 2:
                        mm.then_inc(bank_full[b], 1)
                if k < KD - 2:
                    mm.then_inc(w_used, 1)
            for t in range(NT):
                pe.wait_ge(xn_ready, XN_H1 + t + 1)
                transpose_rows("h1T", t, t % 2)

            def weights_times_tokens(key, out_key):
                slab_ready(key)
                b = claim(out_key)
                for k in range(KD):
                    wh, wl = split_of(key, k, 0, P)
                    mm = product(bank[b][:, :], wh, wl, xt_hi[:, k, :], xt_lo[:, k, :], k == 0, k == KD - 1)
                mm.then_inc(bank_full[b], 1)

            for t in range(NT):
                ready(("h1T", t, 0))
                ready(("h1T", t, 1))
            for h in range(H_MEM):
                weights_times_tokens(("mq", h), ("mq", h))
            for h in range(H_MEM):
                ready(("mk", h))
            for m in range(NM):
                ready(("mv", m))
            for s in range(H_MEM + 1):
                if s < H_MEM:
                    ready(("mq", s))
                    for u in range(2):
                        b = claim(("MS", s, u))
                        for i in range(2):
                            q = slice((2 * u + i) * P, (2 * u + i + 1) * P)
                            mm = product(bank[b][:, i * MEM:(i + 1) * MEM], mq_hi[:, s, q], mq_lo[:, s, q],
                                         mk_hi[:, s, :], mk_lo[:, s, :], True, True)
                        mm.then_inc(bank_full[b], 1)
                if s > 0:
                    h = s - 1
                    pe.wait_ge(inv_ready, 64 + 4 * (h + 1))
                    for j in range(NM):
                        b = claim(("MPT", h, j))
                        for t in range(NT):
                            c0 = (h % 2) * D + t * MEM + j * P
                            mm = pe.transpose(bank[b][:, t * P:(t + 1) * P], work_flat[:, c0:c0 + P], ident[:, :])
                        mm.then_inc(bank_full[b], 1)
                    b = claim(("MPV", h))
                    for j in range(NM):
                        ready(("MPT", h, j))
                        hs = slice(h * P, (h + 1) * P)
                        mm = product(bank[b][:, :], mv_hi[:, j, hs], mv_lo[:, j, hs], mp_hi[:, 2 * (h % 2) + j, :],
                                     mp_lo[:, 2 * (h % 2) + j, :], j == 0, j == NM - 1)
                    mm.then_inc(bank_full[b], 1)
            ready(("MPV", H_MEM - 1))
            for n in range(2):
                tokens_times_weights([("mo", n, k) for k in range(0, H_MEM, 2)], lambda t, _: ("mo", n, t), mo_hi,
                                     mo_lo, HALF, [0, 1, 2, 3])
            for t in range(NT):
                pe.wait_ge(xn_ready, XN_H2 + t + 1)
                transpose_rows("h2T", t, t % 2)
            for t in range(NT):
                ready(("h2T", t, 0))
                ready(("h2T", t, 1))

            def claim_gate(f):
                if f >= 4:
                    pe.wait_ge(silu_done, f - 3)
                    pe.wait_ge(h_done, f - 3)

            for f in range(NF):
                claim_gate(f)
                for name in ("gate", "up"):
                    slab_ready((name, f))
                    b = use[(name, f)][0]
                    if f < 4:
                        claim((name, f))
                    for k in range(KD):
                        wh, wl = split_of((name, f), k, 0, P)
                        mm = product(bank[b][:, :], wh, wl, xt_hi[:, k, :], xt_lo[:, k, :], k == 0, k == KD - 1)
                    mm.then_inc(bank_full[b], 1)
            pe.wait_ge(silu_done, NF)
            pe.wait_ge(h_done, NF)
            for k in range(NF):
                slab_ready(("down", k))
                pe.wait_ge(h_lo_done, k + 1)
                for t in range(NT):
                    ts = slice(t * P, (t + 1) * P)
                    for n in range(2):
                        b = use[("down", t, n)][0]
                        wh, wl = split_of(("down", k), 0, n * HALF, (n + 1) * HALF)
                        mm = product(bank[b][:, :], ht_hi[:, k, ts], ht_lo[:, k, ts], wh, wl, k == 0, k == NF - 1)
                        if k == NF - 1:
                            mm.then_inc(bank_full[b], 1)
                if k < NF - 1:
                    mm.then_inc(w_used, 1)


_INS = ["x", "mem", "mix_norm_g", "w_in", "cq_norm_g", "ckv_norm_g", "w_uq", "w_ukv", "forget_bias", "mla_out_g",
        "fox_out_g", "w_out", "mem_q_norm_g", "mem_kv_norm_g", "w_mq", "w_mkv", "w_mo", "ffn_norm_g", "w_gate",
        "w_up", "w_down", "final_norm_g"]


def rope_tables():
    inv = (1.0 / (np.float32(10000.0) ** (np.arange(0, ROPE, 2, dtype=np.float32) / np.float32(ROPE)))).astype(np.float32)
    ang = np.arange(SEQ, dtype=np.float32)[:, None] * inv[None, :]
    cos, sin = np.cos(ang).astype(np.float32), np.sin(ang).astype(np.float32)
    both = [np.concatenate([m, m], axis=1) for m in (cos, sin)]
    s = np.float32(-MLA_SCALE)
    return np.stack([both[0] * s, both[1] * s, both[0], both[1]]).astype(np.float32)


def kernel(**inputs):
    import numpy as _np
    import concourse.bacc as _bacc
    from concourse import mybir as _mybir
    from concourse.bass_utils import run_bass_kernel_spmd as _run

    nc = _bacc.Bacc("TRN2", target_bir_lowering=False, num_devices=1)
    arrays, aps = {}, {}
    for name in _INS + ["rope"]:
        v = _np.ascontiguousarray(inputs[name]) if name != "rope" else rope_tables()
        arrays[f"in_{name}_dram"] = v
        aps[name] = nc.dram_tensor(f"in_{name}_dram", v.shape, _mybir.dt.from_np(v.dtype), kind="ExternalInput").ap()
    out = nc.dram_tensor("out_0_dram", (1, SEQ, D), _mybir.dt.float32, kind="ExternalOutput").ap()
    build(nc, aps, out)
    r = _run(nc, [arrays], core_ids=[0])
    return r.results[0]["out_0_dram"]
```

```python
from contextlib import ExitStack

import numpy as np
import concourse.bass as bass
from concourse import mybir

F32 = mybir.dt.float32
F32R = mybir.dt.float32r
BF16 = mybir.dt.bfloat16
ALU = mybir.AluOpType
ACT = mybir.ActivationFunctionType
AX = mybir.AxisListType

P = 128
D = 1024
SEQ = 512
MEM = 256
NT = SEQ // P
NM = MEM // P
KD = D // P
NH = 8
HD = 64
ROPE = 32
QK = HD + ROPE
Q_LORA = 384
KV_LORA = 256
CQ, CKV = Q_LORA // P, KV_LORA // P
H_MEM = 4
MEM_HD = 128
D_FF = 2816
NF = D_FF // P
HALF = 512
EPS = 1e-6
SLOT = 1024
TILE_ORDER = (3, 2, 0, 1)
RAW = 3
SPLIT = 2
MLA_SCALE = float(QK) ** -0.5
FOX_SCALE = float(HD) ** -0.5
MEM_SCALE = float(MEM_HD) ** -0.5
MASKED = 1e30
P_OFF = [0, 128, 384, 768]
P_COLS = 1280
NC_LAT = CQ + CKV
RF = ROPE + NH
FOX_SLOTS = ((-4, -3, -2, -1), (0, 2, 3, 5), (7, 8, 10, 11), (13, 14, 16, 17))
MLA_SLOTS = ((1, 2, 4, 5), (7, 8, 10, 11), (14, 16, 17, 20))
SLOTS = 3


def fitted(fam):
    if fam == 0:
        slots = {("cT", c): FOX_SLOTS[c] for c in range(NC_LAT - 1)}
    else:
        slots = {("mk", h): MLA_SLOTS[h] for h in range(H_MEM - 1)}
    plan = {slot: (name, q) for name, places in slots.items() for q, slot in enumerate(places)}
    return plan

C_CQ, C_CKV, C_ROPE, C_QF, C_KF, C_VF, C_F = 0, 384, 640, 672, 1184, 1696, 2208


MEM_STEPS = ([("mq", 0), ("mq", 1), ("MS", 0), ("mq", 2), ("MPT", 0), ("MS", 1), ("mq", 3), ("MPV", 0), ("MPT", 1),
              ("MS", 2), ("MPV", 1), ("mo", 0, 0, 0), ("mo", 0, 0, 1), ("MPT", 2), ("MS", 3), ("MPV", 2),
              ("mo", 0, 0, 2), ("mo", 0, 0, 3), ("MPT", 3), ("MPV", 3)]
             + [("mo", 0, 2, t) for t in range(NT)] + [("mo", 1, k, t) for t in range(NT) for k in (0, 2)])


OUT_BANKS = [(4, 7, 0, 1), (2, 3, 5, 6)] * 2


UQ_BANKS = (0, 1, 4, 7, 2, 3, 5, 6)


class Banks:

    def __init__(self):
        self.turns = [0] * 8
        self.hi_turns = [0] * 8
        self.use = {}

    def add(self, key, bank, split=False):
        self.turns[bank] += 1
        if split:
            self.hi_turns[bank] += 1
        self.use[key] = (bank, self.turns[bank], self.hi_turns[bank])


def plan_banks():
    bk = Banks()
    for t in range(NT):
        for half in range(2):
            bk.add(("xT", t, half), 2 * t + half, True)
    for t in range(NT):
        bk.add(("vf", t), t, True)
    bk.add(("rf",), 4)
    for t in range(NT):
        bk.add(("qf", t), 4 + t)
    bk.add(("rft",), 0)
    bk.add(("cum",), 0)
    for t in range(NT):
        bk.add(("kf", t), t)

    s_turn = [0]

    def attention(heads):
        first, last = heads[0], heads[-1]
        plan = fitted(first // NH)

        def scores(g, i):
            bk.add(("S", g, i), s_turn[0] % 2)
            if i == 2:
                bk.use[("S", g, 0)] = bk.use[("S", g, 2)]
            s_turn[0] += 1

        def transposed(g, part):
            bk.add(("PT", g, part), (2, 3, 5)[part], True)

        def qkt(g):
            bk.add(("QT", g), 4, True)
            bk.add(("KT", g), 5, True)

        def fit(g, slot):
            name, quarter = plan.get((g - first) * SLOTS + slot, (None, 0))
            if name and quarter == 0:
                bk.add(name, 7, True)

        fit(first, -4)
        fit(first, -3)
        qkt(first)
        fit(first, -2)
        fit(first, -1)
        if first:
            for m in range(NM):
                for half in range(2):
                    bk.add(("memT", m, half), ((7, 6), (2, 3))[m][half], True)
        for g in heads:
            scores(g, 3)
            scores(g, 2)
            if g == NH:
                bk.add(("ssq", 0), 6)
            fit(g, 0)
            if g < last:
                qkt(g + 1)
            if g > first + 1:
                bk.add(("PV", g - 2), 6, True)
            if g > first:
                transposed(g - 1, 0)
            scores(g, 1)
            fit(g, 1)
            if g > first:
                transposed(g - 1, 1)
                transposed(g - 1, 2)
            fit(g, 2)
        bk.add(("cT", NC_LAT - 1) if first == 0 else ("mk", H_MEM - 1), 7, True)
        bk.add(("PV", last - 1), 6, True)
        for t in range(NT if first else 0):
            bk.add(("out", 0, t), OUT_BANKS[0][t])
        for part in range(3):
            transposed(last, part)
        bk.add(("PV", last), 6, True)

    attention(list(range(NH)))
    bk.add(("cssq",), 6)
    for t in range(NT):
        for n in range(2):
            bk.add(("uq", t, n), UQ_BANKS[2 * t + n])
    for t in range(NT):
        for n in range(2):
            bk.add(("ukv", t, n), 2 * t + n, True)
    attention(list(range(NH, 2 * NH)))
    for stage in range(1, 4):
        if stage == 2:
            bk.add(("ssq", 1), 4)
        for t in range(NT):
            bk.add(("out", stage, t), OUT_BANKS[stage][t])
    for m in range(NM):
        bk.add(("mv", m), m, True)
    for t in range(NT):
        for half in range(2):
            bk.add(("h1T", t, half), (2 * t + half + 2) % 8, True)
    for step in MEM_STEPS:
        if step[0] == "mq":
            bk.add(step, 4 + step[1], True)
        elif step[0] == "MS":
            for u in range(2):
                bk.add(("MS", step[1], u), u)
        elif step[0] == "MPT":
            for j in range(NM):
                bk.add(("MPT", step[1], j), 2 + j, True)
        elif step[0] == "MPV":
            bk.add(step, 2, True)
        elif step[0] == "mo" and step[2] == 0:
            bk.add(("mo", step[1], step[3]), 4 * (1 - step[1]) + step[3])
    for t in range(NT):
        for half in range(2):
            bk.add(("h2T", t, half), (2 * t + half) % 8, True)
    for f in range(NF):
        bk.add(("gate", f), 2 * (f % 4))
        bk.add(("up", f), 2 * (f % 4) + 1)
    for t in range(NT):
        for n in range(2):
            bk.add(("down", t, n), 2 * t + n)
    return bk.use


def build(nc, a, out):
    use = plan_banks()

    with ExitStack() as ctx:
        def sb(name, shape, dt=F32):
            return ctx.enter_context(nc.sbuf_tensor(name, shape, dt))

        def sem(name):
            return ctx.enter_context(nc.semaphore(name))

        w_raw = sb("w_raw", [P, RAW, SLOT])
        w_hi = sb("w_hi", [P, SPLIT, SLOT], F32R)
        w_lo = sb("w_lo", [P, SPLIT, SLOT], F32R)
        xt_hi = sb("xt_hi", [P, KD, SEQ], F32R)
        xt_lo = sb("xt_lo", [P, KD, SEQ], F32R)
        resid = sb("resid", [P, NT, D])
        work = sb("work", [P, 2, D])
        nat = sb("nat", [P, 2 * NT * NH * QK])
        arena = sb("arena", [P, NF * 2 * HALF], F32R)
        ident = sb("ident", [P, P])
        ident_bf = sb("ident_bf", [P, P], BF16)
        mask_bf = sb("mask_bf", [P, P], BF16)
        upto = sb("upto", [P, P])
        ones = sb("ones", [P, P])
        rope_tab = sb("rope_tab", [P, 2, NT, ROPE])
        rope_a = sb("rope_a", [P, NT, ROPE])
        rope_b = sb("rope_b", [P, NT, ROPE])
        krf = sb("krf", [P, NT, ROPE + NH])
        kro = sb("kro", [P, NT, ROPE])
        fbias = sb("fbias", [P, NH])
        fz = sb("fz", [P, NT, NH])
        fa = sb("fa", [P, NT, NH])
        fe = sb("fe", [P, NT, NH])
        fl = sb("fl", [P, NT, NH])
        logf = sb("logf", [P, NT, NH])
        g_out = sb("g_out", [P, NH])
        g_lat = sb("g_lat", [P, NC_LAT])
        q_scale = sb("q_scale", [P, NT])
        NNORM = 4 + 4 + 4 + 8 + 2 + 4 + 4 + 4
        ssq = sb("ssq", [P, NNORM])
        msq = sb("msq", [P, NNORM])
        rstd = sb("rstd", [P, NNORM])
        neg_half = sb("neg_half", [P, 4])
        neg_max = sb("neg_max", [P, 2 * NH, NT])
        row_sum = sb("row_sum", [P, 2 * NH, NT])
        row_inv = sb("row_inv", [P, 2 * NH, NT])

        resid_flat = resid[:, :, :].rearrange("p t n -> p (t n)")
        work_flat = work[:, :, :].rearrange("p t n -> p (t n)")
        nat_q = nat[:, 0:NT * NH * QK].rearrange("p (t h c) -> p t h c", t=NT, h=NH)
        nat_k = nat[:, NT * NH * QK:].rearrange("p (t h c) -> p t h c", t=NT, h=NH)
        g_mix = nat[:, 0:D]
        x_rows = [work[:, 0, :], work[:, 1, :], nat[:, D:2 * D], nat[:, 2 * D:3 * D]]
        lat_acc = resid_flat[:, 2560:3584].rearrange("p (f n) -> p f n", f=2)
        lat_tmp = resid_flat[:, 3584:4096]
        g_memkv = resid_flat[:, 2560:3584]
        mem_rows = [resid_flat[:, m * P_COLS:m * P_COLS + D] for m in range(NM)]
        q_cos, q_sin = (work_flat[:, D + i * HALF:D + (i + 1) * HALF].rearrange(
            "p (t h c) -> p t h c", t=2, h=NH) for i in range(2))
        rf_t = resid_flat[0:RF, 0:SEQ]
        sq_acc = work_flat[:, 0:HALF]
        sq_tmp = work_flat[:, 2 * HALF:4 * HALF].rearrange("p (f n) -> p f n", f=2)
        h_rows = [work[:, 0, :], work[:, 1, :], nat[:, 0:D], nat[:, D:2 * D]]
        g_memq, g_ffn, g_final = (nat[:, 2048 + i * D:3072 + i * D] for i in range(3))
        silu_buf = nat[:, 0:2 * HALF].rearrange("p (s n) -> p s n", s=2)
        h_buf = nat[:, 2 * HALF:4 * HALF].rearrange("p (s n) -> p s n", s=2)

        def region(start, *dims):
            n = int(np.prod(dims))
            ap = arena[:, start:start + n]
            if len(dims) == 2:
                ap = ap.rearrange("p (a b) -> p a b", a=dims[0])
            return ap

        qt_hi, qt_lo, kt_hi, kt_lo = (region(i * 1024, 2, HALF) for i in range(4))
        pt_hi, pt_lo = region(4096, 2, P_COLS), region(6656, 2, P_COLS)
        ct_hi, ct_lo = region(9216, NC_LAT, HALF), region(11776, NC_LAT, HALF)
        vm_hi, vm_lo = xt_hi[:, 0:4, :], xt_lo[:, 0:4, :]
        vf_hi, vf_lo = region(14336, NT, HALF), region(16384, NT, HALF)
        of_hi, of_lo = region(18432, NT, HALF), region(20480, NT, HALF)
        om_hi, om_lo = vf_hi, vf_lo
        mt_hi, mt_lo = (x[:, 4:8, :].rearrange("p a (b n) -> p (a b) n", b=2) for x in (xt_hi, xt_lo))
        mem_junk = [region(6656 + m * D, 1, D)[:, 0, :] for m in range(NM)]
        mk_hi, mk_lo = region(9216, H_MEM, MEM), region(10240, H_MEM, MEM)
        mv_hi, mv_lo = region(11264, NM, HALF), region(12288, NM, HALF)
        mq_hi, mq_lo = region(0, H_MEM, HALF), region(2048, H_MEM, HALF)
        mp_hi, mp_lo = region(18432, 4, HALF), region(20480, 4, HALF)
        mo_hi, mo_lo = region(14336, H_MEM, HALF), region(16384, H_MEM, HALF)
        ht_hi, ht_lo = region(0, NF, HALF), region(NF * HALF, NF, HALF)

        bank = [ctx.enter_context(nc.psum_tensor(f"bank{i}", [P, HALF], F32)) for i in range(8)]

        bank_full = [sem(f"bank_full{i}") for i in range(8)]
        bank_hi = [sem(f"bank_hi{i}") for i in range(8)]
        bank_free = [sem(f"bank_free{i}") for i in range(8)]
        x_loaded = [sem(f"x_loaded{t}") for t in range(NT)]
        x_again = sem("x_again")
        consts_loaded = sem("consts_loaded")
        g_mix_loaded = sem("g_mix_loaded")
        mem_loaded = [sem(f"mem_loaded{m}") for m in range(NM)]
        g_memkv_loaded = sem("g_memkv_loaded")
        late_loaded = sem("late_loaded")
        w_loaded = [sem(f"w_loaded{i}") for i in range(RAW)]
        w_hi_done = sem("w_hi_done")
        w_lo_done = sem("w_lo_done")
        w_used = sem("w_used")
        consts_made = sem("consts_made")
        nat_cleared = sem("nat_cleared")
        ssq_ready = sem("ssq_ready")
        rstd_ready = sem("rstd_ready")
        xn_ready = sem("xn_ready")
        forget_z = sem("forget_z")
        forget_l = sem("forget_l")
        logf_ready = sem("logf_ready")
        krope_nat = sem("krope_nat")
        max_ready = sem("max_ready")
        exp_done = sem("exp_done")
        inv_ready = sem("inv_ready")
        probs_ready = sem("probs_ready")
        sq_ready = sem("sq_ready")
        sq_added = sem("sq_added")
        lat_sq_ready = sem("lat_sq_ready")
        lat_sq_added = sem("lat_sq_added")
        q_scale_ready = sem("q_scale_ready")
        k_nat = sem("k_nat")
        qrope_nat = sem("qrope_nat")
        resid_done = sem("resid_done")
        silu_done = sem("silu_done")
        h_done = sem("h_done")
        h_hi_done = sem("h_hi_done")
        h_lo_done = sem("h_lo_done")
        stored = sem("stored")
        act_chain = sem("act_chain")
        dve_chain = sem("dve_chain")
        pool_chain = sem("pool_chain")

        def rows(w):
            return w.rearrange("(k p) n -> p k n", p=P)

        slabs = []

        def slab(key, *pieces):
            slabs.append((key, pieces))

        w_in = rows(a["w_in"][0])
        for name, c in (("vf", C_VF), ("rf", C_ROPE), ("qf", C_QF), ("kf", C_KF)):
            if name == "rf":
                slab(("rf", 0), (KD, RF, 0, ROPE, w_in[:, :, C_ROPE:C_ROPE + ROPE]),
                     (KD, RF, ROPE, RF, w_in[:, :, C_F:C_F + NH]))
                continue
            for k in range(0, KD, 2):
                slab((name, k), (2, 512, 0, 512, w_in[:, k:k + 2, c:c + 512]))
        for c in range(NC_LAT):
            slab(("cT", c), (KD, 128, 0, 128, w_in[:, :, C_CQ + c * P:C_CQ + (c + 1) * P]))
        for k in range(CQ):
            slab(("uq", k), (1, 768, 0, 768, rows(a["w_uq"][0])[:, k:k + 1, :]))
        for k in range(CKV):
            slab(("ukv", k), (1, 1024, 0, 1024, rows(a["w_ukv"][0])[:, k:k + 1, :]))
        w_mkv = a["w_mkv"][0].rearrange("(k p) (h s n) -> p k h s n", p=P, h=H_MEM, s=2)
        for h in range(H_MEM):
            slab(("mk", h), (KD, 128, 0, 128, w_mkv[:, :, h, 0, :]))
        w_o = rows(a["w_out"][0])
        for stage in range(4):
            k0, n0 = (4 if stage < 2 else 0), HALF * (stage % 2)
            for k in range(k0, k0 + 4, 2):
                slab(("out", stage, k), (2, 512, 0, 512, w_o[:, k:k + 2, n0:n0 + HALF]))
        for k in range(0, KD, 2):
            slab(("mv", k), *[(8, 128, 0, 128, (kk, w_mkv[:, k + kk, :, 1, :])) for kk in (0, 1)])
        for h in range(H_MEM):
            slab(("mq", h), (KD, 128, 0, 128, rows(a["w_mq"][0])[:, :, h * P:(h + 1) * P]))
        for n in range(2):
            for k in range(0, H_MEM, 2):
                slab(("mo", n, k), (2, 512, 0, 512, rows(a["w_mo"][0])[:, k:k + 2, n * HALF:(n + 1) * HALF]))
        for f in range(NF):
            for name in ("gate", "up"):
                slab((name, f), (KD, 128, 0, 128, rows(a[f"w_{name}"][0])[:, :, f * P:(f + 1) * P]))
        for k in range(NF):
            slab(("down", k), (1, 1024, 0, 1024, rows(a["w_down"][0])[:, k:k + 1, :]))
        NS = len(slabs)
        loads_upto, seen = [], [0] * RAW
        for n, (_, pieces) in enumerate(slabs):
            seen[n % RAW] += 16 * len(pieces)
            loads_upto.append(seen[n % RAW])
        number = {key: n for n, (key, _) in enumerate(slabs)}

        ends = {}
        for name in ("vf", "qf", "kf"):
            ends[(name, KD - 2)] = (name, NT - 1)
        ends[("rf", 0)] = ("rf",)
        for c in range(NC_LAT):
            ends[("cT", c)] = ("cT", c)
        ends[("uq", CQ - 1)], ends[("ukv", CKV - 1)] = ("uq", NT - 1, 1), ("ukv", NT - 1, 1)
        for stage in range(4):
            ends[("out", stage, 6 if stage < 2 else 2)] = ("out", stage, NT - 1)
        for h in range(H_MEM):
            ends[("mk", h)], ends[("mq", h)] = ("mk", h), ("mq", h)
        ends[("mv", KD - 2)] = ("mv", NM - 1)
        for n in range(2):
            ends[("mo", n, H_MEM - 2)] = ("mo", n, NT - 1)
        for f in range(NF):
            ends[("gate", f)], ends[("up", f)] = ("gate", f), ("up", f)
        ends[("down", NF - 1)] = ("down", NT - 1, 1)
        released, count = [], 0
        for key, _ in slabs:
            if key in ends:
                b, turn, _ = use[ends[key]]
                released.append((bank_full[b], turn))
            else:
                count += 1
                released.append((w_used, count))

        def slab_cols(n):
            return slabs[n][1][0][0] * slabs[n][1][0][1]

        def split_of(key, k, c0, c1):
            n = number[key]
            width = slabs[n][1][0][1]
            s = slice(k * width + c0, k * width + c1)
            return w_hi[:, n % SPLIT, s], w_lo[:, n % SPLIT, s]

        N_X, N_CQ, N_CKV, N_OUT, N_MEM, N_H1, N_H2, N_H3 = 0, 4, 8, 12, 20, 22, 26, 30

        def ssq_step(col):
            return col + 1 if col < N_CQ else col - 15

        def norm_step(col):
            if col < N_CQ:
                return col + 1
            steps = {N_CQ: 5, N_CKV: 6, N_MEM: 7, N_MEM + 1: 7, N_OUT: 8, N_OUT + 4: 9}
            return steps[col] if col in steps else col - 12

        XN_X, XN_MEM, XN_H1, XN_H2, XN_H3 = 0, 4, 6, 10, 14

        def score_col(i):
            return 3 * P if i == 0 else 0

        def squares_added(g):
            return 3 * (g // NH) + (g % NH) // 2

        block = ctx.enter_context(nc.Block())

        @block.sync
        def _(sp):
            def load_slab(n):
                key, pieces = slabs[n]
                slot = n % RAW
                if n >= RAW:
                    sp.wait_ge(w_lo_done, n - RAW + 1)
                for kk, width, c0, c1, src in pieces:
                    dst = w_raw[:, slot, 0:kk * width].rearrange("p (k n) -> p k n", k=kk)[:, :, c0:c1]
                    if isinstance(src, tuple):
                        dst = dst[:, 4 * src[0]:4 * src[0] + 4, :]
                        src = src[1]
                    sp.dma_start(dst, src).then_inc(w_loaded[slot], 16)

            for t in range(NT):
                sp.dma_start(resid[:, t, :], a["x"][0, t * P:(t + 1) * P, :]).then_inc(x_loaded[t], 16)
                if t == 0:
                    sp.dma_start(g_mix, a["mix_norm_g"].partition_broadcast(P)[:, 0, :]).then_inc(g_mix_loaded, 16)
            for n in range(RAW):
                load_slab(n)
            sp.dma_start(fbias[:, :], a["forget_bias"].partition_broadcast(P)[:, 0, :]).then_inc(consts_loaded, 16)
            sp.dma_start(rope_tab[:, :, :, :], a["rope"].rearrange("s (t p) c -> p s t c", p=P)).then_inc(consts_loaded, 16)
            sp.dma_start(g_out[:, 0:4], a["fox_out_g"][0].rearrange("(c p) -> p c", p=P),
                         allow_slow_non_contiguous=True).then_inc(consts_loaded, 16)
            sp.dma_start(g_out[:, 4:8], a["mla_out_g"][0].rearrange("(c p) -> p c", p=P),
                         allow_slow_non_contiguous=True).then_inc(consts_loaded, 16)
            for g, name, n in ((g_lat[:, 0:CQ], "cq_norm_g", CQ), (g_lat[:, CQ:], "ckv_norm_g", CKV)):
                sp.dma_start(g, a[name][0].rearrange("(c p) -> p c", p=P),
                             allow_slow_non_contiguous=True).then_inc(consts_loaded, 16)

            for n in range(RAW, number[("ukv", 0)]):
                load_slab(n)
            b, turn, _ = use[("PT", NH - 1, 2)]
            sp.wait_ge(bank_full[b], turn)
            for m in range(NM):
                sp.dma_start(mem_rows[m], a["mem"][0, m * P:(m + 1) * P, :]).then_inc(mem_loaded[m], 16)
            b, turn, _ = use[("cssq",)]
            sp.wait_ge(bank_full[b], turn)
            sp.dma_start(g_memkv, a["mem_kv_norm_g"].partition_broadcast(P)[:, 0, :]).then_inc(g_memkv_loaded, 16)
            first_late = number[("out", 0, 4)] + RAW
            for n in range(number[("ukv", 0)], first_late):
                load_slab(n)
            b, n_turn, _ = use[("KT", 2 * NH - 1)]
            sp.wait_ge(bank_full[b], n_turn)
            for g, name in ((g_memq, "mem_q_norm_g"), (g_ffn, "ffn_norm_g")):
                sp.dma_start(g, a[name].partition_broadcast(P)[:, 0, :]).then_inc(late_loaded, 16)
            sp.dma_start(g_final, a["final_norm_g"].partition_broadcast(P)).then_inc(late_loaded, 16)
            b, n_turn, _ = use[("PT", 2 * NH - 1, 2)]
            sp.wait_ge(bank_full[b], n_turn)
            sp.dma_start(resid[:, :, :], a["x"][0].rearrange("(t p) n -> p t n", p=P)).then_inc(x_again, 16)
            for n in range(first_late, NS):
                load_slab(n)
            for t in range(NT):
                sp.wait_ge(xn_ready, XN_H3 + t + 1)
                sp.dma_start(out[0, t * P:(t + 1) * P, :], h_rows[t]).then_inc(stored, 16)
            sp.wait_ge(stored, 16 * NT)

        @block.gpsimd
        def _(pool):
            pool.memset(neg_half[:, :], -0.5).then_inc(pool_chain, 1)
            pool.memset(ones[:, :], 1.0).then_inc(pool_chain, 1)
            pool.memset(ident[:, :], 0.0).then_inc(pool_chain, 1)
            pool.memset(ident_bf[:, :], 0.0).then_inc(pool_chain, 1)
            pool.memset(mask_bf[:, :], 0.0).then_inc(pool_chain, 1)
            pool.wait_ge(pool_chain, 5)
            for m in (ident, ident_bf):
                pool.affine_select(out=m[:, :], in_=m[:, :], compare_op=ALU.not_equal, fill=1.0, base=0,
                                   pattern=[[-1, P]], channel_multiplier=1).then_inc(consts_made, 1)
            pool.affine_select(out=mask_bf[:, :], in_=mask_bf[:, :], compare_op=ALU.is_ge, fill=MASKED, base=0,
                               pattern=[[-1, P]], channel_multiplier=1).then_inc(consts_made, 1)
            pool.affine_select(out=upto[:, :], in_=ones[:, :], compare_op=ALU.is_ge, fill=0.0, base=0,
                               pattern=[[1, P]], channel_multiplier=-1).then_inc(consts_made, 1)
            chain = [5]

            def link(ins):
                chain[0] += 1
                ins.then_inc(pool_chain, 1)
                pool.wait_ge(pool_chain, chain[0])

            def make_rstd(col, width, dim):
                if N_CQ <= col < N_MEM:
                    b, n, _ = use[("cssq",) if col < N_OUT else ("ssq", (col - N_OUT) // 4)]
                    pool.wait_ge(bank_free[b], n)
                else:
                    pool.wait_ge(ssq_ready, ssq_step(col + width - 1))
                c = slice(col, col + width)
                link(pool.tensor_scalar(msq[:, c], ssq[:, c], 1.0 / dim, EPS, ALU.mult, ALU.add))
                pool.tensor_tensor(rstd[:, c], msq[:, c], neg_half[:, 0:width], ALU.pow).then_inc(rstd_ready, 1)

            for t in range(NT):
                make_rstd(N_X + t, 1, D)
            pool.wait_ge(xn_ready, XN_X + NT)
            for t in range(2, NT):
                b, turn, _ = use[("xT", t, 1)]
                pool.wait_ge(bank_full[b], turn)
            link(pool.memset(nat[:, :], 0.0))
            pool.memset(nat_q[:, :, :, HD + 1:HD + 2], 1.0).then_inc(nat_cleared, 1)
            pool.memset(nat_k[:, :, :, HD:HD + 1], 1.0).then_inc(nat_cleared, 1)
            def normalise(g, i):
                pool.wait_ge(inv_ready, 3 * g + {3: 1, 2: 2, 0: 2, 1: 3}[i])
                s = (g % 2) * P_COLS + P_OFF[i]
                p = resid_flat[:, s:s + P * (i + 1)]
                pool.tensor_scalar(p, p, row_inv[:, g, i:i + 1], None, ALU.mult).then_inc(probs_ready, 1)

            def add_squares(g):
                pair = (g % NH) // 2
                if g % 2 == 0 or pair == 0:
                    return
                pool.wait_ge(sq_ready, g + 1)
                n = squares_added(g)
                if n > 1:
                    pool.wait_ge(sq_added, n - 1)
                pool.tensor_tensor(sq_acc, sq_acc, sq_tmp[:, pair % 2, :], ALU.add).then_inc(sq_added, 1)

            def add_latent_squares(c):
                if c in (0, CQ):
                    return
                pool.wait_ge(lat_sq_ready, c + 1)
                if c > 1:
                    pool.wait_ge(lat_sq_added, 1)
                if c > CQ:
                    pool.wait_ge(lat_sq_added, 2)
                acc = lat_acc[:, 0 if c < CQ else 1, :]
                pool.tensor_tensor(acc, acc, lat_tmp, ALU.add).then_inc(lat_sq_added, 1)

            for fam in range(2):
                plan = fitted(fam)
                for g in range(fam * NH, (fam + 1) * NH):
                    for i in TILE_ORDER:
                        normalise(g, i)
                    if g == NH:
                        make_rstd(N_OUT, 4, HALF)
                    if g > fam * NH + 1:
                        add_squares(g - 2)
                    for slot in range(SLOTS):
                        name, quarter = plan.get((g % NH) * SLOTS + slot, (None, 0))
                        if fam == 0 and name and quarter == 3:
                            add_latent_squares(name[1])
                add_squares((fam + 1) * NH - 2)
                if fam == 0:
                    add_latent_squares(NC_LAT - 1)
                    make_rstd(N_CQ, 4, Q_LORA)
                    pool.wait_ge(rstd_ready, norm_step(N_CQ))
                    pool.tensor_scalar(q_scale[:, :], rstd[:, N_CQ:N_CQ + 4], -MLA_SCALE, None,
                                       ALU.mult).then_inc(q_scale_ready, 1)
                    make_rstd(N_CKV, 4, KV_LORA)
                add_squares((fam + 1) * NH - 1)
                if fam == 0:
                    make_rstd(N_MEM, NM, D)
                if fam == 1:
                    make_rstd(N_OUT + 4, 4, HALF)
            for base in (N_H1, N_H2, N_H3):
                for t in range(NT):
                    make_rstd(base + t, 1, D)

        @block.scalar
        def _(act):
            chain = [0]

            def full(key):
                b, n, _ = use[key]
                act.wait_ge(bank_full[b], n)
                return b

            def take_hi(key, dst, rows_=slice(0, P), cols=slice(0, HALF), scale=1.0, view=None):
                b = full(key)
                src = bank[b][rows_, cols]
                if view:
                    src = view(src)
                act.activation(dst, src, ACT.Copy, scale=scale).then_inc(bank_hi[b], 1)

            def summed(key):
                b, n, _ = use[key]
                act.wait_ge(bank_free[b], n)

            def split_slab(n):
                if n >= NS:
                    return
                cols = slab_cols(n)
                act.wait_ge(w_loaded[n % RAW], loads_upto[n])
                if n >= SPLIT:
                    act.wait_ge(*released[n - SPLIT])
                act.activation(w_hi[:, n % SPLIT, 0:cols], w_raw[:, n % RAW, 0:cols], ACT.Copy).then_inc(w_hi_done, 1)

            def square_rows(src, junk, col):
                act.activation(junk, src, ACT.Square, accum_out=ssq[:, col:col + 1]).then_inc(ssq_ready, 1)

            def take_transposed(name, t, hi):
                for half in range(2):
                    take_hi((name, t, half), hi[:, 4 * half:4 * half + 4, t * P:(t + 1) * P],
                            view=lambda s: s.rearrange("p (c n) -> p c n", c=4))

            def eat(key):
                if number[key] >= 1:
                    split_slab(number[key] + 1)

            for t in range(NT):
                act.wait_ge(x_loaded[t], 16)
                square_rows(resid[:, t, :], x_rows[t], N_X + t)
                if t == 1:
                    split_slab(0)
                if t == 2:
                    split_slab(1)
                if t >= 1:
                    take_transposed("xT", t - 1, xt_hi)
            take_transposed("xT", NT - 1, xt_hi)
            for k in range(0, KD, 2):
                eat(("vf", k))
            for t in range(NT):
                take_hi(("vf", t), vf_hi[:, t, :])
            eat(("rf", 0))
            b = full(("rf",))
            act.activation(rf_t, bank[b][0:RF, :], ACT.Copy).then_inc(bank_free[b], 1)
            eat(("qf", 0))
            b = full(("rft",))
            act.activation(krf[:, :, :], bank[b][:, 0:NT * RF].rearrange("p (t n) -> p t n", t=NT),
                           ACT.Copy).then_inc(bank_free[b], 1)
            act.wait_ge(forget_z, 1)
            act.activation(fe[:, :, :], fa[:, :, :], ACT.Exp, scale=-1.0).then_inc(act_chain, 1)
            act.wait_ge(act_chain, 1)
            act.activation(fl[:, :, :], fe[:, :, :], ACT.Ln, bias=1.0).then_inc(forget_l, 1)
            for k in range(2, KD, 2):
                eat(("qf", k))
            act.wait_ge(nat_cleared, 2)
            for t in range(NT):
                b = full(("qf", t))
                act.activation(nat_q[:, t, :, 0:HD], bank[b][:, :].rearrange("p (h c) -> p h c", h=NH), ACT.Copy,
                               scale=-FOX_SCALE).then_inc(bank_free[b], 1)
            for k in range(0, KD, 2):
                eat(("kf", k))
            for t in range(NT):
                b = full(("kf", t))
                act.activation(nat_k[:, t, :, 0:HD], bank[b][:, :].rearrange("p (h c) -> p h c", h=NH),
                               ACT.Copy).then_inc(bank_free[b], 1)

            def exp_scores(g, i):
                b, n, _ = use[("S", g, i)]
                act.wait_ge(max_ready, 4 * g + {3: 1, 2: 3, 0: 3, 1: 4}[i])
                s = (g % 2) * P_COLS + P_OFF[i]
                w, c = P * (i + 1), score_col(i)
                ins = act.activation(resid_flat[:, s:s + w], bank[b][:, c:c + w], ACT.Exp, scale=-1.0,
                                     bias=neg_max[:, g, i:i + 1], accum_out=row_sum[:, g, i:i + 1])
                if i != 2:
                    ins.then_inc(bank_free[b], 1)

            def pt_hi_half(g, part):
                lo, hi = ((0, 512), (512, 1024), (1024, 1280))[part]
                take_hi(("PT", g, part), pt_hi[:, g % 2, lo:hi], cols=slice(0, hi - lo))

            def take_ssq(fam):
                b = full(("ssq", fam))
                act.activation(ssq[:, N_OUT + 4 * fam:N_OUT + 4 * fam + 4], bank[b][:, 0:4],
                               ACT.Copy).then_inc(bank_free[b], 1)

            def attention(first, last, o_hi):
                def qk_hi(g):
                    take_hi(("QT", g), qt_hi[0:QK, g % 2, :], rows_=slice(0, QK))
                    take_hi(("KT", g), kt_hi[0:QK, g % 2, :], rows_=slice(0, QK))

                def head_out(g):
                    r = slice(HD * (g % 2), HD * (g % 2) + HD)
                    pair = (g % NH) // 2
                    b, n, m = use[("PV", g)]
                    act.wait_ge(bank_full[b], n)
                    if pair == 3 and g % 2 == 0:
                        act.wait_ge(sq_added, squares_added(g - 4))
                    elif pair == 2 and g % 2 == 0 and g > NH:
                        act.wait_ge(sq_added, 3)
                    sq = sq_acc[r, :] if pair == 0 else sq_tmp[r, pair % 2, :]
                    act.activation(sq, bank[b][r, :], ACT.Square).then_inc(sq_ready, 1)
                    act.activation(o_hi[r, pair, :], bank[b][r, :], ACT.Copy,
                                   scale=g_out[r, g // 2:g // 2 + 1]).then_inc(bank_hi[b], 1)

                plan = fitted(first // NH)

                def fit(g, slot):
                    n = (g - first) * SLOTS + slot
                    name, quarter = plan.get(n, (None, 0))
                    if name:
                        fit_product(name, quarter)

                def fit_product(name, quarter):
                    if quarter == 3:
                        b = full(name)
                        if name[0] == "mk":
                            take_hi(name, mk_hi[:, name[1], :], cols=slice(0, MEM))
                            return
                        c = name[1]
                        fam = 0 if c < CQ else 1
                        if c in (2, CQ + 1):
                            act.wait_ge(lat_sq_added, 1 if c == 2 else 2)
                        act.activation(lat_acc[:, fam, :] if c in (0, CQ) else lat_tmp, bank[b][:, :],
                                       ACT.Square).then_inc(lat_sq_ready, 1)
                        take_hi(name, ct_hi[:, c, :], scale=g_lat[:, c:c + 1])

                if first == 0:
                    eat(("cT", 0))
                qk_hi(first)
                fit(first, -2)
                fit(first, -1)
                if first:
                    take_transposed("memT", 0, mt_hi)
                for g in range(first, last + 1):
                    for i in (3, 2, 0):
                        exp_scores(g, i)
                    if g == NH:
                        eat(("ukv", 1))
                        take_transposed("memT", 1, mt_hi)
                        take_ssq(0)
                    fit(g, 0)
                    if g < last:
                        qk_hi(g + 1)
                    if g > first + 1:
                        head_out(g - 2)
                    if g > first:
                        pt_hi_half(g - 1, 0)
                    exp_scores(g, 1)
                    fit(g, 1)
                    if g > first:
                        pt_hi_half(g - 1, 1)
                        pt_hi_half(g - 1, 2)
                    fit(g, 2)
                    for slot in range(SLOTS):
                        name, quarter = plan.get((g - first) * SLOTS + slot, (None, 0))
                        if name and quarter == 0:
                            eat(name)
                extra = ("cT", NC_LAT - 1) if first == 0 else ("mk", H_MEM - 1)
                eat(extra)
                fit_product(extra, 3)
                head_out(last - 1)
                if first:
                    eat(("out", 0, 4))
                for part in range(3):
                    pt_hi_half(last, part)
                if first:
                    eat(("out", 0, 6))
                head_out(last)

            act.wait_ge(consts_loaded, 96)
            attention(0, NH - 1, of_hi)
            eat(("uq", 0))
            b = full(("cssq",))
            act.activation(ssq[:, N_CQ:N_CQ + 8], bank[b][:, 0:8], ACT.Copy).then_inc(bank_free[b], 1)
            eat(("uq", 1))
            for m in range(NM):
                act.wait_ge(mem_loaded[m], 16)
                square_rows(mem_rows[m], mem_junk[m], N_MEM + m)
            eat(("uq", 2))
            act.wait_ge(q_scale_ready, 1)
            for t in range(NT):
                for n in range(2):
                    b = full(("uq", t, n))
                    act.activation(nat_q[:, t, 4 * n:4 * n + 4, :],
                                   bank[b][:, 0:384].rearrange("p (h c) -> p h c", h=4), ACT.Copy,
                                   scale=q_scale[:, t:t + 1]).then_inc(bank_free[b], 1)
            eat(("ukv", 0))
            act.wait_ge(rstd_ready, norm_step(N_CKV))
            for t in range(NT):
                for n in range(2):
                    b = full(("ukv", t, n))
                    kv = bank[b][:, :].rearrange("p (h s c) -> p h s c", h=4, s=2)
                    kv_scale = rstd[:, N_CKV + t:N_CKV + t + 1]
                    act.activation(nat_k[:, t, 4 * n:4 * n + 4, 0:HD], kv[:, :, 0, :], ACT.Copy,
                                   scale=kv_scale).then_inc(k_nat, 1)
                    act.activation(vm_hi[:, t, 256 * n:256 * n + 256].rearrange("p (h c) -> p h c", h=4),
                                   kv[:, :, 1, :], ACT.Copy, scale=kv_scale).then_inc(bank_hi[b], 1)
            attention(NH, 2 * NH - 1, om_hi)
            for stage in range(1, 4):
                if stage == 2:
                    take_ssq(1)
                for k in (4, 6) if stage < 2 else (0, 2):
                    eat(("out", stage, k))
            for t in range(NT):
                if t < NM:
                    eat(("mv", 2 * t))
                summed(("out", 3, t))
                square_rows(resid[:, t, :], h_rows[t], N_H1 + t)
            for k in range(2 * NM, KD, 2):
                eat(("mv", k))
            for m in range(NM):
                take_hi(("mv", m), mv_hi[:, m, :])
            for t in range(NT):
                take_transposed("h1T", t, xt_hi)
            for step in MEM_STEPS:
                kind, h = step[0], step[1]
                if kind == "mq":
                    eat(step)
                    take_hi(step, mq_hi[:, h, :], scale=-MEM_SCALE)
                elif kind == "MS":
                    for u in range(2):
                        b = use[("MS", h, u)][0]
                        act.wait_ge(max_ready, 64 + 2 * h + u + 1)
                        for i in range(2):
                            t = 2 * u + i
                            p = work_flat[:, (h % 2) * D + t * MEM:(h % 2) * D + (t + 1) * MEM]
                            ins = act.activation(p, bank[b][:, i * MEM:(i + 1) * MEM], ACT.Exp, scale=-1.0,
                                                 bias=neg_max[:, h, t:t + 1], accum_out=row_sum[:, h, t:t + 1])
                            if i:
                                ins.then_inc(bank_free[b], 1)
                elif kind == "MPT":
                    for j in range(NM):
                        take_hi(("MPT", h, j), mp_hi[:, 2 * (h % 2) + j, :])
                elif kind == "MPV":
                    take_hi(step, mo_hi[:, h, :])
                elif step[3] == 0:
                    eat(("mo", h, step[2]))
            for t in range(NT):
                summed(("mo", 1, t))
                square_rows(resid[:, t, :], h_rows[t], N_H2 + t)
                if t >= 1:
                    take_transposed("h2T", t - 1, xt_hi)
            take_transposed("h2T", NT - 1, xt_hi)

            def act_ffn(f):
                b, n, _ = use[("gate", f)]
                act.wait_ge(bank_full[b], n)
                if f >= 2:
                    act.wait_ge(h_done, f - 1)
                act.activation(silu_buf[:, f % 2, :], bank[b][:, :], ACT.Silu).then_inc(silu_done, 1)
                act.wait_ge(h_done, f + 1)
                act.activation(ht_hi[:, f, :], h_buf[:, f % 2, :], ACT.Copy).then_inc(h_hi_done, 1)

            for f in range(NF):
                eat(("gate", f))
                eat(("up", f))
                if f >= 1:
                    act_ffn(f - 1)
            eat(("down", 0))
            act_ffn(NF - 1)
            for k in range(1, NF):
                eat(("down", k))
            for t in range(NT):
                act.wait_ge(resid_done, t + 1)
                square_rows(resid[:, t, :], h_rows[t], N_H3 + t)

        @block.vector
        def _(dve):
            chain = [0]

            def link(ins):
                chain[0] += 1
                ins.then_inc(dve_chain, 1)
                dve.wait_ge(dve_chain, chain[0])

            def take_lo(key, dst, hi, rows_=slice(0, P), cols=slice(0, HALF), scale=None, view=None):
                b, n, m = use[key]
                dve.wait_ge(bank_hi[b], m)
                src = bank[b][rows_, cols]
                if view:
                    src = view(src)
                if scale is None:
                    dve.tensor_tensor(dst, src, hi.bitcast(F32), ALU.subtract).then_inc(bank_free[b], 1)
                else:
                    dve.scalar_tensor_tensor(dst, src, scale, hi.bitcast(F32), ALU.mult,
                                             ALU.subtract).then_inc(bank_free[b], 1)

            def split_slab(n):
                if n >= NS:
                    return
                cols = slab_cols(n)
                dve.wait_ge(w_hi_done, n + 1)
                dve.tensor_tensor(w_lo[:, n % SPLIT, 0:cols], w_raw[:, n % RAW, 0:cols],
                                  w_hi[:, n % SPLIT, 0:cols].bitcast(F32), ALU.subtract).then_inc(w_lo_done, 1)

            def eat(key):
                if number[key] >= 1:
                    split_slab(number[key] + 1)

            def norm_rows(dst, src, col, gain):
                dve.wait_ge(rstd_ready, norm_step(col))
                return dve.scalar_tensor_tensor(dst, src, rstd[:, col:col + 1], gain, ALU.mult, ALU.mult)

            def take_transposed(name, t, hi, lo):
                for half in range(2):
                    s = (slice(None), slice(4 * half, 4 * half + 4), slice(t * P, (t + 1) * P))
                    take_lo((name, t, half), lo[s], hi[s], view=lambda x: x.rearrange("p (c n) -> p c n", c=4))

            dve.wait_ge(g_mix_loaded, 16)
            for t in range(NT):
                norm_rows(x_rows[t], resid[:, t, :], N_X + t, g_mix).then_inc(xn_ready, 1)
                if t == 1:
                    split_slab(0)
                if t == 2:
                    split_slab(1)
                if t >= 1:
                    take_transposed("xT", t - 1, xt_hi, xt_lo)
            take_transposed("xT", NT - 1, xt_hi, xt_lo)
            for k in range(0, KD, 2):
                eat(("vf", k))
            for t in range(NT):
                take_lo(("vf", t), vf_lo[:, t, :], vf_hi[:, t, :])
            eat(("rf", 0))
            eat(("qf", 0))
            dve.wait_ge(consts_loaded, 96)
            b, n, _ = use[("rft",)]
            dve.wait_ge(bank_free[b], n)
            link(dve.tensor_tensor(fz[:, :, :], krf[:, :, ROPE:], fbias[:, :].unsqueeze(1).to_broadcast([P, NT, NH]), ALU.add))
            dve.scalar_tensor_tensor(fa[:, :, :], fz[:, :, :], -1.0, fz[:, :, :], ALU.mult,
                                     ALU.max).then_inc(forget_z, 1)
            x1, x2 = krf[:, :, 0:16], krf[:, :, 16:32]
            cos, sin = rope_tab[:, 0, :, 0:16], rope_tab[:, 1, :, 0:16]
            ra, rb = rope_a[:, :, :], rope_b[:, :, :]
            link(dve.tensor_tensor(ra[:, :, 0:16], x1, cos, ALU.mult))
            link(dve.tensor_tensor(ra[:, :, 16:32], x2, cos, ALU.mult))
            link(dve.tensor_tensor(rb[:, :, 0:16], x2, sin, ALU.mult))
            link(dve.tensor_tensor(rb[:, :, 16:32], x1, sin, ALU.mult))
            link(dve.tensor_tensor(kro[:, :, 0:16], ra[:, :, 0:16], rb[:, :, 0:16], ALU.subtract))
            link(dve.tensor_tensor(kro[:, :, 16:32], ra[:, :, 16:32], rb[:, :, 16:32], ALU.add))
            dve.wait_ge(forget_l, 1)
            dve.scalar_tensor_tensor(logf[:, :, :], fz[:, :, :], 0.0, fl[:, :, :], ALU.min,
                                     ALU.subtract).then_inc(logf_ready, 1)
            for k in range(2, KD, 2):
                eat(("qf", k))
            b, n, _ = use[("cum",)]
            dve.wait_ge(bank_full[b], n)
            dve.wait_ge(nat_cleared, 2)
            cum = bank[b][:, 0:NT * NH].rearrange("p (t h) -> p t h", t=NT)
            dve.tensor_scalar(nat_q[:, :, :, HD], cum, -1.0, None, ALU.mult).then_inc(krope_nat, 1)
            dve.tensor_copy(nat_k[:, :, :, HD + 1], cum).then_inc(bank_free[b], 1)
            for k in range(0, KD, 2):
                eat(("kf", k))

            def negated_max(g, i):
                b, n, _ = use[("S", g, i)]
                dve.wait_ge(bank_full[b], n)
                c = score_col(i)
                dve.tensor_reduce(neg_max[:, g, i:i + 1], bank[b][:, c:c + P * (i + 1)], AX.X,
                                  ALU.min).then_inc(max_ready, 1)

            def invert(g, i):
                b, n, _ = use[("S", g, i)]
                dve.wait_ge(bank_free[b], n)
                c = slice(0, 3, 2) if i == 2 else slice(i, i + 1)
                dve.reciprocal(row_inv[:, g, c], row_sum[:, g, c]).then_inc(inv_ready, 1)

            def pt_lo_half(g, part):
                lo, hi = ((0, 512), (512, 1024), (1024, 1280))[part]
                take_lo(("PT", g, part), pt_lo[:, g % 2, lo:hi], pt_hi[:, g % 2, lo:hi], cols=slice(0, hi - lo))

            def attention(first, last, o_hi, o_lo):
                def qk_lo(g):
                    r = slice(0, QK)
                    take_lo(("QT", g), qt_lo[r, g % 2, :], qt_hi[r, g % 2, :], rows_=r)
                    take_lo(("KT", g), kt_lo[r, g % 2, :], kt_hi[r, g % 2, :], rows_=r)

                def head_out(g):
                    r = slice(HD * (g % 2), HD * (g % 2) + HD)
                    c = (g % NH) // 2
                    take_lo(("PV", g), o_lo[r, c, :], o_hi[r, c, :], rows_=r, scale=g_out[r, g // 2:g // 2 + 1])

                plan = fitted(first // NH)

                def fit(g, slot):
                    n = (g - first) * SLOTS + slot
                    name, quarter = plan.get(n, (None, 0))
                    if name:
                        fit_product(name, quarter)

                def fit_product(name, quarter):
                    if quarter == 3:
                        c = name[1]
                        if name[0] == "mk":
                            take_lo(name, mk_lo[:, c, :], mk_hi[:, c, :], cols=slice(0, MEM))
                        else:
                            take_lo(name, ct_lo[:, c, :], ct_hi[:, c, :], scale=g_lat[:, c:c + 1])

                if first == 0:
                    eat(("cT", 0))
                qk_lo(first)
                fit(first, -2)
                fit(first, -1)
                if first:
                    take_transposed("memT", 0, mt_hi, mt_lo)
                for g in range(first, last + 1):
                    negated_max(g, 3)
                    negated_max(g, 2)
                    negated_max(g, 0)
                    invert(g, 3)
                    invert(g, 2)
                    if g == NH:
                        eat(("ukv", 1))
                        take_transposed("memT", 1, mt_hi, mt_lo)
                    fit(g, 0)
                    if g < last:
                        qk_lo(g + 1)
                    if g > first + 1:
                        head_out(g - 2)
                    negated_max(g, 1)
                    if g > first:
                        pt_lo_half(g - 1, 0)
                    invert(g, 1)
                    fit(g, 1)
                    if g > first:
                        pt_lo_half(g - 1, 1)
                        pt_lo_half(g - 1, 2)
                    fit(g, 2)
                    for slot in range(SLOTS):
                        name, quarter = plan.get((g - first) * SLOTS + slot, (None, 0))
                        if name and quarter == 0:
                            eat(name)
                extra = ("cT", NC_LAT - 1) if first == 0 else ("mk", H_MEM - 1)
                eat(extra)
                fit_product(extra, 3)
                head_out(last - 1)
                if first:
                    eat(("out", 0, 4))
                for part in range(3):
                    pt_lo_half(last, part)
                if first:
                    eat(("out", 0, 6))
                head_out(last)

            attention(0, NH - 1, of_hi, of_lo)
            b, n, _ = use[("KT", NH - 1)]
            dve.wait_ge(bank_full[b], n)
            dve.tensor_copy(nat_k[:, :, :, HD:QK],
                            kro[:, :, :].unsqueeze(2).to_broadcast([P, NT, NH, ROPE])).then_inc(krope_nat, 1)
            for k in range(2):
                eat(("uq", k))
            dve.wait_ge(g_memkv_loaded, 16)
            for m in range(NM):
                norm_rows(mem_rows[m], mem_rows[m], N_MEM + m, g_memkv).then_inc(xn_ready, 1)
            eat(("uq", 2))
            for ts in (slice(0, 2), slice(2, 4)):
                if ts.start:
                    dve.wait_ge(qrope_nat, 1)
                for n in range(2):
                    b, turn, _ = use[("uq", ts.stop - 1, n)]
                    dve.wait_ge(bank_free[b], turn)
                q_rope = nat_q[:, ts, :, HD:QK]
                cos_part, sin_part = q_cos, q_sin
                for dst, which in ((cos_part, 0), (sin_part, 1)):
                    table = rope_tab[:, which, ts, :].unsqueeze(2).to_broadcast([P, 2, NH, ROPE])
                    link(dve.tensor_tensor(dst, q_rope, table, ALU.mult))
                link(dve.tensor_tensor(q_rope[:, :, :, 0:16], cos_part[:, :, :, 0:16], sin_part[:, :, :, 16:32],
                                       ALU.subtract))
                dve.tensor_tensor(q_rope[:, :, :, 16:32], cos_part[:, :, :, 16:32], sin_part[:, :, :, 0:16],
                                  ALU.add).then_inc(qrope_nat, 1)
                if ts.start == 0:
                    eat(("ukv", 0))
            for t in range(NT):
                for n in range(2):
                    s = slice(256 * n, 256 * n + 256)
                    take_lo(("ukv", t, n), vm_lo[:, t, s].rearrange("p (h c) -> p h c", h=4),
                            vm_hi[:, t, s].rearrange("p (h c) -> p h c", h=4),
                            scale=rstd[:, N_CKV + t:N_CKV + t + 1],
                            view=lambda x: x.rearrange("p (h s c) -> p h s c", h=4, s=2)[:, :, 1, :])
            attention(NH, 2 * NH - 1, om_hi, om_lo)
            dve.wait_ge(x_again, 16)
            for stage in range(4):
                if stage:
                    for k in (4, 6) if stage < 2 else (0, 2):
                        eat(("out", stage, k))
                fam, s = stage // 2, slice(HALF * (stage % 2), HALF * (stage % 2) + HALF)
                dve.wait_ge(rstd_ready, norm_step(N_OUT + 4 * fam))
                for t in range(NT):
                    b, n, _ = use[("out", stage, t)]
                    if stage >= 2:
                        before, turn, _ = use[("out", stage - 2, t)]
                        dve.wait_ge(bank_free[before], turn)
                    dve.wait_ge(bank_full[b], n)
                    dve.scalar_tensor_tensor(resid[:, t, s], bank[b][:, :],
                                             rstd[:, N_OUT + 4 * fam + t:N_OUT + 4 * fam + t + 1], resid[:, t, s],
                                             ALU.mult, ALU.add).then_inc(bank_free[b], 1)
            dve.wait_ge(late_loaded, 48)
            for t in range(NT):
                if t < NM:
                    eat(("mv", 2 * t))
                norm_rows(h_rows[t], resid[:, t, :], N_H1 + t, g_memq).then_inc(xn_ready, 1)
            for k in range(2 * NM, KD, 2):
                eat(("mv", k))
            for m in range(NM):
                take_lo(("mv", m), mv_lo[:, m, :], mv_hi[:, m, :])
            for t in range(NT):
                take_transposed("h1T", t, xt_hi, xt_lo)
            for step in MEM_STEPS:
                kind, h = step[0], step[1]
                if kind == "mq":
                    eat(step)
                    take_lo(step, mq_lo[:, h, :], mq_hi[:, h, :], scale=-MEM_SCALE)
                elif kind == "MS":
                    for u in range(2):
                        b, n, _ = use[("MS", h, u)]
                        dve.wait_ge(bank_full[b], n)
                        dve.tensor_reduce(neg_max[:, h, 2 * u:2 * u + 2],
                                          bank[b][:, :].rearrange("p (i k) -> p i k", i=2), AX.X,
                                          ALU.min).then_inc(max_ready, 1)
                    for u in range(2):
                        b, n, _ = use[("MS", h, u)]
                        dve.wait_ge(bank_free[b], n)
                        link(dve.reciprocal(row_inv[:, h, 2 * u:2 * u + 2], row_sum[:, h, 2 * u:2 * u + 2]))
                        for t in range(2 * u, 2 * u + 2):
                            p = work_flat[:, (h % 2) * D + t * MEM:(h % 2) * D + (t + 1) * MEM]
                            dve.tensor_scalar(p, p, row_inv[:, h, t:t + 1], None, ALU.mult).then_inc(inv_ready, 1)
                elif kind == "MPT":
                    for j in range(NM):
                        take_lo(("MPT", h, j), mp_lo[:, 2 * (h % 2) + j, :], mp_hi[:, 2 * (h % 2) + j, :])
                elif kind == "MPV":
                    take_lo(step, mo_lo[:, h, :], mo_hi[:, h, :])
                else:
                    n, k, t = step[1:]
                    if t == 0:
                        eat(("mo", n, k))
                    if k == 2:
                        b, turn, _ = use[("mo", n, t)]
                        dve.wait_ge(bank_full[b], turn)
                        s = slice(n * HALF, (n + 1) * HALF)
                        dve.tensor_tensor(resid[:, t, s], bank[b][:, :], resid[:, t, s],
                                          ALU.add).then_inc(bank_free[b], 1)
            for t in range(NT):
                norm_rows(h_rows[t], resid[:, t, :], N_H2 + t, g_ffn).then_inc(xn_ready, 1)
                if t >= 1:
                    take_transposed("h2T", t - 1, xt_hi, xt_lo)
            take_transposed("h2T", NT - 1, xt_hi, xt_lo)

            def dve_ffn(f):
                b, n, _ = use[("up", f)]
                bg = use[("gate", f)][0]
                dve.wait_ge(bank_full[b], n)
                dve.wait_ge(silu_done, f + 1)
                if f >= 2:
                    dve.wait_ge(h_lo_done, f - 1)
                    dve.wait_ge(h_hi_done, f - 1)
                dve.tensor_tensor(h_buf[:, f % 2, :], bank[b][:, :], silu_buf[:, f % 2, :], ALU.mult).then_inc(h_done, 1)
                dve.wait_ge(h_hi_done, f + 1)
                dve.tensor_tensor(ht_lo[:, f, :], h_buf[:, f % 2, :], ht_hi[:, f, :].bitcast(F32),
                                  ALU.subtract).then_inc(h_lo_done, 1)

            for f in range(NF):
                eat(("gate", f))
                eat(("up", f))
                if f >= 1:
                    dve_ffn(f - 1)
            eat(("down", 0))
            dve_ffn(NF - 1)
            for k in range(1, NF):
                eat(("down", k))
            for t in range(NT):
                for n in range(2):
                    b, turn, _ = use[("down", t, n)]
                    dve.wait_ge(bank_full[b], turn)
                    s = slice(n * HALF, (n + 1) * HALF)
                    ins = dve.tensor_tensor(resid[:, t, s], bank[b][:, :], resid[:, t, s], ALU.add)
                    if n == 1:
                        ins.then_inc(resid_done, 1)
                    else:
                        ins.then_inc(dve_chain, 1)
                        chain[0] += 1
                if t >= 1:
                    norm_rows(h_rows[t - 1], resid[:, t - 1, :], N_H3 + t - 1, g_final).then_inc(xn_ready, 1)
            norm_rows(h_rows[NT - 1], resid[:, NT - 1, :], N_H3 + NT - 1, g_final).then_inc(xn_ready, 1)

        @block.tensor
        def _(pe):
            def claim(key):
                b, n, _ = use[key]
                if n > 1:
                    pe.wait_ge(bank_free[b], n - 1)
                return b

            def ready(key):
                b, n, _ = use[key]
                pe.wait_ge(bank_free[b], n)

            def product(dst, a_hi, a_lo, b_hi, b_lo, first, last):
                pe.matmul(dst, a_hi, b_hi, start=first, stop=False, skip_group_check=True)
                pe.matmul(dst, a_hi, b_lo, start=False, stop=False, skip_group_check=True)
                return pe.matmul(dst, a_lo, b_hi, start=False, stop=last, skip_group_check=True)

            def slab_ready(key):
                pe.wait_ge(w_lo_done, number[key] + 1)

            def transpose_rows(name, t, src):
                for half in range(2):
                    b = claim((name, t, half))
                    for c in range(4):
                        mm = pe.transpose(bank[b][:, c * P:(c + 1) * P],
                                          src[:, (4 * half + c) * P:(4 * half + c + 1) * P], ident[:, :])
                    mm.then_inc(bank_full[b], 1)

            def tokens_times_weights(keys, out_key, lhs_hi, lhs_lo, cols, chunks, halves=1, tile_ready=None,
                                     after_first=None):
                per = slabs[number[keys[0]]][1][0][0]
                for s, key in enumerate(keys):
                    slab_ready(key)
                    for t in range(NT):
                        if s == 0 and tile_ready:
                            tile_ready(t)
                        for n in range(halves):
                            okey = out_key(t, n)
                            b = claim(okey) if s == 0 else use[okey][0]
                            for k in range(per):
                                c = chunks[s * per + k]
                                ts = slice(t * P, (t + 1) * P)
                                wh, wl = split_of(key, k, n * cols, (n + 1) * cols)
                                mm = product(bank[b][:, 0:cols], lhs_hi[:, c, ts], lhs_lo[:, c, ts], wh, wl,
                                             s == 0 and k == 0, s == len(keys) - 1 and k == per - 1)
                            last = t == NT - 1 and n == halves - 1
                            if s == len(keys) - 1:
                                mm.then_inc(bank_full[b], 1)
                            elif last:
                                mm.then_inc(w_used, 1)
                    if s == 0 and after_first:
                        after_first()

            def in_projection(name, tile_ready=None, after_first=None):
                tokens_times_weights([(name, k) for k in range(0, KD, 2)], lambda t, n: (name, t), xt_hi, xt_lo,
                                     HALF, list(range(KD)), tile_ready=tile_ready, after_first=after_first)

            def transposed_ready(name, t):
                ready((name, t, 0))
                ready((name, t, 1))

            pe.wait_ge(consts_made, 4)
            for t in range(NT):
                pe.wait_ge(xn_ready, XN_X + t + 1)
                transpose_rows("xT", t, x_rows[t])
            in_projection("vf", lambda t: transposed_ready("xT", t))
            slab_ready(("rf", 0))
            b = claim(("rf",))
            for k in range(KD):
                wh, wl = split_of(("rf", 0), k, 0, RF)
                mm = product(bank[b][0:RF, :], wh, wl, xt_hi[:, k, :], xt_lo[:, k, :], k == 0, k == KD - 1)
            mm.then_inc(bank_full[b], 1)

            def rf_transposes():
                ready(("rf",))
                b = claim(("rft",))
                for t in range(NT):
                    mm = pe.transpose(bank[b][:, RF * t:RF * (t + 1)], rf_t[:, t * P:(t + 1) * P], ident[0:RF, 0:RF])
                mm.then_inc(bank_full[b], 1)

            in_projection("qf", after_first=rf_transposes)
            b = claim(("cum",))
            pe.wait_ge(logf_ready, 1)
            for t in range(NT):
                for u in range(t + 1):
                    mm = pe.matmul(bank[b][:, t * NH:(t + 1) * NH], upto[:, :] if u == t else ones[:, :],
                                   logf[:, u, :], start=(u == 0), stop=(u == t), skip_group_check=True)
            mm.then_inc(bank_full[b], 1)
            in_projection("kf")

            def weights_times_tokens(key, chunks, cols, rhs_hi, rhs_lo, where=slice(0, SEQ)):
                b = use[key][0]
                for k in chunks:
                    wh, wl = split_of(key, k, 0, P)
                    mm = product(bank[b][:, cols], wh, wl, rhs_hi[:, k, where], rhs_lo[:, k, where], k == 0,
                                 k == KD - 1)
                return mm

            def attention(first, last, v_hi, v_lo):
                def qk_transposes(g):
                    if g == 0:
                        for t in range(NT):
                            ready(("qf", t))
                            ready(("kf", t))
                            ready(("vf", t))
                        ready(("cum",))
                        pe.wait_ge(krope_nat, 1)
                    if g == NH:
                        pe.wait_ge(krope_nat, 2)
                        pe.wait_ge(qrope_nat, 2)
                        pe.wait_ge(k_nat, 2 * NT - 1)
                    h = g % NH
                    for name, src in (("QT", nat_q), ("KT", nat_k)):
                        b = claim((name, g))
                        for t in range(NT):
                            mm = pe.transpose(bank[b][0:QK, t * P:(t + 1) * P], src[:, t, h, :], ident[:, :])
                        mm.then_inc(bank_full[b], 1)

                def scores(g, *tiles):
                    b = claim(("S", g, tiles[0]))
                    if tiles[0] == 3:
                        ready(("QT", g))
                        ready(("KT", g))
                    for i in tiles:
                        w = P * (i + 1)
                        q, k = slice(i * P, w), slice(0, w)
                        c = score_col(i)
                        product(bank[b][:, c:c + w], qt_hi[0:QK, g % 2, q], qt_lo[0:QK, g % 2, q],
                                kt_hi[0:QK, g % 2, k], kt_lo[0:QK, g % 2, k], True, False)
                        mm = pe.matmul(bank[b][:, c + i * P:c + w], ident_bf[:, :], mask_bf[:, :], start=False,
                                       stop=True, skip_group_check=True)
                    mm.then_inc(bank_full[b], 1)

                def probs_transposes(g, part):
                    if part == 0:
                        pe.wait_ge(probs_ready, 4 * (g + 1))
                    b = claim(("PT", g, part))
                    blocks = (((0, 0), (1, 0), (2, 0), (3, 0)), ((1, 1), (2, 1), (3, 1), (3, 3)),
                              ((2, 2), (3, 2)))[part]
                    for n, (i, j) in enumerate(blocks):
                        s = (g % 2) * P_COLS + P_OFF[i] + j * P
                        mm = pe.transpose(bank[b][:, n * P:(n + 1) * P], resid_flat[:, s:s + P], ident[:, :])
                    mm.then_inc(bank_full[b], 1)

                def values(g):
                    b = claim(("PV", g))
                    c = (g % NH) // 2
                    for part in range(3):
                        ready(("PT", g, part))
                    for j, s in enumerate((0, 512, 1024, 896)):
                        w = SEQ - P * j
                        vs = slice(c * P, (c + 1) * P)
                        mm = product(bank[b][:, P * j:SEQ], v_hi[:, j, vs], v_lo[:, j, vs],
                                     pt_hi[:, g % 2, s:s + w], pt_lo[:, g % 2, s:s + w], j == 0, j == NT - 1)
                    mm.then_inc(bank_full[b], 1)

                plan = fitted(first // NH)

                def fit(g, slot):
                    name, quarter = plan.get((g - first) * SLOTS + slot, (None, 0))
                    if not name:
                        return
                    fit_product(name, quarter)

                def fit_product(name, quarter):
                    if quarter == 0:
                        slab_ready(name)
                        claim(name)
                        if name == ("mk", 0):
                            transposed_ready("memT", 0)
                            transposed_ready("memT", 1)
                    rhs = (xt_hi, xt_lo) if name[0] == "cT" else (mt_hi, mt_lo)
                    width = SEQ if name[0] == "cT" else MEM
                    mm = weights_times_tokens(name, (2 * quarter, 2 * quarter + 1), slice(0, width), *rhs,
                                              where=slice(0, width))
                    if quarter == 3:
                        mm.then_inc(bank_full[use[name][0]], 1)

                fit(first, -4)
                fit(first, -3)
                qk_transposes(first)
                fit(first, -2)
                fit(first, -1)
                if first:
                    for m in range(NM):
                        pe.wait_ge(xn_ready, XN_MEM + m + 1)
                        transpose_rows("memT", m, mem_rows[m])
                for g in range(first, last + 1):
                    scores(g, 3)
                    scores(g, 2, 0)
                    if g == NH:
                        sum_squares(0)
                        pe.wait_ge(k_nat, 2 * NT)
                        for t in range(NT):
                            for n in range(2):
                                ready(("ukv", t, n))
                    fit(g, 0)
                    if g < last:
                        qk_transposes(g + 1)
                    if g > first + 1:
                        values(g - 2)
                    if g > first:
                        probs_transposes(g - 1, 0)
                    scores(g, 1)
                    fit(g, 1)
                    if g > first:
                        probs_transposes(g - 1, 1)
                        probs_transposes(g - 1, 2)
                    fit(g, 2)
                for quarter in range(4):
                    fit_product(("cT", NC_LAT - 1) if first == 0 else ("mk", H_MEM - 1), quarter)
                values(last - 1)

                def last_transposes():
                    for part in range(3):
                        probs_transposes(last, part)

                if first:
                    out_projection(0, after_first=last_transposes)
                    values(last)
                else:
                    last_transposes()
                return values

            def out_projection(stage, after_first=None):
                fam = stage // 2
                tokens_times_weights([("out", stage, k) for k in ((4, 6) if stage < 2 else (0, 2))],
                                     lambda t, n: ("out", stage, t), *((of_hi, of_lo), (om_hi, om_lo))[fam],
                                     HALF, [0, 1, 2, 3], after_first=after_first)

            def sum_over_features(b, col, squares):
                for t in range(NT):
                    mm = pe.matmul(bank[b][:, col + t:col + t + 1], squares[:, t * P:(t + 1) * P], ones[:, 0:1],
                                   start=True, stop=True)
                return mm

            def sum_squares(fam):
                b = claim(("ssq", fam))
                pe.wait_ge(sq_added, 3 * (fam + 1))
                sum_over_features(b, 0, sq_acc).then_inc(bank_full[b], 1)

            values = attention(0, NH - 1, vf_hi, vf_lo)

            def latents_ready(t):
                if t == 0:
                    for c in range(NC_LAT):
                        ready(("cT", c))
                if t == 2:
                    values(NH - 1)
                if t == NT - 1:
                    b = claim(("cssq",))
                    pe.wait_ge(lat_sq_ready, NC_LAT)
                    pe.wait_ge(lat_sq_added, NC_LAT - 2)
                    sum_over_features(b, 0, lat_acc[:, 0, :])
                    sum_over_features(b, 4, lat_acc[:, 1, :]).then_inc(bank_full[b], 1)

            tokens_times_weights([("uq", k) for k in range(CQ)], lambda t, n: ("uq", t, n), ct_hi, ct_lo, 384,
                                 [0, 1, 2], 2, tile_ready=latents_ready)
            tokens_times_weights([("ukv", k) for k in range(CKV)], lambda t, n: ("ukv", t, n), ct_hi, ct_lo, 512,
                                 [3, 4], 2)
            ready(("PV", NH - 1))
            attention(NH, 2 * NH - 1, vm_hi, vm_lo)
            for stage in range(1, 4):
                if stage == 2:
                    sum_squares(1)
                    ready(("PV", 2 * NH - 1))
                out_projection(stage)
            for k in range(0, KD, 2):
                slab_ready(("mv", k))
                for m in range(NM):
                    b = claim(("mv", m)) if k == 0 else use[("mv", m)][0]
                    ms = slice(m * P, (m + 1) * P)
                    for kk in range(2):
                        n = number[("mv", k)] % SPLIT
                        ws = slice(kk * HALF, (kk + 1) * HALF)
                        mm = product(bank[b][:, :], mt_hi[:, k + kk, ms], mt_lo[:, k + kk, ms], w_hi[:, n, ws],
                                     w_lo[:, n, ws], k + kk == 0, k + kk == KD - 1)
                    if k == KD - 2:
                        mm.then_inc(bank_full[b], 1)
                if k < KD - 2:
                    mm.then_inc(w_used, 1)
            for t in range(NT):
                pe.wait_ge(xn_ready, XN_H1 + t + 1)
                transpose_rows("h1T", t, h_rows[t])

            def with_all_tokens(key, name=None):
                if name is None:
                    weights_times_tokens(key, range(KD), slice(0, SEQ), xt_hi, xt_lo
                                         ).then_inc(bank_full[use[key][0]], 1)
                    return
                for half in range(2):
                    transposed_ready(name, 2 * half)
                    transposed_ready(name, 2 * half + 1)
                    s = slice(256 * half, 256 * half + 256)
                    mm = weights_times_tokens(key, range(KD), s, xt_hi, xt_lo, where=s)
                mm.then_inc(bank_full[use[key][0]], 1)

            for step in MEM_STEPS:
                kind, h = step[0], step[1]
                if kind == "mq":
                    slab_ready(step)
                    claim(step)
                    with_all_tokens(step, "h1T" if h == 0 else None)
                elif kind == "MS":
                    ready(("mq", h))
                    ready(("mk", h))
                    for u in range(2):
                        b = claim(("MS", h, u))
                        for i in range(2):
                            q = slice((2 * u + i) * P, (2 * u + i + 1) * P)
                            mm = product(bank[b][:, i * MEM:(i + 1) * MEM], mq_hi[:, h, q], mq_lo[:, h, q],
                                         mk_hi[:, h, :], mk_lo[:, h, :], True, True)
                        mm.then_inc(bank_full[b], 1)
                elif kind == "MPT":
                    pe.wait_ge(inv_ready, 3 * 2 * NH + 4 * (h + 1))
                    for j in range(NM):
                        b = claim(("MPT", h, j))
                        for t in range(NT):
                            c0 = (h % 2) * D + t * MEM + j * P
                            mm = pe.transpose(bank[b][:, t * P:(t + 1) * P], work_flat[:, c0:c0 + P], ident[:, :])
                        mm.then_inc(bank_full[b], 1)
                elif kind == "MPV":
                    b = use[step][0]
                    for j in range(NM):
                        ready(("mv", j))
                        ready(("MPT", h, j))
                    claim(step)
                    for j in range(NM):
                        hs = slice(h * P, (h + 1) * P)
                        mm = product(bank[b][:, :], mv_hi[:, j, hs], mv_lo[:, j, hs], mp_hi[:, 2 * (h % 2) + j, :],
                                     mp_lo[:, 2 * (h % 2) + j, :], j == 0, j == NM - 1)
                    mm.then_inc(bank_full[b], 1)
                else:
                    n, k, t = step[1:]
                    b = use[("mo", n, t)][0]
                    if k == 0:
                        claim(("mo", n, t))
                    slab_ready(("mo", n, k))
                    ready(("MPV", k + 1))
                    ts = slice(t * P, (t + 1) * P)
                    for kk in range(2):
                        mm = product(bank[b][:, :], mo_hi[:, k + kk, ts], mo_lo[:, k + kk, ts],
                                     *split_of(("mo", n, k), kk, 0, HALF), k + kk == 0, k + kk == H_MEM - 1)
                    if k == 2:
                        mm.then_inc(bank_full[b], 1)
                    elif t == NT - 1:
                        mm.then_inc(w_used, 1)
            for t in range(NT):
                pe.wait_ge(xn_ready, XN_H2 + t + 1)
                transpose_rows("h2T", t, h_rows[t])

            def claim_gate(f):
                if f >= 4:
                    pe.wait_ge(silu_done, f - 3)
                    pe.wait_ge(h_done, f - 3)

            for name in ("gate", "up"):
                claim((name, 0))
                slab_ready((name, 0))
            for half in range(2):
                transposed_ready("h2T", 2 * half)
                transposed_ready("h2T", 2 * half + 1)
                s = slice(256 * half, 256 * half + 256)
                for name in ("gate", "up"):
                    mm = weights_times_tokens((name, 0), range(KD), s, xt_hi, xt_lo, where=s)
                    if half:
                        mm.then_inc(bank_full[use[(name, 0)][0]], 1)
            for f in range(1, NF):
                claim_gate(f)
                for name in ("gate", "up"):
                    slab_ready((name, f))
                    if f < 4:
                        claim((name, f))
                    with_all_tokens((name, f))

            def down(k, t):
                ts = slice(t * P, (t + 1) * P)
                for n in range(2):
                    b = use[("down", t, n)][0]
                    mm = product(bank[b][:, :], ht_hi[:, k, ts], ht_lo[:, k, ts],
                                 *split_of(("down", k), 0, n * HALF, (n + 1) * HALF), k == 0, k == NF - 1)
                    if k == NF - 1:
                        mm.then_inc(bank_full[b], 1)
                    elif t == (1 if k == 0 else NT - 1) and n == 1:
                        mm.then_inc(w_used, 1)

            slab_ready(("down", 0))
            pe.wait_ge(h_lo_done, 1)
            for t in (2, 3, 0, 1):
                claim_gate({2: NF, 3: NF + 1, 0: NF + 2, 1: NF + 3}[t])
                down(0, t)
            for k in range(1, NF - 2):
                slab_ready(("down", k))
                pe.wait_ge(h_lo_done, k + 1)
                for t in range(NT):
                    down(k, t)
            slab_ready(("down", NF - 2))
            pe.wait_ge(h_lo_done, NF)
            down(NF - 2, 0)
            down(NF - 2, 1)
            slab_ready(("down", NF - 1))
            for t in range(NT):
                if t >= 2:
                    down(NF - 2, t)
                down(NF - 1, t)


_INS = ["x", "mem", "mix_norm_g", "w_in", "cq_norm_g", "ckv_norm_g", "w_uq", "w_ukv", "forget_bias", "mla_out_g",
        "fox_out_g", "w_out", "mem_q_norm_g", "mem_kv_norm_g", "w_mq", "w_mkv", "w_mo", "ffn_norm_g", "w_gate",
        "w_up", "w_down", "final_norm_g"]


def rope_tables():
    inv = (1.0 / (np.float32(10000.0) ** (np.arange(0, ROPE, 2, dtype=np.float32) / np.float32(ROPE)))).astype(np.float32)
    ang = np.arange(SEQ, dtype=np.float32)[:, None] * inv[None, :]
    cos, sin = np.cos(ang).astype(np.float32), np.sin(ang).astype(np.float32)
    both = [np.concatenate([m, m], axis=1) for m in (cos, sin)]
    return np.stack(both)


def kernel(**inputs):
    import numpy as _np
    import concourse.bacc as _bacc
    from concourse import mybir as _mybir
    from concourse.bass_utils import run_bass_kernel_spmd as _run

    nc = _bacc.Bacc("TRN2", target_bir_lowering=False, num_devices=1)
    arrays, aps = {}, {}
    for name in _INS + ["rope"]:
        v = _np.ascontiguousarray(inputs[name]) if name != "rope" else rope_tables()
        arrays[f"in_{name}_dram"] = v
        aps[name] = nc.dram_tensor(f"in_{name}_dram", v.shape, _mybir.dt.from_np(v.dtype), kind="ExternalInput").ap()
    out = nc.dram_tensor("out_0_dram", (1, SEQ, D), _mybir.dt.float32, kind="ExternalOutput").ap()
    build(nc, aps, out)
    r = _run(nc, [arrays], core_ids=[0])
    return r.results[0]["out_0_dram"]
```

```python
from contextlib import ExitStack

import numpy as np
import concourse.bass as bass
from concourse import mybir

F32 = mybir.dt.float32
F32R = mybir.dt.float32r
BF16 = mybir.dt.bfloat16
ALU = mybir.AluOpType
ACT = mybir.ActivationFunctionType
AX = mybir.AxisListType

P = 128
D = 1024
SEQ = 512
MEM = 256
NT = SEQ // P
NM = MEM // P
KD = D // P
NH = 8
HD = 64
ROPE = 32
QK = HD + ROPE
Q_LORA = 384
KV_LORA = 256
CQ, CKV = Q_LORA // P, KV_LORA // P
H_MEM = 4
MEM_HD = 128
D_FF = 2816
NF = D_FF // P
HALF = 512
EPS = 1e-6
SLOT = 1024
TILE_ORDER = (3, 2, 0, 1)
RAW = 3
SPLIT = 2
MLA_SCALE = float(QK) ** -0.5
FOX_SCALE = float(HD) ** -0.5
MEM_SCALE = float(MEM_HD) ** -0.5
MASKED = 1e30
P_OFF = [0, 128, 384, 768]
P_COLS = 1280
NC_LAT = CQ + CKV
RF = ROPE + NH
FOX_SLOTS = ((-4, -3, -2, -1), (1, 2, 3, 5), (7, 8, 10, 11), (13, 14, 16, 17))
MLA_SLOTS = ((2, 3, 4, 5), (7, 8, 10, 11), (14, 16, 17, 20))
SLOTS = 3


def fitted(fam):
    if fam == 0:
        slots = {("cT", c): FOX_SLOTS[c] for c in range(NC_LAT - 1)}
    else:
        slots = {("mk", h): MLA_SLOTS[h] for h in range(H_MEM - 1)}
    plan = {slot: (name, q) for name, places in slots.items() for q, slot in enumerate(places)}
    return plan


C_CQ, C_CKV, C_ROPE, C_QF, C_KF, C_VF, C_F = 0, 384, 640, 672, 1184, 1696, 2208

MEM_STEPS = ([("mq", 0), ("mq", 1), ("MS", 0), ("mq", 2), ("MS", 1), ("mq", 3), ("MPT", 0), ("MPT", 1), ("MS", 2),
              ("MPV", 0), ("MPV", 1), ("MS", 3), ("mo", 0, 0, 0), ("mo", 0, 0, 1), ("MPT", 2), ("mo", 0, 0, 2),
              ("MPT", 3), ("MPV", 2), ("MPV", 3), ("mo", 0, 0, 3)]
             + [("mo", 0, 2, t) for t in range(NT)]
             + [("mo", 1, 0, 0), ("mo", 1, 0, 1), ("mo", 1, 2, 0), ("mo", 1, 2, 1), ("h2T", 0, 0), ("h2T", 0, 1),
                ("square", 0), ("mo", 1, 0, 2), ("mo", 1, 2, 2), ("h2T", 0, 2), ("h2T", 0, 3), ("square", 1),
                ("mo", 1, 0, 3), ("mo", 1, 2, 3), ("h2T", 1, 0), ("h2T", 1, 1), ("h2T", 1, 2), ("square", 2),
                ("h2T", 1, 3), ("square", 3)])
OUT_BANKS = [(5, 7, 0, 1), (2, 3, 4, 6)] * 2
H1T_BANKS = [(5, 7, 0, 1), (2, 3, 4, 6)]
UQ_BANKS = (0, 1, 5, 7, 2, 3, 4, 6)


class Banks:

    def __init__(self):
        self.turns = [0] * 8
        self.hi_turns = [0] * 8
        self.use = {}

    def add(self, key, bank, split=False):
        self.turns[bank] += 1
        if split:
            self.hi_turns[bank] += 1
        self.use[key] = (bank, self.turns[bank], self.hi_turns[bank])


def plan_banks():
    bk = Banks()
    for t in range(NT):
        for half in range(2):
            bk.add(("xT", t, half), 2 * t + half, True)
    for t in range(NT):
        bk.add(("vf", t), t, True)
    bk.add(("rf",), 7)
    for t in range(NT):
        bk.add(("qf", t), 4 + t)
    bk.add(("rft",), 0)
    bk.add(("cum",), 3)
    for t in range(NT):
        bk.add(("kf", t), t)

    s_turn = [0]

    def attention(heads):
        first, last = heads[0], heads[-1]
        plan = fitted(first // NH)

        def scores(g, i):
            bk.add(("S", g, i), s_turn[0] % 2)
            if i == 2:
                bk.use[("S", g, 0)] = bk.use[("S", g, 2)]
            s_turn[0] += 1

        def transposed(g, part):
            bk.add(("PT", g, part), (2, 3, 4)[part], True)

        def qkt(g):
            bk.add(("QT", g), 4, True)
            bk.add(("KT", g), 5, True)

        def fit(g, slot):
            name, quarter = plan.get((g - first) * SLOTS + slot, (None, 0))
            if name and quarter == 0:
                bk.add(name, 7, True)

        fit(first, -4)
        fit(first, -3)
        qkt(first)
        fit(first, -2)
        fit(first, -1)
        if first:
            for m in range(NM):
                for half in range(2):
                    bk.add(("memT", m, half), ((7, 6), (2, 3))[m][half], True)
        for g in heads:
            scores(g, 3)
            scores(g, 2)
            if g == NH:
                bk.add(("ssq", 0), 6)
            fit(g, 0)
            if g < last:
                qkt(g + 1)
            if g > first + 1:
                bk.add(("PV", g - 2), 6, True)
            if g > first:
                transposed(g - 1, 0)
            scores(g, 1)
            fit(g, 1)
            if g > first:
                transposed(g - 1, 1)
                transposed(g - 1, 2)
            fit(g, 2)
        bk.add(("cT", NC_LAT - 1) if first == 0 else ("mk", H_MEM - 1), 7, True)
        bk.add(("PV", last - 1), 6, True)
        for t in range(NT if first else 0):
            bk.add(("out", 0, t), OUT_BANKS[0][t])
        for part in range(3):
            transposed(last, part)
        bk.add(("PV", last), 6, True)

    attention(list(range(NH)))
    bk.add(("cssq",), 4)
    for t in range(NT):
        for n in range(2):
            bk.add(("uq", t, n), UQ_BANKS[2 * t + n])
    for t in range(NT):
        for n in range(2):
            bk.add(("ukv", t, n), 2 * t + n, True)
    attention(list(range(NH, 2 * NH)))
    for stage in range(1, 4):
        if stage == 2:
            bk.add(("ssq", 1), 5)
        elif stage == 3:
            for t in range(NT):
                bk.add(("h1T", t, 0), H1T_BANKS[0][t], True)
        for t in range(NT):
            bk.add(("out", stage, t), OUT_BANKS[stage][t])
    for m in range(NM):
        bk.add(("mv", m), (7, 5)[m], True)
    for t in range(NT):
        bk.add(("h1T", t, 1), H1T_BANKS[1][t], True)
    for step in MEM_STEPS:
        if step[0] == "mq":
            bk.add(step, (0, 5, 4, 5)[step[1]], True)
        elif step[0] == "MS":
            for u in range(2):
                bk.add(("MS", step[1], u), u)
        elif step[0] == "MPT":
            for j in range(NM):
                bk.add(("MPT", step[1], j), (2, 6, 2, 0)[step[1]] + j, True)
        elif step[0] == "MPV":
            bk.add(step, 2 + step[1] % 2, True)
        elif step[0] == "mo" and step[2] == 0:
            bk.add(("mo", step[1], step[3]), 4 * (1 - step[1]) + step[3])
        elif step[0] == "h2T":
            bk.add(("h2T", step[2], step[1]), 4 + step[2], True)
    for f in range(NF):
        bk.add(("gate", f), 2 * (f % 4))
        bk.add(("up", f), 2 * (f % 4) + 1)
        if f == 0:
            bk.add(("rstd rows",), 7)
    for t in range(NT):
        for n in range(2):
            bk.add(("down", t, n), 2 * t + n)
    return bk.use


def build(nc, a, out):
    use = plan_banks()

    with ExitStack() as ctx:
        def sb(name, shape, dt=F32):
            return ctx.enter_context(nc.sbuf_tensor(name, shape, dt))

        def sem(name):
            return ctx.enter_context(nc.semaphore(name))

        w_raw = sb("w_raw", [P, RAW, SLOT])
        w_hi = sb("w_hi", [P, SPLIT, SLOT], F32R)
        w_lo = sb("w_lo", [P, SPLIT, SLOT], F32R)
        xt_hi = sb("xt_hi", [P, KD, SEQ], F32R)
        xt_lo = sb("xt_lo", [P, KD, SEQ], F32R)
        resid = sb("resid", [P, NT, D])
        work = sb("work", [P, 2, D])
        nat = sb("nat", [P, 2 * NT * NH * QK])
        arena = sb("arena", [P, NF * 2 * HALF], F32R)
        ident = sb("ident", [P, P])
        ident_bf = sb("ident_bf", [P, P], BF16)
        mask_bf = sb("mask_bf", [P, P], BF16)
        upto = sb("upto", [P, P])
        ones = sb("ones", [P, P])
        rope_tab = sb("rope_tab", [P, 2, NT, ROPE])
        rope_a = sb("rope_a", [P, NT, ROPE])
        rope_b = sb("rope_b", [P, NT, ROPE])
        krf = sb("krf", [P, NT, ROPE + NH])
        kro = sb("kro", [P, NT, ROPE])
        fbias = sb("fbias", [P, NH])
        fz = sb("fz", [P, NT, NH])
        fa = sb("fa", [P, NT, NH])
        fe = sb("fe", [P, NT, NH])
        fl = sb("fl", [P, NT, NH])
        logf = sb("logf", [P, NT, NH])
        g_out = sb("g_out", [P, NH])
        g_lat = sb("g_lat", [P, NC_LAT])
        q_scale = sb("q_scale", [P, NT])
        NNORM = 4 + 4 + 4 + 8 + 2 + 4 + 4 + 4
        ssq = sb("ssq", [P, NNORM])
        msq = sb("msq", [P, NNORM])
        rstd = sb("rstd", [P, NNORM])
        neg_half = sb("neg_half", [P, 4])
        row_max = sb("row_max", [P, H_MEM, NT])
        neg_max = sb("neg_max", [P, 2 * NH, NT])
        row_sum = sb("row_sum", [P, 2 * NH, NT])
        row_inv = sb("row_inv", [P, 2 * NH, NT])

        resid_flat = resid[:, :, :].rearrange("p t n -> p (t n)")
        work_flat = work[:, :, :].rearrange("p t n -> p (t n)")
        nat_q = nat[:, 0:NT * NH * QK].rearrange("p (t h c) -> p t h c", t=NT, h=NH)
        nat_k = nat[:, NT * NH * QK:].rearrange("p (t h c) -> p t h c", t=NT, h=NH)
        g_mix = nat[:, 0:D]
        x_rows = [work[:, 0, :], work[:, 1, :], nat[:, D:2 * D], nat[:, 2 * D:3 * D]]
        lat_acc = resid_flat[:, 2560:3584].rearrange("p (f n) -> p f n", f=2)
        lat_tmp = resid_flat[:, 3584:4096]
        g_memkv = resid_flat[:, 2560:3584]
        mem_rows = [resid_flat[:, m * P_COLS:m * P_COLS + D] for m in range(NM)]
        q_cos, q_sin = (work_flat[:, D + i * HALF:D + (i + 1) * HALF].rearrange(
            "p (t h c) -> p t h c", t=2, h=NH) for i in range(2))
        rf_t = resid_flat[0:RF, 0:SEQ]
        sq_acc = work_flat[:, 0:HALF]
        sq_tmp = work_flat[:, 2 * HALF:4 * HALF].rearrange("p (f n) -> p f n", f=2)
        h_rows = [work[:, 0, :], work[:, 1, :], nat[:, 0:D], nat[:, D:2 * D]]
        g_memq, g_ffn, g_final = (nat[:, 2048 + i * D:3072 + i * D] for i in range(3))
        gate_buf = nat[:, 4 * HALF:6 * HALF].rearrange("p (s n) -> p s n", s=2)
        rstd_rows = nat[:, 6 * HALF:7 * HALF]
        rstd_diag = nat[:, 7 * HALF:8 * HALF]
        silu_buf = nat[:, 0:2 * HALF].rearrange("p (s n) -> p s n", s=2)
        h_buf = nat[:, 2 * HALF:4 * HALF].rearrange("p (s n) -> p s n", s=2)

        def region(start, *dims):
            n = int(np.prod(dims))
            ap = arena[:, start:start + n]
            if len(dims) == 2:
                ap = ap.rearrange("p (a b) -> p a b", a=dims[0])
            return ap

        qt_hi, qt_lo, kt_hi, kt_lo = (region(i * 1024, 2, HALF) for i in range(4))
        pt_hi, pt_lo = region(4096, 2, P_COLS), region(6656, 2, P_COLS)
        ct_hi, ct_lo = region(9216, NC_LAT, HALF), region(11776, NC_LAT, HALF)
        vm_hi, vm_lo = xt_hi[:, 0:4, :], xt_lo[:, 0:4, :]
        vf_hi, vf_lo = region(14336, NT, HALF), region(16384, NT, HALF)
        of_hi, of_lo = region(18432, NT, HALF), region(20480, NT, HALF)
        om_hi, om_lo = vf_hi, vf_lo
        mt_hi, mt_lo = (x[:, 4:8, :].rearrange("p a (b n) -> p (a b) n", b=2) for x in (xt_hi, xt_lo))
        mem_junk = [region(6656 + m * D, 1, D)[:, 0, :] for m in range(NM)]
        mk_hi, mk_lo = region(9216, H_MEM, MEM), region(10240, H_MEM, MEM)
        mv_hi, mv_lo = region(11264, NM, HALF), region(12288, NM, HALF)
        square_junk = [region(4096 + t * D, 1, D)[:, 0, :] for t in range(NT)]
        mq_hi, mq_lo = region(0, H_MEM, HALF), region(2048, H_MEM, HALF)
        mp_hi, mp_lo = region(18432, 4, HALF), region(20480, 4, HALF)
        mo_hi, mo_lo = region(14336, H_MEM, HALF), region(16384, H_MEM, HALF)
        ht_hi, ht_lo = region(0, NF, HALF), region(NF * HALF, NF, HALF)

        bank = [ctx.enter_context(nc.psum_tensor(f"bank{i}", [P, HALF], F32)) for i in range(8)]

        bank_full = [sem(f"bank_full{i}") for i in range(8)]
        bank_hi = [sem(f"bank_hi{i}") for i in range(8)]
        bank_free = [sem(f"bank_free{i}") for i in range(8)]
        x_loaded = [sem(f"x_loaded{t}") for t in range(NT)]
        x_again = sem("x_again")
        consts_loaded = sem("consts_loaded")
        g_mix_loaded = sem("g_mix_loaded")
        mem_loaded = [sem(f"mem_loaded{m}") for m in range(NM)]
        g_memkv_loaded = sem("g_memkv_loaded")
        late_loaded = sem("late_loaded")
        w_loaded = [sem(f"w_loaded{i}") for i in range(RAW)]
        w_hi_done = sem("w_hi_done")
        w_lo_done = sem("w_lo_done")
        w_used = sem("w_used")
        consts_made = sem("consts_made")
        nat_cleared = sem("nat_cleared")
        ssq_ready = sem("ssq_ready")
        rstd_ready = sem("rstd_ready")
        xn_ready = sem("xn_ready")
        forget_z = sem("forget_z")
        forget_l = sem("forget_l")
        logf_ready = sem("logf_ready")
        nat_extra = sem("nat_extra")
        max_ready = sem("max_ready")
        inv_ready = sem("inv_ready")
        probs_ready = sem("probs_ready")
        sq_ready = sem("sq_ready")
        sq_added = sem("sq_added")
        lat_sq_ready = sem("lat_sq_ready")
        lat_sq_added = sem("lat_sq_added")
        q_scale_ready = sem("q_scale_ready")
        k_nat = sem("k_nat")
        qrope_nat = sem("qrope_nat")
        resid_done = sem("resid_done")
        diag_ready = sem("diag_ready")
        row_max_ready = sem("row_max_ready")
        gate_scaled = sem("gate_scaled")
        silu_done = sem("silu_done")
        h_done = sem("h_done")
        h_hi_done = sem("h_hi_done")
        h_lo_done = sem("h_lo_done")
        stored = sem("stored")
        act_chain = sem("act_chain")
        dve_chain = sem("dve_chain")
        pool_chain = sem("pool_chain")

        def rows(w):
            return w.rearrange("(k p) n -> p k n", p=P)

        slabs = []

        def slab(key, *pieces):
            slabs.append((key, pieces))

        w_in = rows(a["w_in"][0])
        for name, c in (("vf", C_VF), ("rf", C_ROPE), ("qf", C_QF), ("kf", C_KF)):
            if name == "rf":
                slab(("rf", 0), (KD, RF, 0, ROPE, w_in[:, :, C_ROPE:C_ROPE + ROPE]),
                     (KD, RF, ROPE, RF, w_in[:, :, C_F:C_F + NH]))
                continue
            for k in range(0, KD, 2):
                slab((name, k), (2, 512, 0, 512, w_in[:, k:k + 2, c:c + 512]))
        for c in range(NC_LAT):
            slab(("cT", c), (KD, 128, 0, 128, w_in[:, :, C_CQ + c * P:C_CQ + (c + 1) * P]))
        for k in range(CQ):
            slab(("uq", k), (1, 768, 0, 768, rows(a["w_uq"][0])[:, k:k + 1, :]))
        for k in range(CKV):
            slab(("ukv", k), (1, 1024, 0, 1024, rows(a["w_ukv"][0])[:, k:k + 1, :]))
        w_mkv = a["w_mkv"][0].rearrange("(k p) (h s n) -> p k h s n", p=P, h=H_MEM, s=2)
        for h in range(H_MEM):
            slab(("mk", h), (KD, 128, 0, 128, w_mkv[:, :, h, 0, :]))
        w_o = rows(a["w_out"][0])
        for stage in range(4):
            k0, n0 = (4 if stage < 2 else 0), HALF * (stage % 2)
            for k in range(k0, k0 + 4, 2):
                slab(("out", stage, k), (2, 512, 0, 512, w_o[:, k:k + 2, n0:n0 + HALF]))
        for k in range(0, KD, 2):
            slab(("mv", k), *[(8, 128, 0, 128, (kk, w_mkv[:, k + kk, :, 1, :])) for kk in (0, 1)])
        for h in range(H_MEM):
            slab(("mq", h), (KD, 128, 0, 128, rows(a["w_mq"][0])[:, :, h * P:(h + 1) * P]))
        for n in range(2):
            for k in range(0, H_MEM, 2):
                slab(("mo", n, k), (2, 512, 0, 512, rows(a["w_mo"][0])[:, k:k + 2, n * HALF:(n + 1) * HALF]))
        for f in range(NF):
            for name in ("gate", "up"):
                slab((name, f), (KD, 128, 0, 128, rows(a[f"w_{name}"][0])[:, :, f * P:(f + 1) * P]))
        for k in range(NF):
            slab(("down", k), (1, 1024, 0, 1024, rows(a["w_down"][0])[:, k:k + 1, :]))
        NS = len(slabs)
        loads_upto, seen = [], [0] * RAW
        for n, (_, pieces) in enumerate(slabs):
            seen[n % RAW] += 16 * len(pieces)
            loads_upto.append(seen[n % RAW])
        number = {key: n for n, (key, _) in enumerate(slabs)}

        ends = {}
        for name in ("vf", "qf", "kf"):
            ends[(name, KD - 2)] = (name, NT - 1)
        ends[("rf", 0)] = ("rf",)
        for c in range(NC_LAT):
            ends[("cT", c)] = ("cT", c)
        ends[("uq", CQ - 1)], ends[("ukv", CKV - 1)] = ("uq", NT - 1, 1), ("ukv", NT - 1, 1)
        for stage in range(4):
            ends[("out", stage, 6 if stage < 2 else 2)] = ("out", stage, NT - 1)
        for h in range(H_MEM):
            ends[("mk", h)], ends[("mq", h)] = ("mk", h), ("mq", h)
        ends[("mv", KD - 2)] = ("mv", NM - 1)
        for n in range(2):
            ends[("mo", n, H_MEM - 2)] = ("mo", n, NT - 1)
        for f in range(NF):
            ends[("gate", f)], ends[("up", f)] = ("gate", f), ("up", f)
        ends[("down", NF - 1)] = ("down", NT - 1, 1)
        released, count = [], 0
        for key, _ in slabs:
            if key in ends:
                b, turn, _ = use[ends[key]]
                released.append((bank_full[b], turn))
            else:
                count += 1
                released.append((w_used, count))

        def slab_cols(n):
            return slabs[n][1][0][0] * slabs[n][1][0][1]

        def split_of(key, k, c0, c1):
            n = number[key]
            width = slabs[n][1][0][1]
            s = slice(k * width + c0, k * width + c1)
            return w_hi[:, n % SPLIT, s], w_lo[:, n % SPLIT, s]

        N_X, N_CQ, N_CKV, N_OUT, N_MEM, N_H1, N_H2, N_H3 = 0, 4, 8, 12, 20, 22, 26, 30

        def ssq_step(col):
            return col + 1 if col < N_CQ else col - 15

        def norm_step(col):
            if col < N_CQ:
                return col + 1
            steps = {N_CQ: 5, N_CKV: 6, N_MEM: 7, N_MEM + 1: 7, N_OUT: 8, N_OUT + 4: 9}
            return steps[col] if col in steps else col - 12

        XN_X, XN_MEM, XN_H1, XN_H2, XN_H3 = 0, 4, 6, 14, 22

        def score_col(i):
            return 3 * P if i == 0 else 0

        def squares_added(g):
            return 3 * (g // NH) + (g % NH) // 2

        block = ctx.enter_context(nc.Block())

        @block.sync
        def _(sp):
            def load_slab(n):
                key, pieces = slabs[n]
                slot = n % RAW
                if n >= RAW:
                    sp.wait_ge(w_lo_done, n - RAW + 1)
                for kk, width, c0, c1, src in pieces:
                    dst = w_raw[:, slot, 0:kk * width].rearrange("p (k n) -> p k n", k=kk)[:, :, c0:c1]
                    if isinstance(src, tuple):
                        dst = dst[:, 4 * src[0]:4 * src[0] + 4, :]
                        src = src[1]
                    sp.dma_start(dst, src).then_inc(w_loaded[slot], 16)

            for t in range(NT):
                sp.dma_start(resid[:, t, :], a["x"][0, t * P:(t + 1) * P, :]).then_inc(x_loaded[t], 16)
                if t == 0:
                    sp.dma_start(g_mix, a["mix_norm_g"].partition_broadcast(P)[:, 0, :]).then_inc(g_mix_loaded, 16)
            for n in range(RAW):
                load_slab(n)
            sp.dma_start(fbias[:, :], a["forget_bias"].partition_broadcast(P)[:, 0, :]).then_inc(consts_loaded, 16)
            sp.dma_start(rope_tab[:, :, :, :], a["rope"].rearrange("s (t p) c -> p s t c", p=P)).then_inc(consts_loaded, 16)
            sp.dma_start(g_out[:, 0:4], a["fox_out_g"][0].rearrange("(c p) -> p c", p=P),
                         allow_slow_non_contiguous=True).then_inc(consts_loaded, 16)
            sp.dma_start(g_out[:, 4:8], a["mla_out_g"][0].rearrange("(c p) -> p c", p=P),
                         allow_slow_non_contiguous=True).then_inc(consts_loaded, 16)
            for g, name, n in ((g_lat[:, 0:CQ], "cq_norm_g", CQ), (g_lat[:, CQ:], "ckv_norm_g", CKV)):
                sp.dma_start(g, a[name][0].rearrange("(c p) -> p c", p=P),
                             allow_slow_non_contiguous=True).then_inc(consts_loaded, 16)

            for n in range(RAW, number[("ukv", 0)]):
                load_slab(n)
            b, turn, _ = use[("PT", NH - 1, 2)]
            sp.wait_ge(bank_full[b], turn)
            for m in range(NM):
                sp.dma_start(mem_rows[m], a["mem"][0, m * P:(m + 1) * P, :]).then_inc(mem_loaded[m], 16)
            b, turn, _ = use[("cssq",)]
            sp.wait_ge(bank_full[b], turn)
            sp.dma_start(g_memkv, a["mem_kv_norm_g"].partition_broadcast(P)[:, 0, :]).then_inc(g_memkv_loaded, 16)
            first_late = number[("out", 0, 4)] + RAW
            for n in range(number[("ukv", 0)], first_late):
                load_slab(n)
            b, n_turn, _ = use[("KT", 2 * NH - 1)]
            sp.wait_ge(bank_full[b], n_turn)
            for g, name in ((g_memq, "mem_q_norm_g"), (g_ffn, "ffn_norm_g")):
                sp.dma_start(g, a[name].partition_broadcast(P)[:, 0, :]).then_inc(late_loaded, 16)
            sp.dma_start(g_final, a["final_norm_g"].partition_broadcast(P)).then_inc(late_loaded, 16)
            b, n_turn, _ = use[("PT", 2 * NH - 1, 2)]
            sp.wait_ge(bank_full[b], n_turn)
            sp.dma_start(resid[:, :, :], a["x"][0].rearrange("(t p) n -> p t n", p=P)).then_inc(x_again, 16)
            for n in range(first_late, NS):
                load_slab(n)
            for t in range(NT):
                for half in range(2):
                    sp.wait_ge(xn_ready, XN_H3 + 2 * t + half + 1)
                    s = slice(half * HALF, (half + 1) * HALF)
                    sp.dma_start(out[0, t * P:(t + 1) * P, s], h_rows[t][:, s]).then_inc(stored, 16)
            sp.wait_ge(stored, 2 * 16 * NT)

        @block.gpsimd
        def _(pool):
            pool.memset(neg_half[:, :], -0.5).then_inc(pool_chain, 1)
            pool.memset(ones[:, :], 1.0).then_inc(pool_chain, 1)
            pool.memset(ident[:, :], 0.0).then_inc(pool_chain, 1)
            pool.memset(ident_bf[:, :], 0.0).then_inc(pool_chain, 1)
            pool.memset(mask_bf[:, :], 0.0).then_inc(pool_chain, 1)
            pool.wait_ge(pool_chain, 5)
            for m in (ident, ident_bf):
                pool.affine_select(out=m[:, :], in_=m[:, :], compare_op=ALU.not_equal, fill=1.0, base=0,
                                   pattern=[[-1, P]], channel_multiplier=1).then_inc(consts_made, 1)
            pool.affine_select(out=mask_bf[:, :], in_=mask_bf[:, :], compare_op=ALU.is_ge, fill=MASKED, base=0,
                               pattern=[[-1, P]], channel_multiplier=1).then_inc(consts_made, 1)
            pool.affine_select(out=upto[:, :], in_=ones[:, :], compare_op=ALU.is_ge, fill=0.0, base=0,
                               pattern=[[1, P]], channel_multiplier=-1).then_inc(consts_made, 1)
            chain = [5]

            def link(ins):
                chain[0] += 1
                ins.then_inc(pool_chain, 1)
                pool.wait_ge(pool_chain, chain[0])

            def make_rstd(col, width, dim):
                if N_CQ <= col < N_MEM:
                    b, n, _ = use[("cssq",) if col < N_OUT else ("ssq", (col - N_OUT) // 4)]
                    pool.wait_ge(bank_free[b], n)
                else:
                    pool.wait_ge(ssq_ready, ssq_step(col + width - 1))
                c = slice(col, col + width)
                link(pool.tensor_scalar(msq[:, c], ssq[:, c], 1.0 / dim, EPS, ALU.mult, ALU.add))
                pool.tensor_tensor(rstd[:, c], msq[:, c], neg_half[:, 0:width], ALU.pow).then_inc(rstd_ready, 1)

            for t in range(NT):
                make_rstd(N_X + t, 1, D)
            pool.wait_ge(xn_ready, XN_X + NT)
            for t in range(2, NT):
                b, turn, _ = use[("xT", t, 1)]
                pool.wait_ge(bank_full[b], turn)
            link(pool.memset(nat[:, :], 0.0))
            pool.memset(nat_q[:, :, :, HD + 1:HD + 2], 1.0).then_inc(nat_cleared, 1)
            pool.memset(nat_k[:, :, :, HD:HD + 1], 1.0).then_inc(nat_cleared, 1)

            def normalise(g, i):
                pool.wait_ge(inv_ready, 3 * g + {3: 1, 2: 2, 0: 2, 1: 3}[i])
                s = (g % 2) * P_COLS + P_OFF[i]
                p = resid_flat[:, s:s + P * (i + 1)]
                pool.tensor_scalar(p, p, row_inv[:, g, i:i + 1], None, ALU.mult).then_inc(probs_ready, 1)

            def add_squares(g):
                pair = (g % NH) // 2
                if g % 2 == 0 or pair == 0:
                    return
                pool.wait_ge(sq_ready, g + 1)
                n = squares_added(g)
                if n > 1:
                    pool.wait_ge(sq_added, n - 1)
                pool.tensor_tensor(sq_acc, sq_acc, sq_tmp[:, pair % 2, :], ALU.add).then_inc(sq_added, 1)

            def add_latent_squares(c):
                if c in (0, CQ):
                    return
                pool.wait_ge(lat_sq_ready, c + 1)
                if c > 1:
                    pool.wait_ge(lat_sq_added, 1)
                if c > CQ:
                    pool.wait_ge(lat_sq_added, 2)
                acc = lat_acc[:, 0 if c < CQ else 1, :]
                pool.tensor_tensor(acc, acc, lat_tmp, ALU.add).then_inc(lat_sq_added, 1)

            for fam in range(2):
                plan = fitted(fam)
                for g in range(fam * NH, (fam + 1) * NH):
                    for i in TILE_ORDER:
                        normalise(g, i)
                    if g == NH:
                        make_rstd(N_OUT, 4, HALF)
                    if g > fam * NH + 1:
                        add_squares(g - 2)
                    for slot in range(SLOTS):
                        name, quarter = plan.get((g % NH) * SLOTS + slot, (None, 0))
                        if fam == 0 and name and quarter == 3:
                            add_latent_squares(name[1])
                add_squares((fam + 1) * NH - 2)
                if fam == 0:
                    add_latent_squares(NC_LAT - 1)
                    make_rstd(N_CQ, 4, Q_LORA)
                    pool.wait_ge(rstd_ready, norm_step(N_CQ))
                    pool.tensor_scalar(q_scale[:, :], rstd[:, N_CQ:N_CQ + 4], -MLA_SCALE, None,
                                       ALU.mult).then_inc(q_scale_ready, 1)
                    make_rstd(N_CKV, 4, KV_LORA)
                add_squares((fam + 1) * NH - 1)
                if fam == 0:
                    make_rstd(N_MEM, NM, D)
                if fam == 1:
                    make_rstd(N_OUT + 4, 4, HALF)
            for base in (N_H1, N_H2, N_H3):
                for t in range(NT):
                    make_rstd(base + t, 1, D)

        @block.scalar
        def _(act):
            def full(key):
                b, n, _ = use[key]
                act.wait_ge(bank_full[b], n)
                return b

            def take_hi(key, dst, rows_=slice(0, P), cols=slice(0, HALF), scale=1.0, view=None):
                b = full(key)
                src = bank[b][rows_, cols]
                if view:
                    src = view(src)
                act.activation(dst, src, ACT.Copy, scale=scale).then_inc(bank_hi[b], 1)

            def summed(key):
                b, n, _ = use[key]
                act.wait_ge(bank_free[b], n)

            def split_slab(n):
                if n >= NS:
                    return
                cols = slab_cols(n)
                act.wait_ge(w_loaded[n % RAW], loads_upto[n])
                if n >= SPLIT:
                    act.wait_ge(*released[n - SPLIT])
                act.activation(w_hi[:, n % SPLIT, 0:cols], w_raw[:, n % RAW, 0:cols], ACT.Copy).then_inc(w_hi_done, 1)

            def square_rows(src, junk, col):
                act.activation(junk, src, ACT.Square, accum_out=ssq[:, col:col + 1]).then_inc(ssq_ready, 1)

            def take_transposed(name, t, half, hi):
                for half in (half,) if half is not None else range(2):
                    take_hi((name, t, half), hi[:, 4 * half:4 * half + 4, t * P:(t + 1) * P],
                            view=lambda s: s.rearrange("p (c n) -> p c n", c=4))

            def eat(key):
                if number[key] >= 1:
                    split_slab(number[key] + 1)

            for t in range(NT):
                act.wait_ge(x_loaded[t], 16)
                square_rows(resid[:, t, :], x_rows[t], N_X + t)
                if t >= 1:
                    take_transposed("xT", t - 1, None, xt_hi)
                if t == 2:
                    split_slab(0)
            split_slab(1)
            take_transposed("xT", NT - 1, None, xt_hi)
            for k in range(0, KD, 2):
                eat(("vf", k))
            for t in range(NT):
                take_hi(("vf", t), vf_hi[:, t, :])
            eat(("rf", 0))
            b = full(("rf",))
            act.activation(rf_t, bank[b][0:RF, :], ACT.Copy).then_inc(bank_free[b], 1)
            eat(("qf", 0))
            b = full(("rft",))
            act.activation(krf[:, :, :], bank[b][:, 0:NT * RF].rearrange("p (t n) -> p t n", t=NT),
                           ACT.Copy).then_inc(bank_free[b], 1)
            act.wait_ge(forget_z, 1)
            act.activation(fe[:, :, :], fa[:, :, :], ACT.Exp, scale=-1.0).then_inc(act_chain, 1)
            act.wait_ge(act_chain, 1)
            act.activation(fl[:, :, :], fe[:, :, :], ACT.Ln, bias=1.0).then_inc(forget_l, 1)
            for k in range(2, KD, 2):
                eat(("qf", k))
            act.wait_ge(nat_cleared, 2)
            for t in range(NT):
                b = full(("qf", t))
                act.activation(nat_q[:, t, :, 0:HD], bank[b][:, :].rearrange("p (h c) -> p h c", h=NH), ACT.Copy,
                               scale=-FOX_SCALE).then_inc(bank_free[b], 1)
            for k in range(0, KD, 2):
                eat(("kf", k))
            for t in range(NT):
                b = full(("kf", t))
                act.activation(nat_k[:, t, :, 0:HD], bank[b][:, :].rearrange("p (h c) -> p h c", h=NH),
                               ACT.Copy).then_inc(bank_free[b], 1)

            def exp_scores(g, i):
                b, n, _ = use[("S", g, i)]
                act.wait_ge(max_ready, 4 * g + {3: 1, 2: 3, 0: 3, 1: 4}[i])
                s = (g % 2) * P_COLS + P_OFF[i]
                w, c = P * (i + 1), score_col(i)
                ins = act.activation(resid_flat[:, s:s + w], bank[b][:, c:c + w], ACT.Exp, scale=-1.0,
                                     bias=neg_max[:, g, i:i + 1], accum_out=row_sum[:, g, i:i + 1])
                if i != 2:
                    ins.then_inc(bank_free[b], 1)

            def pt_hi_half(g, part):
                lo, hi = ((0, 512), (512, 1024), (1024, 1280))[part]
                take_hi(("PT", g, part), pt_hi[:, g % 2, lo:hi], cols=slice(0, hi - lo))

            def take_ssq(fam):
                b = full(("ssq", fam))
                act.activation(ssq[:, N_OUT + 4 * fam:N_OUT + 4 * fam + 4], bank[b][:, 0:4],
                               ACT.Copy).then_inc(bank_free[b], 1)

            def attention(first, last, o_hi):
                def qk_hi(g):
                    take_hi(("QT", g), qt_hi[0:QK, g % 2, :], rows_=slice(0, QK))
                    take_hi(("KT", g), kt_hi[0:QK, g % 2, :], rows_=slice(0, QK))

                def head_out(g):
                    r = slice(HD * (g % 2), HD * (g % 2) + HD)
                    pair = (g % NH) // 2
                    b, n, m = use[("PV", g)]
                    act.wait_ge(bank_full[b], n)
                    if pair == 3 and g % 2 == 0:
                        act.wait_ge(sq_added, squares_added(g - 4))
                    sq = sq_acc[r, :] if pair == 0 else sq_tmp[r, pair % 2, :]
                    act.activation(sq, bank[b][r, :], ACT.Square).then_inc(sq_ready, 1)
                    act.activation(o_hi[r, pair, :], bank[b][r, :], ACT.Copy,
                                   scale=g_out[r, g // 2:g // 2 + 1]).then_inc(bank_hi[b], 1)

                plan = fitted(first // NH)

                def fit(g, slot):
                    n = (g - first) * SLOTS + slot
                    name, quarter = plan.get(n, (None, 0))
                    if name:
                        fit_product(name, quarter)

                def fit_product(name, quarter):
                    if quarter == 3:
                        b = full(name)
                        if name[0] == "mk":
                            take_hi(name, mk_hi[:, name[1], :], cols=slice(0, MEM))
                            return
                        c = name[1]
                        fam = 0 if c < CQ else 1
                        if c in (2, CQ + 1):
                            act.wait_ge(lat_sq_added, 1 if c == 2 else 2)
                        act.activation(lat_acc[:, fam, :] if c in (0, CQ) else lat_tmp, bank[b][:, :],
                                       ACT.Square).then_inc(lat_sq_ready, 1)
                        take_hi(name, ct_hi[:, c, :], scale=g_lat[:, c:c + 1])

                if first == 0:
                    eat(("cT", 0))
                qk_hi(first)
                fit(first, -2)
                fit(first, -1)
                if first:
                    for m in range(NM):
                        take_transposed("memT", m, None, mt_hi)
                    eat(("ukv", 1))
                for g in range(first, last + 1):
                    for i in (3, 2, 0):
                        exp_scores(g, i)
                    if g == NH:
                        take_ssq(0)
                    fit(g, 0)
                    if g < last:
                        qk_hi(g + 1)
                    if g > first + 1:
                        head_out(g - 2)
                    if g > first:
                        pt_hi_half(g - 1, 0)
                    exp_scores(g, 1)
                    fit(g, 1)
                    if g > first:
                        pt_hi_half(g - 1, 1)
                        pt_hi_half(g - 1, 2)
                    fit(g, 2)
                    for slot in range(SLOTS):
                        name, quarter = plan.get((g - first) * SLOTS + slot, (None, 0))
                        if name and quarter == 0:
                            eat(name)
                extra = ("cT", NC_LAT - 1) if first == 0 else ("mk", H_MEM - 1)
                eat(extra)
                fit_product(extra, 3)
                head_out(last - 1)
                if first:
                    eat(("out", 0, 4))
                for part in range(3):
                    pt_hi_half(last, part)
                if first:
                    eat(("out", 0, 6))
                head_out(last)

            act.wait_ge(consts_loaded, 96)
            attention(0, NH - 1, of_hi)
            eat(("uq", 0))
            b = full(("cssq",))
            act.activation(ssq[:, N_CQ:N_CQ + 8], bank[b][:, 0:8], ACT.Copy).then_inc(bank_free[b], 1)
            eat(("uq", 1))
            for m in range(NM):
                act.wait_ge(mem_loaded[m], 16)
                square_rows(mem_rows[m], mem_junk[m], N_MEM + m)
            eat(("uq", 2))
            act.wait_ge(q_scale_ready, 1)
            for t in range(NT):
                for n in range(2):
                    b = full(("uq", t, n))
                    act.activation(nat_q[:, t, 4 * n:4 * n + 4, :],
                                   bank[b][:, 0:384].rearrange("p (h c) -> p h c", h=4), ACT.Copy,
                                   scale=q_scale[:, t:t + 1]).then_inc(bank_free[b], 1)
            eat(("ukv", 0))
            act.wait_ge(rstd_ready, norm_step(N_CKV))
            for t in range(NT):
                for n in range(2):
                    b = full(("ukv", t, n))
                    kv = bank[b][:, :].rearrange("p (h s c) -> p h s c", h=4, s=2)
                    kv_scale = rstd[:, N_CKV + t:N_CKV + t + 1]
                    act.activation(nat_k[:, t, 4 * n:4 * n + 4, 0:HD], kv[:, :, 0, :], ACT.Copy,
                                   scale=kv_scale).then_inc(k_nat, 1)
                    act.activation(vm_hi[:, t, 256 * n:256 * n + 256].rearrange("p (h c) -> p h c", h=4),
                                   kv[:, :, 1, :], ACT.Copy, scale=kv_scale).then_inc(bank_hi[b], 1)
            attention(NH, 2 * NH - 1, om_hi)
            for stage in range(1, 4):
                if stage == 2:
                    take_ssq(1)
                for k in (4, 6) if stage < 2 else (0, 2):
                    eat(("out", stage, k))
                    if (stage, k) == (3, 0):
                        for t in range(NT):
                            take_transposed("h1T", t, 0, xt_hi)
            for k in range(0, KD, 2):
                eat(("mv", k))
            for m in range(NM):
                take_hi(("mv", m), mv_hi[:, m, :])
            for t in range(NT):
                take_transposed("h1T", t, 1, xt_hi)
            for step in MEM_STEPS:
                kind, h = step[0], step[1]
                if kind == "mq":
                    eat(step)
                    if h == 0:
                        for t in range(NT):
                            square_rows(resid[:, t, :], square_junk[t], N_H1 + t)
                    take_hi(step, mq_hi[:, h, :], scale=MEM_SCALE)
                elif kind == "MS":
                    for u in range(2):
                        b = use[("MS", h, u)][0]
                        act.wait_ge(max_ready, 2 * NH * NT + 2 * h + u + 1)
                        for i in range(2):
                            t = 2 * u + i
                            p = work_flat[:, (h % 2) * D + t * MEM:(h % 2) * D + (t + 1) * MEM]
                            ins = act.activation(p, bank[b][:, i * MEM:(i + 1) * MEM], ACT.Exp,
                                                 scale=rstd[:, N_H1 + t:N_H1 + t + 1],
                                                 bias=neg_max[:, h, t:t + 1], accum_out=row_sum[:, h, t:t + 1])
                            if i:
                                ins.then_inc(bank_free[b], 1)
                elif kind == "MPT":
                    for j in range(NM):
                        take_hi(("MPT", h, j), mp_hi[:, 2 * (h % 2) + j, :])
                elif kind == "MPV":
                    take_hi(step, mo_hi[:, h, :])
                elif kind == "mo":
                    if step[3] == (NT - 1 if step[1:3] == (1, 2) else 0):
                        eat(("mo", h, step[2]))
                elif kind == "h2T":
                    take_transposed("h2T", step[2], h, xt_hi)
                    if step[1:] == (1, 1):
                        eat(("gate", 0))
                else:
                    summed(("mo", 1, h))
                    square_rows(resid[:, h, :], square_junk[h], N_H2 + h)
            eat(("up", 0))
            b = full(("rstd rows",))
            act.activation(rstd_rows, bank[b][:, :], ACT.Copy).then_inc(bank_free[b], 1)

            def act_ffn(f):
                act.wait_ge(gate_scaled, f + 1)
                if f >= 2:
                    act.wait_ge(h_done, f - 1)
                act.activation(silu_buf[:, f % 2, :], gate_buf[:, f % 2, :], ACT.Silu).then_inc(silu_done, 1)
                act.wait_ge(h_done, f + 1)
                act.activation(ht_hi[:, f, :], h_buf[:, f % 2, :], ACT.Copy).then_inc(h_hi_done, 1)

            for f in range(NF):
                if f >= 1:
                    eat(("gate", f))
                    eat(("up", f))
                if f >= 1:
                    act_ffn(f - 1)
            eat(("down", 0))
            act_ffn(NF - 1)
            for k in range(1, NF):
                eat(("down", k))
            for t in range(NT):
                act.wait_ge(resid_done, t + 1)
                square_rows(resid[:, t, :], h_rows[t], N_H3 + t)

        @block.vector
        def _(dve):
            chain = [0]

            def link(ins):
                chain[0] += 1
                ins.then_inc(dve_chain, 1)
                dve.wait_ge(dve_chain, chain[0])

            def take_lo(key, dst, hi, rows_=slice(0, P), cols=slice(0, HALF), scale=None, view=None):
                b, _, m = use[key]
                dve.wait_ge(bank_hi[b], m)
                src = bank[b][rows_, cols]
                if view:
                    src = view(src)
                if scale is None:
                    dve.tensor_tensor(dst, src, hi.bitcast(F32), ALU.subtract).then_inc(bank_free[b], 1)
                else:
                    dve.scalar_tensor_tensor(dst, src, scale, hi.bitcast(F32), ALU.mult,
                                             ALU.subtract).then_inc(bank_free[b], 1)

            def split_slab(n):
                if n >= NS:
                    return
                cols = slab_cols(n)
                dve.wait_ge(w_hi_done, n + 1)
                dve.tensor_tensor(w_lo[:, n % SPLIT, 0:cols], w_raw[:, n % RAW, 0:cols],
                                  w_hi[:, n % SPLIT, 0:cols].bitcast(F32), ALU.subtract).then_inc(w_lo_done, 1)

            def eat(key):
                if number[key] >= 1:
                    split_slab(number[key] + 1)

            def norm_rows(dst, src, col, gain):
                dve.wait_ge(rstd_ready, norm_step(col))
                return dve.scalar_tensor_tensor(dst, src, rstd[:, col:col + 1], gain, ALU.mult, ALU.mult)

            def take_transposed(name, t, half, hi, lo):
                for half in (half,) if half is not None else range(2):
                    s = (slice(None), slice(4 * half, 4 * half + 4), slice(t * P, (t + 1) * P))
                    take_lo((name, t, half), lo[s], hi[s], view=lambda x: x.rearrange("p (c n) -> p c n", c=4))

            dve.wait_ge(g_mix_loaded, 16)
            for t in range(NT):
                norm_rows(x_rows[t], resid[:, t, :], N_X + t, g_mix).then_inc(xn_ready, 1)
                if t >= 1:
                    take_transposed("xT", t - 1, None, xt_hi, xt_lo)
                if t == 2:
                    split_slab(0)
            take_transposed("xT", NT - 1, None, xt_hi, xt_lo)
            split_slab(1)
            for k in range(0, KD, 2):
                eat(("vf", k))
            for t in range(NT):
                take_lo(("vf", t), vf_lo[:, t, :], vf_hi[:, t, :])
            eat(("rf", 0))
            eat(("qf", 0))
            dve.wait_ge(consts_loaded, 96)
            b, n, _ = use[("rft",)]
            dve.wait_ge(bank_free[b], n)
            link(dve.tensor_tensor(fz[:, :, :], krf[:, :, ROPE:], fbias[:, :].unsqueeze(1).to_broadcast([P, NT, NH]), ALU.add))
            dve.scalar_tensor_tensor(fa[:, :, :], fz[:, :, :], -1.0, fz[:, :, :], ALU.mult,
                                     ALU.max).then_inc(forget_z, 1)
            x1, x2 = krf[:, :, 0:16], krf[:, :, 16:32]
            cos, sin = rope_tab[:, 0, :, 0:16], rope_tab[:, 1, :, 0:16]
            ra, rb = rope_a[:, :, :], rope_b[:, :, :]
            link(dve.tensor_tensor(ra[:, :, 0:16], x1, cos, ALU.mult))
            link(dve.tensor_tensor(ra[:, :, 16:32], x2, cos, ALU.mult))
            link(dve.tensor_tensor(rb[:, :, 0:16], x2, sin, ALU.mult))
            link(dve.tensor_tensor(rb[:, :, 16:32], x1, sin, ALU.mult))
            link(dve.tensor_tensor(kro[:, :, 0:16], ra[:, :, 0:16], rb[:, :, 0:16], ALU.subtract))
            link(dve.tensor_tensor(kro[:, :, 16:32], ra[:, :, 16:32], rb[:, :, 16:32], ALU.add))
            dve.wait_ge(forget_l, 1)
            dve.scalar_tensor_tensor(logf[:, :, :], fz[:, :, :], 0.0, fl[:, :, :], ALU.min,
                                     ALU.subtract).then_inc(logf_ready, 1)
            for k in range(2, KD, 2):
                eat(("qf", k))
            b, n, _ = use[("cum",)]
            dve.wait_ge(bank_full[b], n)
            dve.wait_ge(nat_cleared, 2)
            cum = bank[b][:, 0:NT * NH].rearrange("p (t h) -> p t h", t=NT)
            dve.tensor_scalar(nat_q[:, :, :, HD], cum, -1.0, None, ALU.mult).then_inc(nat_extra, 1)
            dve.tensor_copy(nat_k[:, :, :, HD + 1], cum).then_inc(bank_free[b], 1)
            for k in range(0, KD, 2):
                eat(("kf", k))

            def negated_max(g, i):
                b, n, _ = use[("S", g, i)]
                dve.wait_ge(bank_full[b], n)
                c = score_col(i)
                dve.tensor_reduce(neg_max[:, g, i:i + 1], bank[b][:, c:c + P * (i + 1)], AX.X,
                                  ALU.min).then_inc(max_ready, 1)

            def invert(g, i):
                b, n, _ = use[("S", g, i)]
                dve.wait_ge(bank_free[b], n)
                c = slice(0, 3, 2) if i == 2 else slice(i, i + 1)
                dve.reciprocal(row_inv[:, g, c], row_sum[:, g, c]).then_inc(inv_ready, 1)

            def pt_lo_half(g, part):
                lo, hi = ((0, 512), (512, 1024), (1024, 1280))[part]
                take_lo(("PT", g, part), pt_lo[:, g % 2, lo:hi], pt_hi[:, g % 2, lo:hi], cols=slice(0, hi - lo))

            def attention(first, last, o_hi, o_lo):
                def qk_lo(g):
                    r = slice(0, QK)
                    take_lo(("QT", g), qt_lo[r, g % 2, :], qt_hi[r, g % 2, :], rows_=r)
                    take_lo(("KT", g), kt_lo[r, g % 2, :], kt_hi[r, g % 2, :], rows_=r)

                def head_out(g):
                    r = slice(HD * (g % 2), HD * (g % 2) + HD)
                    c = (g % NH) // 2
                    take_lo(("PV", g), o_lo[r, c, :], o_hi[r, c, :], rows_=r, scale=g_out[r, g // 2:g // 2 + 1])

                plan = fitted(first // NH)

                def fit(g, slot):
                    n = (g - first) * SLOTS + slot
                    name, quarter = plan.get(n, (None, 0))
                    if name:
                        fit_product(name, quarter)

                def fit_product(name, quarter):
                    if quarter == 3:
                        c = name[1]
                        if name[0] == "mk":
                            take_lo(name, mk_lo[:, c, :], mk_hi[:, c, :], cols=slice(0, MEM))
                        else:
                            take_lo(name, ct_lo[:, c, :], ct_hi[:, c, :], scale=g_lat[:, c:c + 1])

                if first == 0:
                    eat(("cT", 0))
                qk_lo(first)
                fit(first, -2)
                fit(first, -1)
                if first:
                    take_transposed("memT", 0, None, mt_hi, mt_lo)
                for g in range(first, last + 1):
                    negated_max(g, 3)
                    negated_max(g, 2)
                    negated_max(g, 0)
                    if g == NH:
                        take_transposed("memT", 1, None, mt_hi, mt_lo)
                        eat(("ukv", 1))
                    invert(g, 3)
                    invert(g, 2)
                    fit(g, 0)
                    if g < last:
                        qk_lo(g + 1)
                    if g > first + 1:
                        head_out(g - 2)
                    negated_max(g, 1)
                    if g > first:
                        pt_lo_half(g - 1, 0)
                    invert(g, 1)
                    fit(g, 1)
                    if g > first:
                        pt_lo_half(g - 1, 1)
                        pt_lo_half(g - 1, 2)
                    fit(g, 2)
                    for slot in range(SLOTS):
                        name, quarter = plan.get((g - first) * SLOTS + slot, (None, 0))
                        if name and quarter == 0:
                            eat(name)
                extra = ("cT", NC_LAT - 1) if first == 0 else ("mk", H_MEM - 1)
                eat(extra)
                fit_product(extra, 3)
                head_out(last - 1)
                if first:
                    eat(("out", 0, 4))
                for part in range(3):
                    pt_lo_half(last, part)
                if first:
                    eat(("out", 0, 6))
                head_out(last)

            attention(0, NH - 1, of_hi, of_lo)
            b, n, _ = use[("KT", NH - 1)]
            dve.wait_ge(bank_full[b], n)
            dve.tensor_copy(nat_k[:, :, :, HD:QK],
                            kro[:, :, :].unsqueeze(2).to_broadcast([P, NT, NH, ROPE])).then_inc(nat_extra, 1)
            for k in range(2):
                eat(("uq", k))
            dve.wait_ge(g_memkv_loaded, 16)
            for m in range(NM):
                norm_rows(mem_rows[m], mem_rows[m], N_MEM + m, g_memkv).then_inc(xn_ready, 1)
            eat(("uq", 2))
            for ts in (slice(0, 2), slice(2, 4)):
                if ts.start:
                    dve.wait_ge(qrope_nat, 1)
                for n in range(2):
                    b, turn, _ = use[("uq", ts.stop - 1, n)]
                    dve.wait_ge(bank_free[b], turn)
                q_rope = nat_q[:, ts, :, HD:QK]
                cos_part, sin_part = q_cos, q_sin
                for dst, which in ((cos_part, 0), (sin_part, 1)):
                    table = rope_tab[:, which, ts, :].unsqueeze(2).to_broadcast([P, 2, NH, ROPE])
                    link(dve.tensor_tensor(dst, q_rope, table, ALU.mult))
                link(dve.tensor_tensor(q_rope[:, :, :, 0:16], cos_part[:, :, :, 0:16], sin_part[:, :, :, 16:32],
                                       ALU.subtract))
                dve.tensor_tensor(q_rope[:, :, :, 16:32], cos_part[:, :, :, 16:32], sin_part[:, :, :, 0:16],
                                  ALU.add).then_inc(qrope_nat, 1)
                if ts.start == 0:
                    eat(("ukv", 0))
            for t in range(NT):
                for n in range(2):
                    s = slice(256 * n, 256 * n + 256)
                    take_lo(("ukv", t, n), vm_lo[:, t, s].rearrange("p (h c) -> p h c", h=4),
                            vm_hi[:, t, s].rearrange("p (h c) -> p h c", h=4),
                            scale=rstd[:, N_CKV + t:N_CKV + t + 1],
                            view=lambda x: x.rearrange("p (h s c) -> p h s c", h=4, s=2)[:, :, 1, :])
            attention(NH, 2 * NH - 1, om_hi, om_lo)

            def gain_rows(summed, t, half, gain):
                b, turn, _ = use[summed]
                dve.wait_ge(bank_free[b], turn)
                s = slice(half * HALF, (half + 1) * HALF)
                dve.tensor_tensor(h_rows[t][:, s], resid[:, t, s], gain[:, s], ALU.mult).then_inc(xn_ready, 1)

            dve.wait_ge(x_again, 16)
            dve.wait_ge(late_loaded, 48)
            for stage in range(4):
                if stage:
                    for k in (4, 6) if stage < 2 else (0, 2):
                        eat(("out", stage, k))
                        if (stage, k) == (3, 0):
                            for t in range(NT):
                                take_transposed("h1T", t, 0, xt_hi, xt_lo)
                fam, s = stage // 2, slice(HALF * (stage % 2), HALF * (stage % 2) + HALF)
                dve.wait_ge(rstd_ready, norm_step(N_OUT + 4 * fam))
                for t in range(NT):
                    b, n, _ = use[("out", stage, t)]
                    if stage >= 2:
                        before, turn, _ = use[("out", stage - 2, t)]
                        dve.wait_ge(bank_free[before], turn)
                    if (stage, t) == (3, NT - 1):
                        eat(("mv", 0))
                    dve.wait_ge(bank_full[b], n)
                    dve.scalar_tensor_tensor(resid[:, t, s], bank[b][:, :],
                                             rstd[:, N_OUT + 4 * fam + t:N_OUT + 4 * fam + t + 1], resid[:, t, s],
                                             ALU.mult, ALU.add).then_inc(bank_free[b], 1)
                    if stage >= 2:
                        gain_rows(("out", stage, t), t, stage - 2, g_memq)
            for k in range(2, KD, 2):
                eat(("mv", k))
            for m in range(NM):
                take_lo(("mv", m), mv_lo[:, m, :], mv_hi[:, m, :])
            for t in range(NT):
                take_transposed("h1T", t, 1, xt_hi, xt_lo)
            for step in MEM_STEPS:
                kind, h = step[0], step[1]
                if kind == "mq":
                    eat(step)
                    take_lo(step, mq_lo[:, h, :], mq_hi[:, h, :], scale=MEM_SCALE)
                elif kind == "MS":
                    for u in range(2):
                        b, n, _ = use[("MS", h, u)]
                        dve.wait_ge(bank_full[b], n)
                        c = slice(2 * u, 2 * u + 2)
                        dve.tensor_reduce(row_max[:, h, c], bank[b][:, :].rearrange("p (i k) -> p i k", i=2), AX.X,
                                          ALU.max).then_inc(row_max_ready, 1)
                        if h == 0 and u == 0:
                            dve.wait_ge(rstd_ready, norm_step(N_H1 + NT - 1))
                        dve.wait_ge(row_max_ready, 2 * h + u + 1)
                        dve.scalar_tensor_tensor(neg_max[:, h, c], row_max[:, h, c], -1.0,
                                                 rstd[:, N_H1 + 2 * u:N_H1 + 2 * u + 2], ALU.mult,
                                                 ALU.mult).then_inc(max_ready, 1)
                    for u in range(2):
                        b, n, _ = use[("MS", h, u)]
                        dve.wait_ge(bank_free[b], n)
                        link(dve.reciprocal(row_inv[:, h, 2 * u:2 * u + 2], row_sum[:, h, 2 * u:2 * u + 2]))
                        for t in range(2 * u, 2 * u + 2):
                            p = work_flat[:, (h % 2) * D + t * MEM:(h % 2) * D + (t + 1) * MEM]
                            dve.tensor_scalar(p, p, row_inv[:, h, t:t + 1], None, ALU.mult).then_inc(inv_ready, 1)
                elif kind == "MPT":
                    for j in range(NM):
                        take_lo(("MPT", h, j), mp_lo[:, 2 * (h % 2) + j, :], mp_hi[:, 2 * (h % 2) + j, :])
                elif kind == "MPV":
                    take_lo(step, mo_lo[:, h, :], mo_hi[:, h, :])
                elif kind == "mo":
                    n, k, t = step[1:]
                    late = (n, k) == (1, 2)
                    if t == 0 and not late:
                        eat(("mo", n, k))
                    if t == NT - 1 and late:
                        eat(("mo", n, k))
                    if k == 2:
                        b, turn, _ = use[("mo", n, t)]
                        dve.wait_ge(bank_full[b], turn)
                        s = slice(n * HALF, (n + 1) * HALF)
                        dve.tensor_tensor(resid[:, t, s], bank[b][:, :], resid[:, t, s],
                                          ALU.add).then_inc(bank_free[b], 1)
                        gain_rows(("mo", n, t), t, n, g_ffn)
                elif kind == "h2T":
                    take_transposed("h2T", step[2], h, xt_hi, xt_lo)
                    if step[1:] == (1, 1):
                        eat(("gate", 0))
            dve.wait_ge(xn_ready, XN_H2 + 2 * NT)
            for t in range(NT):
                dve.wait_ge(rstd_ready, norm_step(N_H2 + t))
                dve.tensor_scalar(rstd_diag[:, t * P:(t + 1) * P], ident[:, :], rstd[:, N_H2 + t:N_H2 + t + 1], None,
                                  ALU.mult).then_inc(diag_ready, 1)
            eat(("up", 0))

            def dve_ffn(f):
                bg, turn, _ = use[("gate", f)]
                dve.wait_ge(bank_full[bg], turn)
                if f == 0:
                    br, turn, _ = use[("rstd rows",)]
                    dve.wait_ge(bank_free[br], turn)
                if f >= 2:
                    dve.wait_ge(silu_done, f - 1)
                dve.tensor_tensor(gate_buf[:, f % 2, :], bank[bg][:, :], rstd_rows, ALU.mult).then_inc(gate_scaled, 1)
                b, n, _ = use[("up", f)]
                dve.wait_ge(bank_full[b], n)
                dve.wait_ge(silu_done, f + 1)
                if f >= 2:
                    dve.wait_ge(h_lo_done, f - 1)
                    dve.wait_ge(h_hi_done, f - 1)
                dve.tensor_tensor(h_buf[:, f % 2, :], bank[b][:, :], silu_buf[:, f % 2, :], ALU.mult).then_inc(h_done, 1)
                dve.wait_ge(h_hi_done, f + 1)
                dve.tensor_tensor(ht_lo[:, f, :], h_buf[:, f % 2, :], ht_hi[:, f, :].bitcast(F32),
                                  ALU.subtract).then_inc(h_lo_done, 1)

            for f in range(NF):
                if f >= 1:
                    eat(("gate", f))
                    eat(("up", f))
                if f >= 1:
                    dve_ffn(f - 1)
            eat(("down", 0))
            dve_ffn(NF - 1)
            for k in range(1, NF):
                eat(("down", k))

            def final_norm(t):
                for half in range(2):
                    s = slice(half * HALF, (half + 1) * HALF)
                    norm_rows(h_rows[t][:, s], resid[:, t, s], N_H3 + t, g_final[:, s]).then_inc(xn_ready, 1)

            for t in range(NT):
                for n in range(2):
                    b, turn, _ = use[("down", t, n)]
                    dve.wait_ge(bank_full[b], turn)
                    s = slice(n * HALF, (n + 1) * HALF)
                    ins = dve.scalar_tensor_tensor(resid[:, t, s], bank[b][:, :], rstd[:, N_H2 + t:N_H2 + t + 1],
                                                   resid[:, t, s], ALU.mult, ALU.add)
                    if n == 1:
                        ins.then_inc(resid_done, 1)
                    else:
                        ins.then_inc(dve_chain, 1)
                        chain[0] += 1
                if t >= 1:
                    final_norm(t - 1)
            final_norm(NT - 1)

        @block.tensor
        def _(pe):
            def claim(key):
                b, n, _ = use[key]
                if n > 1:
                    pe.wait_ge(bank_free[b], n - 1)
                return b

            def ready(key):
                b, n, _ = use[key]
                pe.wait_ge(bank_free[b], n)

            def product(dst, a_hi, a_lo, b_hi, b_lo, first, last):
                pe.matmul(dst, a_hi, b_hi, start=first, stop=False, skip_group_check=True)
                pe.matmul(dst, a_hi, b_lo, start=False, stop=False, skip_group_check=True)
                return pe.matmul(dst, a_lo, b_hi, start=False, stop=last, skip_group_check=True)

            def slab_ready(key):
                pe.wait_ge(w_lo_done, number[key] + 1)

            def transpose_rows(name, t, src):
                for half in range(2):
                    b = claim((name, t, half))
                    for c in range(4):
                        mm = pe.transpose(bank[b][:, c * P:(c + 1) * P],
                                          src[:, (4 * half + c) * P:(4 * half + c + 1) * P], ident[:, :])
                    mm.then_inc(bank_full[b], 1)

            def tokens_times_weights(keys, out_key, lhs_hi, lhs_lo, cols, chunks, halves=1, tile_ready=None,
                                     after_first=None):
                per = slabs[number[keys[0]]][1][0][0]
                for s, key in enumerate(keys):
                    slab_ready(key)
                    for t in range(NT):
                        if s == 0 and tile_ready:
                            tile_ready(t)
                        for n in range(halves):
                            okey = out_key(t, n)
                            b = claim(okey) if s == 0 else use[okey][0]
                            for k in range(per):
                                c = chunks[s * per + k]
                                ts = slice(t * P, (t + 1) * P)
                                wh, wl = split_of(key, k, n * cols, (n + 1) * cols)
                                mm = product(bank[b][:, 0:cols], lhs_hi[:, c, ts], lhs_lo[:, c, ts], wh, wl,
                                             s == 0 and k == 0, s == len(keys) - 1 and k == per - 1)
                            if s == len(keys) - 1:
                                mm.then_inc(bank_full[b], 1)
                            elif t == NT - 1 and n == halves - 1:
                                mm.then_inc(w_used, 1)
                    if s == 0 and after_first:
                        after_first()

            def in_projection(name, tile_ready=None, after_first=None):
                tokens_times_weights([(name, k) for k in range(0, KD, 2)], lambda t, n: (name, t), xt_hi, xt_lo,
                                     HALF, list(range(KD)), tile_ready=tile_ready, after_first=after_first)

            def transposed_ready(name, t):
                ready((name, t, 0))
                ready((name, t, 1))

            pe.wait_ge(consts_made, 4)

            def transpose_x(t):
                pe.wait_ge(xn_ready, XN_X + t + 1)
                transpose_rows("xT", t, x_rows[t])

            def x_ready(t):
                if t == 1:
                    transpose_x(NT - 1)
                transposed_ready("xT", t)

            for t in range(NT - 1):
                transpose_x(t)
            in_projection("vf", x_ready)
            slab_ready(("rf", 0))
            b = claim(("rf",))
            for k in range(KD):
                wh, wl = split_of(("rf", 0), k, 0, RF)
                mm = product(bank[b][0:RF, :], wh, wl, xt_hi[:, k, :], xt_lo[:, k, :], k == 0, k == KD - 1)
            mm.then_inc(bank_full[b], 1)

            def rf_transposes():
                ready(("rf",))
                b = claim(("rft",))
                for t in range(NT):
                    mm = pe.transpose(bank[b][:, RF * t:RF * (t + 1)], rf_t[:, t * P:(t + 1) * P], ident[0:RF, 0:RF])
                mm.then_inc(bank_full[b], 1)

            in_projection("qf", after_first=rf_transposes)
            b = claim(("cum",))
            pe.wait_ge(logf_ready, 1)
            for t in range(NT):
                for u in range(t + 1):
                    mm = pe.matmul(bank[b][:, t * NH:(t + 1) * NH], upto[:, :] if u == t else ones[:, :],
                                   logf[:, u, :], start=(u == 0), stop=(u == t), skip_group_check=True)
            mm.then_inc(bank_full[b], 1)
            in_projection("kf")

            def weights_times_tokens(key, chunks, cols, rhs_hi, rhs_lo, where=slice(0, SEQ)):
                b = use[key][0]
                for k in chunks:
                    wh, wl = split_of(key, k, 0, P)
                    mm = product(bank[b][:, cols], wh, wl, rhs_hi[:, k, where], rhs_lo[:, k, where], k == 0,
                                 k == KD - 1)
                return mm

            def attention(first, last, v_hi, v_lo):
                def qk_transposes(g):
                    if g == 0:
                        for t in range(NT):
                            ready(("qf", t))
                            ready(("kf", t))
                            ready(("vf", t))
                        ready(("cum",))
                        pe.wait_ge(nat_extra, 1)
                    if g == NH:
                        pe.wait_ge(nat_extra, 2)
                        pe.wait_ge(qrope_nat, 2)
                        pe.wait_ge(k_nat, 2 * NT - 1)
                    h = g % NH
                    for name, src in (("QT", nat_q), ("KT", nat_k)):
                        b = claim((name, g))
                        for t in range(NT):
                            mm = pe.transpose(bank[b][0:QK, t * P:(t + 1) * P], src[:, t, h, :], ident[:, :])
                        mm.then_inc(bank_full[b], 1)

                def scores(g, *tiles):
                    b = claim(("S", g, tiles[0]))
                    if tiles[0] == 3:
                        ready(("QT", g))
                        ready(("KT", g))
                    for i in tiles:
                        w = P * (i + 1)
                        q, k = slice(i * P, w), slice(0, w)
                        c = score_col(i)
                        product(bank[b][:, c:c + w], qt_hi[0:QK, g % 2, q], qt_lo[0:QK, g % 2, q],
                                kt_hi[0:QK, g % 2, k], kt_lo[0:QK, g % 2, k], True, False)
                        mm = pe.matmul(bank[b][:, c + i * P:c + w], ident_bf[:, :], mask_bf[:, :], start=False,
                                       stop=True, skip_group_check=True)
                    mm.then_inc(bank_full[b], 1)

                def probs_transposes(g, part):
                    if part == 0:
                        pe.wait_ge(probs_ready, 4 * (g + 1))
                    b = claim(("PT", g, part))
                    blocks = (((0, 0), (1, 0), (2, 0), (3, 0)), ((1, 1), (2, 1), (3, 1), (3, 3)),
                              ((2, 2), (3, 2)))[part]
                    for n, (i, j) in enumerate(blocks):
                        s = (g % 2) * P_COLS + P_OFF[i] + j * P
                        mm = pe.transpose(bank[b][:, n * P:(n + 1) * P], resid_flat[:, s:s + P], ident[:, :])
                    mm.then_inc(bank_full[b], 1)

                def values(g):
                    b = claim(("PV", g))
                    c = (g % NH) // 2
                    for part in range(3):
                        ready(("PT", g, part))
                    for j, s in enumerate((0, 512, 1024, 896)):
                        w = SEQ - P * j
                        vs = slice(c * P, (c + 1) * P)
                        mm = product(bank[b][:, P * j:SEQ], v_hi[:, j, vs], v_lo[:, j, vs],
                                     pt_hi[:, g % 2, s:s + w], pt_lo[:, g % 2, s:s + w], j == 0, j == NT - 1)
                    mm.then_inc(bank_full[b], 1)

                plan = fitted(first // NH)

                def fit(g, slot):
                    name, quarter = plan.get((g - first) * SLOTS + slot, (None, 0))
                    if not name:
                        return
                    fit_product(name, quarter)

                def fit_product(name, quarter):
                    if quarter == 0:
                        slab_ready(name)
                        claim(name)
                        if name == ("mk", 0):
                            transposed_ready("memT", 0)
                            transposed_ready("memT", 1)
                    rhs = (xt_hi, xt_lo) if name[0] == "cT" else (mt_hi, mt_lo)
                    width = SEQ if name[0] == "cT" else MEM
                    mm = weights_times_tokens(name, (2 * quarter, 2 * quarter + 1), slice(0, width), *rhs,
                                              where=slice(0, width))
                    if quarter == 3:
                        mm.then_inc(bank_full[use[name][0]], 1)

                fit(first, -4)
                fit(first, -3)
                qk_transposes(first)
                fit(first, -2)
                fit(first, -1)
                if first:
                    for m in range(NM):
                        pe.wait_ge(xn_ready, XN_MEM + m + 1)
                        transpose_rows("memT", m, mem_rows[m])
                for g in range(first, last + 1):
                    scores(g, 3)
                    scores(g, 2, 0)
                    if g == NH:
                        sum_squares(0)
                        pe.wait_ge(k_nat, 2 * NT)
                        for t in range(NT):
                            for n in range(2):
                                ready(("ukv", t, n))
                    fit(g, 0)
                    if g < last:
                        qk_transposes(g + 1)
                    if g > first + 1:
                        values(g - 2)
                    if g > first:
                        probs_transposes(g - 1, 0)
                    scores(g, 1)
                    fit(g, 1)
                    if g > first:
                        probs_transposes(g - 1, 1)
                        probs_transposes(g - 1, 2)
                    fit(g, 2)
                for quarter in range(4):
                    fit_product(("cT", NC_LAT - 1) if first == 0 else ("mk", H_MEM - 1), quarter)
                values(last - 1)

                def last_transposes():
                    for part in range(3):
                        probs_transposes(last, part)

                if first:
                    out_projection(0, after_first=last_transposes)
                    values(last)
                else:
                    last_transposes()
                return values

            def out_projection(stage, after_first=None):
                fam = stage // 2
                tokens_times_weights([("out", stage, k) for k in ((4, 6) if stage < 2 else (0, 2))],
                                     lambda t, n: ("out", stage, t), *((of_hi, of_lo), (om_hi, om_lo))[fam],
                                     HALF, [0, 1, 2, 3], after_first=after_first)

            def sum_over_features(b, col, squares):
                for t in range(NT):
                    mm = pe.matmul(bank[b][:, col + t:col + t + 1], squares[:, t * P:(t + 1) * P], ones[:, 0:1],
                                   start=True, stop=True)
                return mm

            def sum_squares(fam):
                b = claim(("ssq", fam))
                pe.wait_ge(sq_added, 3 * (fam + 1))
                sum_over_features(b, 0, sq_acc).then_inc(bank_full[b], 1)

            values = attention(0, NH - 1, vf_hi, vf_lo)

            def latents_ready(t):
                if t == 0:
                    for c in range(NC_LAT):
                        ready(("cT", c))
                if t == 2:
                    values(NH - 1)
                if t == NT - 1:
                    b = claim(("cssq",))
                    pe.wait_ge(lat_sq_ready, NC_LAT)
                    pe.wait_ge(lat_sq_added, NC_LAT - 2)
                    sum_over_features(b, 0, lat_acc[:, 0, :])
                    sum_over_features(b, 4, lat_acc[:, 1, :]).then_inc(bank_full[b], 1)

            tokens_times_weights([("uq", k) for k in range(CQ)], lambda t, n: ("uq", t, n), ct_hi, ct_lo, 384,
                                 [0, 1, 2], 2, tile_ready=latents_ready)
            tokens_times_weights([("ukv", k) for k in range(CKV)], lambda t, n: ("ukv", t, n), ct_hi, ct_lo, 512,
                                 [3, 4], 2)
            ready(("PV", NH - 1))
            attention(NH, 2 * NH - 1, vm_hi, vm_lo)

            def transpose_half(name, t, half, src):
                b = claim((name, t, half))
                for c in range(4):
                    mm = pe.transpose(bank[b][:, c * P:(c + 1) * P],
                                      src[:, (4 * half + c) * P:(4 * half + c + 1) * P], ident[:, :])
                mm.then_inc(bank_full[b], 1)

            def h1_transposes(half):
                for t in range(NT):
                    pe.wait_ge(xn_ready, XN_H1 + NT * half + t + 1)
                    transpose_half("h1T", t, half, h_rows[t])

            for stage in range(1, 4):
                if stage == 2:
                    sum_squares(1)
                    ready(("PV", 2 * NH - 1))
                out_projection(stage, after_first=(lambda: h1_transposes(0)) if stage == 3 else None)

            def memory_values(k):
                slab_ready(("mv", k))
                for m in range(NM):
                    b = claim(("mv", m)) if k == 0 else use[("mv", m)][0]
                    ms = slice(m * P, (m + 1) * P)
                    for kk in range(2):
                        mm = product(bank[b][:, :], mt_hi[:, k + kk, ms], mt_lo[:, k + kk, ms],
                                     *split_of(("mv", k), 4 * kk, 0, HALF), k + kk == 0, k + kk == KD - 1)
                    if k == KD - 2:
                        mm.then_inc(bank_full[b], 1)
                if k < KD - 2:
                    mm.then_inc(w_used, 1)

            for k in range(0, KD, 2):
                memory_values(k)
            h1_transposes(1)

            def with_all_tokens(key, chunks=range(KD)):
                mm = weights_times_tokens(key, chunks, slice(0, SEQ), xt_hi, xt_lo)
                if chunks[-1] == KD - 1:
                    mm.then_inc(bank_full[use[key][0]], 1)

            def half_of_rows(key, name, half):
                for t in range(NT):
                    ready((name, t, half))
                with_all_tokens(key, range(half * KD // 2, (half + 1) * KD // 2))

            for step in MEM_STEPS:
                kind, h = step[0], step[1]
                if kind == "mq":
                    slab_ready(step)
                    claim(step)
                    if h == 0:
                        half_of_rows(step, "h1T", 0)
                        half_of_rows(step, "h1T", 1)
                    else:
                        with_all_tokens(step)
                elif kind == "MS":
                    ready(("mq", h))
                    ready(("mk", h))
                    for u in range(2):
                        b = claim(("MS", h, u))
                        for i in range(2):
                            q = slice((2 * u + i) * P, (2 * u + i + 1) * P)
                            mm = product(bank[b][:, i * MEM:(i + 1) * MEM], mq_hi[:, h, q], mq_lo[:, h, q],
                                         mk_hi[:, h, :], mk_lo[:, h, :], True, True)
                        mm.then_inc(bank_full[b], 1)
                elif kind == "MPT":
                    pe.wait_ge(inv_ready, 3 * 2 * NH + 4 * (h + 1))
                    for j in range(NM):
                        b = claim(("MPT", h, j))
                        for t in range(NT):
                            c0 = (h % 2) * D + t * MEM + j * P
                            mm = pe.transpose(bank[b][:, t * P:(t + 1) * P], work_flat[:, c0:c0 + P], ident[:, :])
                        mm.then_inc(bank_full[b], 1)
                elif kind == "MPV":
                    b = use[step][0]
                    for j in range(NM):
                        ready(("mv", j))
                        ready(("MPT", h, j))
                    claim(step)
                    for j in range(NM):
                        hs = slice(h * P, (h + 1) * P)
                        mm = product(bank[b][:, :], mv_hi[:, j, hs], mv_lo[:, j, hs], mp_hi[:, 2 * (h % 2) + j, :],
                                     mp_lo[:, 2 * (h % 2) + j, :], j == 0, j == NM - 1)
                    mm.then_inc(bank_full[b], 1)
                elif kind == "mo":
                    n, k, t = step[1:]
                    b = use[("mo", n, t)][0]
                    if k == 0:
                        claim(("mo", n, t))
                    slab_ready(("mo", n, k))
                    ready(("MPV", k + 1))
                    ts = slice(t * P, (t + 1) * P)
                    for kk in range(2):
                        mm = product(bank[b][:, :], mo_hi[:, k + kk, ts], mo_lo[:, k + kk, ts],
                                     *split_of(("mo", n, k), kk, 0, HALF), k + kk == 0, k + kk == H_MEM - 1)
                    if k == 2:
                        mm.then_inc(bank_full[b], 1)
                    elif t == NT - 1:
                        mm.then_inc(w_used, 1)
                elif kind == "h2T":
                    if step[1:] == (1, NT - 1):
                        claim(("gate", 0))
                        slab_ready(("gate", 0))
                        half_of_rows(("gate", 0), "h2T", 0)
                    pe.wait_ge(xn_ready, XN_H2 + NT * step[1] + step[2] + 1)
                    transpose_half("h2T", step[2], step[1], h_rows[step[2]])

            def claim_gate(f):
                if f >= 4:
                    pe.wait_ge(gate_scaled, f - 3)
                    pe.wait_ge(h_done, f - 3)

            claim(("up", 0))
            slab_ready(("up", 0))
            half_of_rows(("up", 0), "h2T", 0)
            half_of_rows(("gate", 0), "h2T", 1)
            half_of_rows(("up", 0), "h2T", 1)
            b = claim(("rstd rows",))
            pe.wait_ge(diag_ready, NT)
            for t in range(NT):
                ts = slice(t * P, (t + 1) * P)
                mm = pe.matmul(bank[b][:, ts], ones[:, :], rstd_diag[:, ts], start=True, stop=True)
            mm.then_inc(bank_full[b], 1)
            for f in range(1, NF):
                claim_gate(f)
                for name in ("gate", "up"):
                    slab_ready((name, f))
                    if f < 4:
                        claim((name, f))
                    with_all_tokens((name, f))

            def down(k, t):
                ts = slice(t * P, (t + 1) * P)
                for n in range(2):
                    b = use[("down", t, n)][0]
                    mm = product(bank[b][:, :], ht_hi[:, k, ts], ht_lo[:, k, ts],
                                 *split_of(("down", k), 0, n * HALF, (n + 1) * HALF), k == 0, k == NF - 1)
                    if k == NF - 1:
                        mm.then_inc(bank_full[b], 1)
                    elif t == (1 if k == 0 else NT - 1) and n == 1:
                        mm.then_inc(w_used, 1)

            slab_ready(("down", 0))
            pe.wait_ge(h_lo_done, 1)
            for t in (2, 3, 0, 1):
                claim_gate({2: NF, 3: NF + 1, 0: NF + 2, 1: NF + 3}[t])
                down(0, t)
            for k in range(1, NF - 2):
                slab_ready(("down", k))
                pe.wait_ge(h_lo_done, k + 1)
                for t in range(NT):
                    down(k, t)
            slab_ready(("down", NF - 2))
            pe.wait_ge(h_lo_done, NF)
            down(NF - 2, 0)
            down(NF - 2, 1)
            slab_ready(("down", NF - 1))
            for t in range(NT):
                if t >= 2:
                    down(NF - 2, t)
                down(NF - 1, t)


_INS = ["x", "mem", "mix_norm_g", "w_in", "cq_norm_g", "ckv_norm_g", "w_uq", "w_ukv", "forget_bias", "mla_out_g",
        "fox_out_g", "w_out", "mem_q_norm_g", "mem_kv_norm_g", "w_mq", "w_mkv", "w_mo", "ffn_norm_g", "w_gate",
        "w_up", "w_down", "final_norm_g"]


def rope_tables():
    inv = (1.0 / (np.float32(10000.0) ** (np.arange(0, ROPE, 2, dtype=np.float32) / np.float32(ROPE)))).astype(np.float32)
    ang = np.arange(SEQ, dtype=np.float32)[:, None] * inv[None, :]
    cos, sin = np.cos(ang).astype(np.float32), np.sin(ang).astype(np.float32)
    both = [np.concatenate([m, m], axis=1) for m in (cos, sin)]
    return np.stack(both)


def kernel(**inputs):
    import numpy as _np
    import concourse.bacc as _bacc
    from concourse import mybir as _mybir
    from concourse.bass_utils import run_bass_kernel_spmd as _run

    nc = _bacc.Bacc("TRN2", target_bir_lowering=False, num_devices=1)
    arrays, aps = {}, {}
    for name in _INS + ["rope"]:
        v = _np.ascontiguousarray(inputs[name]) if name != "rope" else rope_tables()
        arrays[f"in_{name}_dram"] = v
        aps[name] = nc.dram_tensor(f"in_{name}_dram", v.shape, _mybir.dt.from_np(v.dtype), kind="ExternalInput").ap()
    out = nc.dram_tensor("out_0_dram", (1, SEQ, D), _mybir.dt.float32, kind="ExternalOutput").ap()
    build(nc, aps, out)
    r = _run(nc, [arrays], core_ids=[0])
    return r.results[0]["out_0_dram"]
```
